# Optimizing a Trainium2 kernel written in Bass

```python
import jax, jax.numpy as jnp
from jax import lax
import numpy as np

D_MODEL = 1024
BATCH = 1
SEQ = 1024
DEPTH = 1

RWKV_HEADS = 8
RWKV_HEAD_DIM = 64
RWKV_WIDTH = RWKV_HEADS * RWKV_HEAD_DIM
DECAY_LORA = 64
AAA_LORA = 64
MV_LORA = 32
GATE_LORA = 128
GN_EPS = 64e-5
SG_GROUPS = 8
SG_GROUP_DIM = 64
SG_WIDTH = SG_GROUPS * SG_GROUP_DIM
SG_CHUNK = 128
RWKV_COLS = 3 * RWKV_WIDTH + DECAY_LORA + AAA_LORA + GATE_LORA
SG_COLS = 2 * SG_WIDTH
GATE_COLS = 2 * D_MODEL
IN_COLS = RWKV_COLS + SG_COLS + GATE_COLS
N_EXPERTS = 16
N_EXPERT_GROUPS = 4
EXPERTS_PER_GROUP = N_EXPERTS // N_EXPERT_GROUPS
TOP_K = 2
D_FF_EXPERT = 512
MOE_BLOCK = 128
LN_EPS = 1e-5
DEEPNORM_ALPHA = (2 * DEPTH) ** 0.25
DEEPNORM_BETA = (8 * DEPTH) ** -0.25

kernel_name = 'hybrid_rwkv7_spatialgate_grouped_moe_deepnorm'

def _ln(x, eps=LN_EPS):
    xf = x.astype(jnp.float32)
    mu = jnp.mean(xf, -1, keepdims=True)
    var = jnp.mean(jnp.square(xf - mu), -1, keepdims=True)
    return (xf - mu) * lax.rsqrt(var + eps)

def layer_norm(x, g, b, eps=LN_EPS):
    return (_ln(x, eps) * g + b).astype(x.dtype)

def token_shift(z, mu):
    prev = jnp.pad(z[:, :-1], ((0, 0), (1, 0), (0, 0)))
    return z + (prev - z) * mu

def wkv7_scan(r, w, k, v, a, b):
    B, T, H, N = r.shape
    seq = tuple(jnp.moveaxis(t.astype(jnp.float32), 1, 0) for t in (r, w, k, v, a, b))

    def step(S, inp):
        r_t, w_t, k_t, v_t, a_t, b_t = inp
        sa = jnp.einsum('bhvk,bhk->bhv', S, a_t)
        S = S * w_t[:, :, None, :] + sa[..., None] * b_t[:, :, None, :] + v_t[..., None] * k_t[:, :, None, :]
        return S, jnp.einsum('bhvk,bhk->bhv', S, r_t)

    S0 = jnp.zeros((B, H, N, N), jnp.float32)
    _, y = lax.scan(step, S0, seq)
    return jnp.moveaxis(y, 0, 1)

def rwkv7_branch(z, v_first, vmix, mu, w0, w2, a0, a2, g2, k_k, k_a, r_k, gn_g, gn_b):
    B, T, _ = z.shape
    H, N, W = RWKV_HEADS, RWKV_HEAD_DIM, RWKV_WIDTH
    z = token_shift(z, mu)
    o_w = 3 * W
    o_a = o_w + DECAY_LORA
    o_g = o_a + AAA_LORA
    r = z[..., :W]
    k = z[..., W:2 * W]
    v = z[..., 2 * W:3 * W]
    zw = z[..., o_w:o_a]
    za = z[..., o_a:o_g]
    zg = z[..., o_g:]
    w_log = -jax.nn.softplus(-(w0 + jnp.tanh(zw) @ w2)) - 0.5
    decay = jnp.exp(-jnp.exp(w_log.astype(jnp.float32)))
    a = jax.nn.sigmoid(a0 + za @ a2)
    g = jax.nn.sigmoid(zg) @ g2
    if vmix is None:
        v_first = v
    else:
        vm0, vm1, vm2 = vmix
        v = v + (v_first - v) * jax.nn.sigmoid(vm0 + (v @ vm1) @ vm2)
    heads = lambda t: t.reshape(B, T, H, N)
    kk = heads(k * k_k).astype(jnp.float32)
    kk = kk / jnp.maximum(jnp.sqrt(jnp.sum(kk * kk, -1, keepdims=True)), 1e-12)
    k = k * (1 + (a - 1) * k_a)
    rh, kh, vh, ah = heads(r), heads(k), heads(v), heads(a)
    y = wkv7_scan(rh, heads(decay), kh, vh, -kk, kk * ah.astype(jnp.float32))
    y = _ln(y, GN_EPS) * gn_g.reshape(H, N) + gn_b.reshape(H, N)
    y = y + jnp.sum(rh * kh * r_k, -1, keepdims=True) * vh
    return (y.reshape(B, T, W) * g).astype(z.dtype), v_first

def spatial_gating_branch(z, ln_g, ln_b, w_s, b_s):
    B, T, _ = z.shape
    z = jax.nn.gelu(z)
    u, v = z[..., :SG_WIDTH], z[..., SG_WIDTH:]
    v = layer_norm(v, ln_g, ln_b)
    v = v.reshape(B, T // SG_CHUNK, SG_CHUNK, SG_GROUPS, SG_GROUP_DIM)
    causal = jnp.tril(jnp.ones((SG_CHUNK, SG_CHUNK), bool))
    w_m = jnp.where(causal, w_s, 0.0)
    s = jnp.einsum('gts,bnsgd->bntgd', w_m, v) + b_s.T[:, :, None]
    return u * s.reshape(B, T, SG_WIDTH)

def group_limited_route(h, router_w, router_b):
    scores = jax.nn.sigmoid((h @ router_w).astype(jnp.float32))
    sel = (scores + router_b.astype(jnp.float32)).reshape(-1, N_EXPERT_GROUPS, EXPERTS_PER_GROUP)
    group_score = jnp.sum(lax.top_k(sel, TOP_K)[0], -1)
    best = jnp.argmax(group_score, -1)
    in_group = jnp.arange(N_EXPERT_GROUPS)[None, :] == best[:, None]
    masked = jnp.where(in_group[..., None], sel, -jnp.inf).reshape(-1, N_EXPERTS)
    _, idx = lax.top_k(masked, TOP_K)
    wts = jnp.take_along_axis(scores, idx, -1)
    wts = wts / jnp.sum(wts, -1, keepdims=True)
    return idx, wts

def moe_ffn(h, router_w, router_b, e_gate, e_up, e_down):
    B, T, D = h.shape
    hf = h.reshape(-1, D)
    N = hf.shape[0]
    idx, wts = group_limited_route(hf, router_w, router_b)
    A = N * TOP_K
    flat_e = idx.reshape(-1)
    flat_tok = jnp.repeat(jnp.arange(N, dtype=jnp.int32), TOP_K)
    flat_w = wts.reshape(-1)
    order = jnp.argsort(flat_e)
    e_sorted = flat_e[order]
    counts = jnp.bincount(flat_e, length=N_EXPERTS)
    padded = (counts + MOE_BLOCK - 1) // MOE_BLOCK * MOE_BLOCK
    pad_end = jnp.cumsum(padded)
    pad_start = pad_end - padded
    start = jnp.cumsum(counts) - counts
    dest = pad_start[e_sorted] + jnp.arange(A) - start[e_sorted]
    n_blocks = -(-A // MOE_BLOCK) + N_EXPERTS
    P = n_blocks * MOE_BLOCK
    slot_tok = jnp.zeros((P,), jnp.int32).at[dest].set(flat_tok[order])
    slot_w = jnp.zeros((P,), jnp.float32).at[dest].set(flat_w[order])
    block_expert = jnp.minimum(jnp.searchsorted(pad_end, jnp.arange(n_blocks) * MOE_BLOCK, side='right'), N_EXPERTS - 1)
    xb = hf[slot_tok].reshape(n_blocks, MOE_BLOCK, D)

    def expert_block(args):
        xblk, e = args
        hid = jax.nn.silu(xblk @ e_gate[e]) * (xblk @ e_up[e])
        return hid @ e_down[e]

    yb = lax.map(expert_block, (xb, block_expert)).reshape(P, D)
    y = jax.ops.segment_sum(yb * slot_w[:, None].astype(yb.dtype), slot_tok, num_segments=N)
    return y.reshape(B, T, D)

def setup_inputs(seed: int = 0) -> dict:
    key = jax.random.key(seed)
    ks = iter(jax.random.split(key, 40))

    def nrm(shape, scale):
        return jax.random.normal(next(ks), shape, jnp.float32) * scale

    def unif(shape, lo, hi):
        return jax.random.uniform(next(ks), shape, jnp.float32, lo, hi)

    L, D, W, S = DEPTH, D_MODEL, RWKV_WIDTH, SG_WIDTH
    return {
        'x': nrm((BATCH, SEQ, D), 1.0),
        'c': nrm((BATCH, D), 1.0),
        'w_mod': nrm((L, D, 6 * D), 0.5 * D ** -0.5),
        'b_mod': nrm((L, 6 * D), 0.01),
        'w_in': nrm((L, D, IN_COLS), D ** -0.5),
        'rwkv_mu': unif((L, RWKV_COLS), 0.0, 1.0),
        'w0': unif((L, W), -5.0, 0.0),
        'w2': nrm((L, DECAY_LORA, W), 0.5 * DECAY_LORA ** -0.5),
        'a0': nrm((L, W), 0.1),
        'a2': nrm((L, AAA_LORA, W), AAA_LORA ** -0.5),
        'g2': nrm((L, GATE_LORA, W), GATE_LORA ** -0.5),
        'k_k': 0.85 + nrm((L, W), 0.05),
        'k_a': 1.0 + nrm((L, W), 0.05),
        'r_k': nrm((L, RWKV_HEADS, RWKV_HEAD_DIM), 0.1),
        'gn_g': 1.0 + nrm((L, W), 0.05),
        'gn_b': nrm((L, W), 0.01),
        'vm0': nrm((L - 1, W), 0.1),
        'vm1': nrm((L - 1, W, MV_LORA), W ** -0.5),
        'vm2': nrm((L - 1, MV_LORA, W), MV_LORA ** -0.5),
        'sg_ln_g': 1.0 + nrm((L, S), 0.05),
        'sg_ln_b': nrm((L, S), 0.01),
        'w_s': nrm((L, SG_GROUPS, SG_CHUNK, SG_CHUNK), SG_CHUNK ** -0.5),
        'b_s': 1.0 + nrm((L, SG_GROUPS, SG_CHUNK), 0.05),
        'w_branch_a': nrm((L, W, D), W ** -0.5),
        'w_branch_b': nrm((L, S, D), S ** -0.5),
        'w_out': nrm((L, D, D), DEEPNORM_BETA * D ** -0.5),
        'ln1_g': 1.0 + nrm((L, D), 0.05),
        'ln1_b': nrm((L, D), 0.01),
        'router_w': nrm((D, N_EXPERTS), D ** -0.5),
        'router_b': nrm((N_EXPERTS,), 0.01),
        'e_gate': nrm((L, N_EXPERTS, D, D_FF_EXPERT), D ** -0.5),
        'e_up': nrm((L, N_EXPERTS, D, D_FF_EXPERT), D ** -0.5),
        'e_down': nrm((L, N_EXPERTS, D_FF_EXPERT, D), DEEPNORM_BETA * D_FF_EXPERT ** -0.5),
        'ln2_g': 1.0 + nrm((L, D), 0.05),
        'ln2_b': nrm((L, D), 0.01),
    }

def reference(x, c, w_mod, b_mod, w_in, rwkv_mu, w0, w2, a0, a2, g2, k_k, k_a, r_k, gn_g, gn_b,
              vm0, vm1, vm2, sg_ln_g, sg_ln_b, w_s, b_s, w_branch_a, w_branch_b, w_out, ln1_g, ln1_b,
              router_w, router_b, e_gate, e_up, e_down, ln2_g, ln2_b):
    cond = jax.nn.silu(c)
    v_first = None
    for i in range(DEPTH):
        mod = (cond @ w_mod[i] + b_mod[i])[:, None, :]
        shift1, scale1, gate1, shift2, scale2, gate2 = jnp.split(mod, 6, axis=-1)
        h = (_ln(x) * (1 + scale1) + shift1).astype(x.dtype)
        z = h @ w_in[i]
        z_rwkv = z[..., :RWKV_COLS]
        z_sg = z[..., RWKV_COLS:RWKV_COLS + SG_COLS]
        z_gate = z[..., RWKV_COLS + SG_COLS:]
        vmix = None if i == 0 else (vm0[i - 1], vm1[i - 1], vm2[i - 1])
        y_a, v_first = rwkv7_branch(z_rwkv, v_first, vmix, rwkv_mu[i], w0[i], w2[i], a0[i], a2[i], g2[i],
                                    k_k[i], k_a[i], r_k[i], gn_g[i], gn_b[i])
        y_b = spatial_gating_branch(z_sg, sg_ln_g[i], sg_ln_b[i], w_s[i], b_s[i])
        gate_a = jax.nn.sigmoid(z_gate[..., :D_MODEL])
        gate_b = jax.nn.sigmoid(z_gate[..., D_MODEL:])
        mixed = (gate_a * (y_a @ w_branch_a[i]) + gate_b * (y_b @ w_branch_b[i])) @ w_out[i]
        x = layer_norm(DEEPNORM_ALPHA * x + (1 + gate1) * mixed, ln1_g[i], ln1_b[i])
        h = (_ln(x) * (1 + scale2) + shift2).astype(x.dtype)
        ffn = moe_ffn(h, router_w, router_b, e_gate[i], e_up[i], e_down[i])
        x = layer_norm(DEEPNORM_ALPHA * x + (1 + gate2) * ffn, ln2_g[i], ln2_b[i])
    return x


_drawn_inputs = setup_inputs


def setup_inputs(seed=0):
    import zlib

    import numpy as np

    out = dict(_drawn_inputs(seed))
    spreads = {}
    factors = {'a0': 2.75,
     'gn_b': 4.354,
     'sg_ln_g': 2.706,
     'sg_ln_b': 14.574,
     'ln2_b': 5.709,
     'gn_g': 3.354}
    for name, (base, spread) in spreads.items():
        noise = np.random.default_rng([zlib.crc32(name.encode()), seed]).standard_normal(out[name].shape)
        drawn = base * np.exp(spread * noise) if base else spread * noise
        out[name] = __import__('jax').numpy.asarray(drawn.astype(out[name].dtype))
    for name, factor in factors.items():
        out[name] = (out[name] * factor).astype(out[name].dtype)
    return out
```

```python
from contextlib import ExitStack

import numpy as np
import concourse.bass as bass
from concourse import mybir

F32 = mybir.dt.float32
I32 = mybir.dt.int32
U32 = mybir.dt.uint32
ALU = mybir.AluOpType
ACT = mybir.ActivationFunctionType
AX = mybir.AxisListType
ds = bass.ds

P = 128
D = 1024
T = 1024
KC = D // P
NT = T // P
W = 512
NP = W // P
C = 64
NC = T // C
E = 16
EG = 4
F = 512
FC = F // P
NB = 2 * T // P + E
DECAY = float(np.exp(-0.5))
ALPHA = 2.0 ** 0.25
LN_EPS = 1e-5
GN_EPS = 64e-5
BIG = 1e30

CONSTS = ["ident", "up", "upinc", "upfull", "y8", "x8", "o8", "o16", "o32", "headones", "headmean", "ones", "causal"]
COLS = {}
for _name, _n in (("mu", 14), ("w0", 4), ("a0", 4), ("k_k", 4), ("k_a", 4), ("r_k", 4), ("gn_g", 4), ("gn_b", 4),
                  ("shift1", 8), ("scale1", 8), ("shift2", 8), ("scale2", 8), ("c", 8)):
    COLS[_name] = (sum(n for _, n in COLS.values()), _n)
NCOL = sum(n for _, n in COLS.values())
ROWS = {}
for _name, _n in (("sg_ln_g", W), ("sg_ln_b", W), ("gate1", D), ("gate2", D), ("ln1_g", D), ("ln1_b", D),
                  ("ln2_g", D), ("ln2_b", D), ("router_b", E)):
    ROWS[_name] = (sum(n for _, n in ROWS.values()), _n)
NROW = sum(n for _, n in ROWS.values())
Z_ORDER = [12, 13] + [p + 4 * s for p in range(NP) for s in range(3)] + [18, 19, 20, 21] + [14, 15, 16, 17] \
    + list(range(30, 38)) + list(range(22, 30))
Z_V, Z_U, Z_GATE = 14, 18, 22


def constants():
    i = np.arange(P)
    row, col = i[:, None], i[None, :]
    same = lambda n: row // n == col // n
    m = {
        "ident": row == col,
        "up": (row < col) & same(C),
        "upinc": (row <= col) & same(C),
        "upfull": row < col,
        "y8": (row < col) & same(8),
        "x8": (row > col) & same(8),
        "o8": (row > col) & same(16) & ~same(8),
        "o16": (row > col) & same(32) & ~same(16),
        "o32": (row > col) & same(64) & ~same(32),
        "headones": same(64),
        "headmean": same(64) / 64.0,
        "ones": np.ones((P, P)),
        "causal": row <= col,
    }
    table = np.concatenate([np.asarray(m[n], np.float32) for n in CONSTS], axis=1)
    chunk_start = np.ones((P, T), np.float32)
    chunk_start[:, ::C] = 0.0
    small = np.zeros((P, 96), np.float32)
    small[:, 0:EG] = EG - np.arange(EG)
    small[:, EG:EG + E] = E - np.arange(E)
    small[:, 32:32 + NB] = np.arange(NB)
    token = np.arange(T, dtype=np.int32).reshape(NT, P).T.copy()
    return table, chunk_start, small, token


def build(nc, a, out):
    g_d = nc.dram_tensor("g_scratch", (NP, P, T), F32, kind="Internal").ap()
    bonus_d = nc.dram_tensor("bonus_scratch", (NP, P, T), F32, kind="Internal").ap()
    yb_d = nc.dram_tensor("yb_scratch", (NP, P, T), F32, kind="Internal").ap()
    gates_d = nc.dram_tensor("gates_scratch", (2 * KC, P, T), F32, kind="Internal").ap()
    n2_d = nc.dram_tensor("n2_scratch", (T, D), F32, kind="Internal").ap()
    slot_d = nc.dram_tensor("slot_scratch", (NB * P, 1), I32, kind="Internal").ap()
    ys_d = nc.dram_tensor("ys_scratch", (NB * P, D), F32, kind="Internal").ap()

    with ExitStack() as top:
        sems = {}

        def sem(name):
            if name not in sems:
                sems[name] = nc.alloc_semaphore(name=name)
            return sems[name]

        def phase_ends():
            nc.clear_and_free_semaphores(list(sems.values()))
            sems.clear()
            nc.all_engine_barrier()

        def tiles(stack):
            def sb(name, shape, dt=F32):
                return stack.enter_context(nc.sbuf_tensor(name, shape, dt))
            return sb

        sb = tiles(top)
        ps = top.enter_context(nc.psum_tensor("ps", [P, 8, 512], F32))
        consts = sb("consts", [P, len(CONSTS), P])
        cols = sb("cols", [P, NCOL])
        small = sb("small", [P, 96])
        modc = sb("modc", [P, 4, KC])
        k = {n: consts[:, i, :] for i, n in enumerate(CONSTS)}

        def col(name, i):
            return cols[:, COLS[name][0] + i:COLS[name][0] + i + 1]

        def row(name):
            s, n = ROWS[name]
            return a["rows"][s:s + n].partition_broadcast(P)

        def bank(b, n=512):
            return ps[:, b, 0:n]

        def banks(b):
            return ps[:, b:b + 2, :].rearrange("p a n -> p (a n)")

        with ExitStack() as mixer:
            msb = tiles(mixer)
            gate1b = msb("gate1b", [P, D])
            env = dict(nc=nc, a=a, ps=ps, k=k, cols=cols, col=col, row=row, bank=bank, banks=banks, sem=sem,
                       modc=modc, small=small, consts=consts, gate1b=gate1b, tiles=tiles, phase_ends=phase_ends)
            gate2_d = nc.dram_tensor("gate2_scratch", (P, D), F32, kind="Internal").ap()
            with ExitStack() as early:
                esb = tiles(early)
                rt = msb("rt", [P, NP, T])
                at, bt, kt, vt = (esb(n, [P, NP, T]) for n in ("at", "bt", "kt", "vt"))
                pc = esb("pc", [P, NP, NC])
                hT = esb("hT", [P, KC, T])
                ring = esb("ring", [P, 3, 2, KC, P])
                env.update(hT=hT, ring=ring, rt=rt, at=at, bt=bt, kt=kt, vt=vt, pc=pc)
                with ExitStack() as s:
                    project_and_gate(tiles(s), env, yb_d, gate2_d)
                    phase_ends()
                with ExitStack() as s:
                    prepare_recurrence(tiles(s), env, g_d, bonus_d)
                    phase_ends()
                with ExitStack() as s:
                    run_recurrence(tiles(s), env, gates_d)
                    phase_ends()
            with ExitStack() as s:
                x1 = msb("x1", [P, NT, D])
                logits = msb("logits", [P, NT, E])
                mix_branches(tiles(s), env, x1, logits, g_d, bonus_d, yb_d, gates_d, n2_d)
                phase_ends()
            dest = msb("dest", [P, 2, NT], I32)
            wts = msb("wts", [P, 2, NT])
            blocks = msb("blocks", [1, NB], I32)
            with ExitStack() as s:
                route(tiles(s), env, logits, dest, wts, blocks, slot_d)
                phase_ends()
            with ExitStack() as s:
                run_experts(tiles(s), env, blocks, slot_d, n2_d, ys_d)
                phase_ends()
            with ExitStack() as s:
                combine(tiles(s), env, x1, dest, wts, ys_d, gate2_d, out)
                phase_ends()


def project_and_gate(sb, env, yb_d, gate2_d):
    nc, a, ps, k, col, row, bank, banks, sem = (env[n] for n in ("nc", "a", "ps", "k", "col", "row", "bank", "banks", "sem"))
    modc, hT, ring, gate1b = env["modc"], env["hT"], env["ring"], env["gate1b"]
    rt, at, bt, kt, vt = (env[n] for n in ("rt", "at", "bt", "kt", "vt"))
    xs, xn = kt[:, 0:2, :], kt[:, 2:4, :]
    gateb, gate2b = vt[:, 0, :], vt[:, 1, :]
    vg = rt[:].rearrange("p q (a n) -> p (q a) n", n=W)
    u, yb = at[:, 0:2, :], bt[:, 0:2, :]
    stats = sb("stats", [P, NT, 2, 6])
    mv = sb("mv", [P, NT, 2])
    cond = sb("cond", [P, KC])
    condb = sb("condb", [P, KC, P])
    diag = sb("diag", [P, P])
    modr = sb("modr", [P, 4, KC])
    vstats = sb("vstats", [P, NT, 6])
    vmv = sb("vmv", [P, NT, 2])
    lng = sb("lng", [P, W])
    lnb = sb("lnb", [P, W])
    wst = sb("wst", [P, 8, P])
    bsb = sb("bsb", [P, NP, P])

    consts_in, x_in, x_norm, x_turned = sem("consts_in"), [sem("x_in0"), sem("x_in1")], sem("x_norm"), sem("x_turned")
    x_stats, x_rstd, h_evac, h_ready = sem("x_stats"), sem("x_rstd"), sem("h_evac"), sem("h_ready")
    w_in_slot = [sem(f"w_slot{i}") for i in range(3)]
    cond_ready, condb_ready, mod_mm, mod_read = sem("cond_ready"), sem("condb_ready"), sem("mod_mm"), sem("mod_read")
    v_mm, v_gelu, v_var, v_rstd, v_norm, v_scaled = (sem(n) for n in ("v_mm", "v_gelu", "v_var", "v_rstd", "v_norm", "v_scaled"))
    u_mm, u_gelu, s_mm, s_read, yb_ready = (sem(n) for n in ("u_mm", "u_gelu", "s_mm", "s_read", "yb_ready"))
    yb_out, dve_chain, pool_chain, gate2_out = [sem("yb_out0"), sem("yb_out1")], sem("dve_chain0"), sem("pool_chain0"), sem("gate2_out")
    rows_in = sem("rows_in")
    stream = [("mod", g) for g in range(8)] + [("z", Z_V // 2), ("z", Z_V // 2 + 1), ("z", Z_U // 2), ("z", Z_U // 2 + 1)] \
        + [("mod", g) for g in range(8, 24)]
    mod_of = {g: n for n, (what, g) in enumerate(stream) if what == "mod"}
    z_at = {g: n for n, (what, g) in enumerate(stream) if what == "z"}

    def weights_here(eng, n):
        eng.wait_ge(w_in_slot[n % 3], 16 * (n // 3 + 1))

    with nc.Block() as block:
        @block.sync
        def _(sp):
            sp.dma_start(env["consts"][:], a["table"].rearrange("p (n q) -> p n q", q=P)).then_inc(consts_in, 16)
            sp.dma_start(env["cols"][:], a["cols"]).then_inc(consts_in, 16)
            sp.dma_start(env["small"][:], a["small"]).then_inc(consts_in, 16)
            for n, (what, g) in enumerate(stream):
                if n >= 3:
                    before, g0 = stream[n - 3]
                    if before == "mod":
                        sp.wait_ge(mod_mm, g0 + 1)
                    elif g0 < Z_U // 2:
                        sp.wait_ge(v_mm, NT)
                    else:
                        sp.wait_ge(u_mm, 4 * (g0 - Z_U // 2) + 4)
                src = (a["w_mod"] if what == "mod" else a["w_in"])[2 * g:2 * g + 2]
                sp.dma_start(ring[:, n % 3].rearrange("p c k n -> p c (k n)"), src.rearrange("c p n -> p c n")) \
                    .then_inc(w_in_slot[n % 3], 16)
            for i in range(2):
                sp.wait_ge(yb_out[i], 32)
            sp.wait_ge(gate2_out, 16)

        @block.scalar
        def _(act):
            for i in range(NT):
                if i >= 2:
                    act.wait_ge(x_norm, i - 1)
                act.dma_start(xs[:, i % 2, :], a["x"][i * P:(i + 1) * P, :]).then_inc(x_in[i % 2], 16)
                if i == 0:
                    act.dma_start(gateb, row("gate1")).then_inc(rows_in, 16)
                    act.dma_start(gate2b, row("gate2")).then_inc(rows_in, 16)
                    act.dma_start(lng[:], row("sg_ln_g")).then_inc(rows_in, 16)
                    act.dma_start(lnb[:], row("sg_ln_b")).then_inc(rows_in, 16)
                    act.dma_start(wst[:], a["w_s"]).then_inc(rows_in, 16)
                    for h in range(2):
                        act.dma_start(bsb[64 * h:64 * h + 64], a["b_s"].rearrange("(g h) t -> h g t", h=2)[h].partition_broadcast(64)).then_inc(rows_in, 16)
                    act.wait_ge(consts_in, 48)
                    act.activation(cond[:], env["cols"][:, COLS["c"][0]:COLS["c"][0] + KC], ACT.Silu).then_inc(cond_ready, 1)
                act.wait_ge(x_stats, i + 1)
                act.activation(mv[:, i, 1:2], mv[:, i, 1:2], ACT.Sqrt).then_inc(x_rstd, 1)
                if i >= 1:
                    act.wait_ge(x_turned, i)
                    act.copy(hT[:, :, (i - 1) * P:i * P], banks(2 * ((i - 1) % 2)).rearrange("p (k t) -> p k t", k=KC)).then_inc(h_evac, 1)
            act.wait_ge(x_turned, NT)
            act.copy(hT[:, :, (NT - 1) * P:], banks(2 * ((NT - 1) % 2)).rearrange("p (k t) -> p k t", k=KC)).then_inc(h_evac, 1)
            for i in range(NT):
                act.wait_ge(v_mm, i + 1)
                act.activation(vg[:, i, :], bank(i % 4), ACT.Gelu_apprx_tanh).then_inc(v_gelu, 1)
            for p in range(NP):
                if p >= 2:
                    act.wait_ge(yb_ready, p - 1)
                for h in range(2):
                    act.wait_ge(u_mm, 2 * p + h + 1)
                    act.activation(u[:, p % 2, h * 512:(h + 1) * 512], bank((2 * p + h) % 4), ACT.Gelu_apprx_tanh).then_inc(u_gelu, 1)
                if p == 0:
                    act.wait_ge(v_var, 1)
                    act.activation(vmv[:, :, 1:2], vmv[:, :, 1:2], ACT.Sqrt).then_inc(v_rstd, 1)
            for p in range(NP):
                act.wait_ge(yb_ready, p + 1)
                act.dma_start(yb_d[p], yb[:, p % 2, :]).then_inc(yb_out[p % 2], 16)
            act.wait_ge(mod_read, 24)
            act.dma_start(gate2_d, gate2b).then_inc(gate2_out, 16)

        @block.vector
        def _(dve):
            chain = [0]

            def link(ins):
                chain[0] += 1
                ins.then_inc(dve_chain, 1)
                dve.wait_ge(dve_chain, chain[0])

            def mod_group(n, g):
                dve.wait_ge(mod_mm, n + 1)
                part, c0 = g // 4, 2 * (g % 4)
                if part in (2, 5):
                    dst = gate1b if part == 2 else gate2b
                    src = gateb if part == 2 else gate2b
                    s = slice(c0 * P, c0 * P + 256)
                    dve.scalar_tensor_tensor(out=dst[:, s], in0=bank(4 + n % 4, 256), scalar=1.0, in1=src[:, s],
                                             op0=ALU.add, op1=ALU.add).then_inc(mod_read, 1)
                    return
                which = {0: 0, 1: 1, 3: 2, 4: 3}[part]
                for j in range(2):
                    if j or n:
                        dve.wait_ge(dve_chain, chain[0])
                    ins = dve.tensor_tensor_reduce(diag[:], ps[:, 4 + n % 4, j * P:(j + 1) * P], k["ident"], 1.0, 0.0,
                                                   ALU.mult, ALU.add, modr[:, which, c0 + j:c0 + j + 1])
                    if j == 0:
                        chain[0] += 1
                        ins.then_inc(dve_chain, 1)
                    else:
                        ins.then_inc(mod_read, 1)
                dve.wait_ge(mod_read, n + 1)

            dve.wait_ge(cond_ready, 1)
            dve.tensor_copy(condb[:], cond[:].unsqueeze(2).to_broadcast([P, KC, P])).then_inc(condb_ready, 1)
            for i in range(NT):
                dve.wait_ge(x_in[i % 2], 16 * (i // 2 + 1))
                for h in range(2):
                    ins = dve.bn_stats(stats[:, i, h, :], xs[:, i % 2, h * 512:(h + 1) * 512])
                link(ins)
                link(dve.bn_aggr(mv[:, i, :], stats[:, i, :, :].rearrange("p a b -> p (a b)")))
                dve.tensor_scalar(mv[:, i, 1:2], mv[:, i, 1:2], LN_EPS, None, ALU.add).then_inc(x_stats, 1)
                dve.wait_ge(x_rstd, i + 1)
                link(dve.reciprocal(mv[:, i, 1:2], mv[:, i, 1:2]))
                if i >= 2:
                    dve.wait_ge(x_turned, i - 1)
                dve.tensor_scalar(xn[:, i % 2, :], xs[:, i % 2, :], mv[:, i, 0:1], mv[:, i, 1:2], ALU.subtract, ALU.mult).then_inc(x_norm, 1)
            for n in range(8):
                mod_group(n, n)
            for i, (name, c) in enumerate((("shift1", 0), ("scale1", 1))):
                ins = dve.scalar_tensor_tensor(out=modc[:, i, :], in0=modr[:, i, :], scalar=float(c),
                                               in1=env["cols"][:, COLS[name][0]:COLS[name][0] + KC], op0=ALU.add, op1=ALU.add)
            link(ins)
            for kc in range(KC):
                dve.wait_ge(h_evac, NT)
                dve.tensor_scalar(hT[:, kc, :], hT[:, kc, :], modc[:, 1, kc:kc + 1], modc[:, 0, kc:kc + 1], ALU.mult, ALU.add).then_inc(h_ready, 1)
            for i in range(NT):
                dve.wait_ge(v_gelu, i + 1)
                ins = dve.bn_stats(vstats[:, i, :], vg[:, i, :])
            link(ins)
            for i in range(NT):
                ins = dve.bn_aggr(vmv[:, i, :], vstats[:, i, :])
            link(ins)
            dve.tensor_scalar(vmv[:, :, 1:2], vmv[:, :, 1:2], LN_EPS, None, ALU.add).then_inc(v_var, 1)
            dve.wait_ge(v_rstd, 1)
            link(dve.reciprocal(vmv[:, :, 1:2], vmv[:, :, 1:2]))
            for i in range(NT):
                dve.tensor_scalar(vg[:, i, :], vg[:, i, :], vmv[:, i, 0:1], vmv[:, i, 1:2], ALU.subtract, ALU.mult).then_inc(v_norm, 1)
            for p in range(NP):
                dve.wait_ge(s_mm, p + 1)
                if p >= 2:
                    dve.wait_ge(yb_out[p % 2], 16)
                dve.wait_ge(rows_in, 112)
                dve.tensor_tensor(yb[:, p % 2, :].rearrange("p (n t) -> p n t", t=P), banks(4 + 2 * (p % 2)).rearrange("p (n t) -> p n t", t=P),
                                  bsb[:, p, :].unsqueeze(1).to_broadcast([P, NT, P]), ALU.add).then_inc(s_read, 1)
                dve.wait_ge(s_read, p + 1)
                dve.wait_ge(u_gelu, 2 * p + 2)
                dve.tensor_tensor(yb[:, p % 2, :], yb[:, p % 2, :], u[:, p % 2, :], ALU.mult).then_inc(yb_ready, 1)
            for n in range(8, 24):
                mod_group(n, n)
            dve.wait_ge(dve_chain, chain[0])
            dve.wait_ge(mod_read, 24)
            for i, (name, c) in enumerate((("shift2", 0), ("scale2", 1))):
                ins = dve.scalar_tensor_tensor(out=modc[:, 2 + i, :], in0=modr[:, 2 + i, :], scalar=float(c),
                                               in1=env["cols"][:, COLS[name][0]:COLS[name][0] + KC], op0=ALU.add, op1=ALU.add)
            link(ins)

        @block.gpsimd
        def _(pool):
            pool.wait_ge(rows_in, 112)
            pool.wait_ge(consts_in, 48)
            pool.tensor_tensor(wst[:], wst[:], k["causal"].unsqueeze(1).to_broadcast([P, 8, P]), ALU.mult)
            for i in range(NT):
                pool.wait_ge(v_norm, i + 1)
                pool.tensor_tensor(vg[:, i, :], vg[:, i, :], lng[:], ALU.mult).then_inc(pool_chain, 1)
                pool.wait_ge(pool_chain, i + 1)
                pool.tensor_tensor(vg[:, i, :], vg[:, i, :], lnb[:], ALU.add).then_inc(v_scaled, 1)

        @block.tensor
        def _(pe):
            pe.wait_ge(consts_in, 48)
            for i in range(NT):
                pe.wait_ge(x_norm, i + 1)
                if i >= 2:
                    pe.wait_ge(h_evac, i - 1)
                for kc in range(KC):
                    b = 2 * (i % 2) + kc // 4
                    ins = pe.transpose(ps[:, b, (kc % 4) * P:(kc % 4 + 1) * P], xn[:, i % 2, kc * P:(kc + 1) * P], k["ident"])
                ins.then_inc(x_turned, 1)

            def mod_group(n, g):
                pe.wait_ge(condb_ready, 1)
                weights_here(pe, mod_of[g])
                if n == 8:
                    pe.wait_ge(s_read, NP)
                if n >= 4:
                    pe.wait_ge(mod_read, n - 3)
                for kc in range(KC):
                    ins = pe.matmul(bank(4 + n % 4, 256), condb[:, kc, :], ring[:, mod_of[g] % 3, :, kc, :], start=(kc == 0), stop=(kc == KC - 1))
                ins.then_inc(mod_mm, 1)

            for n in range(8):
                mod_group(n, n)
            va, vb = z_at[Z_V // 2], z_at[Z_V // 2 + 1]
            pe.wait_ge(h_ready, KC)
            weights_here(pe, va)
            weights_here(pe, vb)
            pe.wait_ge(h_evac, NT)
            for i in range(NT):
                if i >= 4:
                    pe.wait_ge(v_gelu, i - 3)
                for half, n in enumerate((va, vb)):
                    for kc in range(KC):
                        ins = pe.matmul(ps[:, i % 4, half * 256:half * 256 + 256], hT[:, kc, i * P:(i + 1) * P], ring[:, n % 3, :, kc, :],
                                        start=(kc == 0), stop=(kc == KC - 1))
                ins.then_inc(v_mm, 1)

            def mix(p):
                pe.wait_ge(v_scaled, NT)
                pe.wait_ge(rows_in, 112)
                if p >= 2:
                    pe.wait_ge(s_read, p - 1)
                if p < 2:
                    pe.wait_ge(mod_read, 8)
                for i in range(NT):
                    for h in range(2):
                        g = 2 * p + h
                        ins = pe.matmul(ps[64 * h:64 * h + 64, 4 + 2 * (p % 2) + i // 4, (i % 4) * P:(i % 4 + 1) * P],
                                        vg[:, i, 64 * g:64 * g + 64], wst[:, g, :], start=True, stop=True)
                ins.then_inc(s_mm, 1)

            for p in range(NP):
                n = z_at[(Z_U + p) // 2]
                weights_here(pe, n)
                for h in range(2):
                    m = 2 * p + h
                    pe.wait_ge(v_gelu, NT)
                    if m >= 4:
                        pe.wait_ge(u_gelu, m - 3)
                    for kc in range(KC):
                        ins = pe.matmul(bank(m % 4), ring[:, n % 3, p % 2, kc, :], hT[:, kc, h * 512:(h + 1) * 512], start=(kc == 0), stop=(kc == KC - 1))
                    ins.then_inc(u_mm, 1)
            for p in range(NP):
                mix(p)
            for n in range(8, 24):
                mod_group(n, n)


def prepare_recurrence(sb, env, g_d, bonus_d):
    nc, a, ps, k, col, row, bank, banks, sem = (env[n] for n in ("nc", "a", "ps", "k", "col", "row", "bank", "banks", "sem"))
    hT, ring, rt, at, bt, kt, vt, pc = (env[n] for n in ("hT", "ring", "rt", "at", "bt", "kt", "vt", "pc"))
    reset = sb("reset", [P, T])
    zraw = sb("zraw", [P, 2, T + 1])
    dz = sb("dz", [P, T])
    wa = sb("wa", [P, T])
    sg = sb("sg", [P, T])
    lora = sb("lora", [P, W])
    g2 = sb("g2", [P, W])
    dl = sb("dl", [P, T])
    L = sb("L", [P, T])
    ap_ = sb("ap_", [P, T])
    kk = sb("kk", [P, T])
    t1 = sb("t1", [P, T])
    ein = sb("ein", [P, T])
    gst = sb("gst", [P, T])
    bst = sb("bst", [P, T])
    oka = sb("oka", [P, NP])
    names = ("p_reset_in p_lora_in p_z_mm p_z_evac p_z_mixed p_thw p_sg p_q_mm p_a_mm p_g_mm p_ss_mm p_bs_mm p_dl p_a p_L p_Lx p_ein p_en p_ex "
             "p_g_evac p_kkraw p_sq p_nrm p_kkn p_t1 p_b1 p_bonus p_at p_bt p_kt p_rt p_bta p_zero p_chain p_kmod").split()
    S = {n: sem(n) for n in names}
    w_slot = [sem(f"p_w_slot{i}") for i in range(3)]
    g_out, b_out = sem("p_g_out"), sem("p_b_out")
    NZ = 14
    dst_of = [None, None] + [t for p in range(NP) for t in ((rt, p), (kt, p), (vt, p))]

    with nc.Block() as block:
        @block.sync
        def _(sp):
            sp.dma_start(reset[:], a["chunk_start"]).then_inc(S["p_reset_in"], 16)
            sp.dma_start(lora[0:64, :], a["w2"]).then_inc(S["p_lora_in"], 16)
            sp.dma_start(lora[64:128, :], a["a2"]).then_inc(S["p_lora_in"], 16)
            sp.dma_start(g2[:], a["g2"]).then_inc(S["p_lora_in"], 16)
            for n in range(NZ // 2):
                if n >= 3:
                    sp.wait_ge(S["p_z_mm"], 4 * (n - 2))
                sp.dma_start(ring[:, n % 3].rearrange("p c k n -> p c (k n)"), a["w_in"][2 * n:2 * n + 2].rearrange("c p n -> p c n")).then_inc(w_slot[n % 3], 16)
            for p in range(NP):
                sp.wait_ge(S["p_g_evac"], p + 1)
                sp.dma_start(g_d[p], gst[:]).then_inc(g_out, 16)
                sp.wait_ge(S["p_bonus"], p + 1)
                sp.dma_start(bonus_d[p], bst[:]).then_inc(b_out, 16)
            sp.wait_ge(g_out, 16 * NP)
            sp.wait_ge(b_out, 16 * NP)

        @block.tensor
        def _(pe):
            def z(n):
                if n % 2 == 0:
                    pe.wait_ge(w_slot[n // 2 % 3], 16 * (n // 2 // 3 + 1))
                for h in range(2):
                    m = 2 * n + h
                    if m >= 4:
                        pe.wait_ge(S["p_z_evac"], m - 3)
                    for kc in range(KC):
                        ins = pe.matmul(bank(m % 4), ring[:, n // 2 % 3, n % 2, kc, :], hT[:, kc, h * 512:(h + 1) * 512], start=(kc == 0), stop=(kc == KC - 1))
                    ins.then_inc(S["p_z_mm"], 1)

            def both(b, lhsT, rhs, done):
                for h in range(2):
                    ins = pe.matmul(bank(b + h), lhsT, rhs[:, h * 512:(h + 1) * 512], start=True, stop=True)
                ins.then_inc(S[done], 1)

            z(0)
            z(1)
            for p in range(NP):
                if p == 0:
                    pe.wait_ge(S["p_thw"], 1)
                    pe.wait_ge(S["p_z_mixed"], 2)
                    pe.wait_ge(S["p_lora_in"], 48)
                if p >= 1:
                    pe.wait_ge(S["p_bonus"], p)
                    pe.wait_ge(S["p_g_evac"], p)
                both(4, lora[0:64, p * P:(p + 1) * P], wa[0:64, :], "p_q_mm")
                both(6, lora[64:128, p * P:(p + 1) * P], wa[64:128, :], "p_a_mm")
                z(2 + 3 * p)
                pe.wait_ge(S["p_sg"], 1)
                pe.wait_ge(S["p_a"], p + 1)
                both(6, g2[:, p * P:(p + 1) * P], sg[:], "p_g_mm")
                z(3 + 3 * p)
                z(4 + 3 * p)
                pe.wait_ge(S["p_dl"], p + 1)
                pe.wait_ge(S["p_sq"], p + 1)
                both(4, k["headones"], t1[:], "p_ss_mm")
                pe.wait_ge(S["p_b1"], p + 1)
                pe.wait_ge(S["p_nrm"], p + 1)
                both(4, k["headones"], dz[:], "p_bs_mm")

        @block.scalar
        def _(act):
            def evac(n):
                if n >= 2:
                    act.wait_ge(S["p_z_mixed"], n - 1)
                if n == 0:
                    act.wait_ge(S["p_zero"], 1)
                for h in range(2):
                    act.wait_ge(S["p_z_mm"], 2 * n + h + 1)
                    act.copy(zraw[:, n % 2, 1 + h * 512:1 + (h + 1) * 512], bank((2 * n + h) % 4)).then_inc(S["p_z_evac"], 1)

            evac(0)
            evac(1)
            act.wait_ge(S["p_z_mixed"], 1)
            act.activation(wa[0:64, :], wa[0:64, :], ACT.Tanh).then_inc(S["p_thw"], 1)
            act.wait_ge(S["p_z_mixed"], 2)
            act.activation(sg[:], sg[:], ACT.Sigmoid).then_inc(S["p_sg"], 1)
            for p in range(NP):
                act.wait_ge(S["p_q_mm"], p + 1)
                if p:
                    act.wait_ge(S["p_at"], p)
                act.activation(dl[:], banks(4), ACT.Sigmoid, bias=col("w0", p)).then_inc(S["p_dl"], 1)
                act.wait_ge(S["p_a_mm"], p + 1)
                if p:
                    act.wait_ge(S["p_bt"], p)
                    act.wait_ge(S["p_kt"], p)
                act.activation(ap_[:], banks(6), ACT.Sigmoid, bias=col("a0", p)).then_inc(S["p_a"], 1)
                evac(2 + 3 * p)
                act.wait_ge(S["p_g_mm"], p + 1)
                if p:
                    act.wait_ge(g_out, 16 * p)
                act.copy(gst[:], banks(6)).then_inc(S["p_g_evac"], 1)
                act.wait_ge(S["p_L"], p + 1)
                if p:
                    act.wait_ge(S["p_rt"], p)
                act.activation(ein[:], L[:], ACT.Exp, scale=-DECAY).then_inc(S["p_ein"], 1)
                evac(3 + 3 * p)
                act.wait_ge(S["p_Lx"], p + 1)
                act.activation(dl[:], dl[:], ACT.Exp, scale=-DECAY).then_inc(S["p_ex"], 1)
                act.wait_ge(S["p_ein"], p + 1)
                act.activation(L[:], L[:], ACT.Exp, scale=DECAY).then_inc(S["p_en"], 1)
                evac(4 + 3 * p)
                act.wait_ge(S["p_ss_mm"], p + 1)
                act.activation(t1[:], banks(4), ACT.Sqrt).then_inc(S["p_nrm"], 1)

        @block.gpsimd
        def _(pool):
            for p in range(NP):
                pool.wait_ge(S["p_kkraw"], p + 1)
                if p:
                    pool.wait_ge(S["p_kt"], p)
                    pool.wait_ge(S["p_bt"], p)
                pool.tensor_tensor(t1[:], kk[:], kk[:], ALU.mult).then_inc(S["p_sq"], 1)
                pool.wait_ge(S["p_b1"], p + 1)
                pool.wait_ge(S["p_ein"], p + 1)
                pool.tensor_tensor(rt[:, p, :], rt[:, p, :], ein[:], ALU.mult)
                pool.tensor_copy(pc[:, p, :], ein[:, C - 1::C]).then_inc(S["p_rt"], 1)

        @block.vector
        def _(dve):
            chain = [0]

            def link(ins):
                chain[0] += 1
                ins.then_inc(S["p_chain"], 1)
                dve.wait_ge(S["p_chain"], chain[0])

            dve.memset(zraw[:, :, 0:1], 0.0).then_inc(S["p_zero"], 1)
            link(dve.tensor_scalar(oka[:], env["cols"][:, COLS["k_a"][0]:COLS["k_a"][0] + NP], -1.0, 1.0, ALU.mult, ALU.add))

            def mixed(n):
                dve.wait_ge(S["p_z_evac"], 2 * n + 2)
                c = Z_ORDER[n]
                dst = (wa[:], sg[:])[n] if n < 2 else dst_of[n][0][:, dst_of[n][1], :]
                link(dve.tensor_tensor(dz[:], zraw[:, n % 2, 0:T], zraw[:, n % 2, 1:T + 1], ALU.subtract))
                dve.scalar_tensor_tensor(out=dst, in0=dz[:], scalar=col("mu", c), in1=zraw[:, n % 2, 1:T + 1], op0=ALU.mult, op1=ALU.add) \
                    .then_inc(S["p_z_mixed"], 1)
                dve.wait_ge(S["p_z_mixed"], n + 1)

            dve.wait_ge(S["p_zero"], 1)
            mixed(0)
            mixed(1)
            dve.wait_ge(S["p_reset_in"], 16)
            for p in range(NP):
                r_, k_, v_ = rt[:, p, :], kt[:, p, :], vt[:, p, :]
                if p:
                    dve.wait_ge(S["p_bs_mm"], p)
                mixed(2 + 3 * p)
                dve.wait_ge(S["p_dl"], p + 1)
                dve.tensor_tensor_scan(L[:], reset[:], dl[:], 0.0, ALU.mult, ALU.add).then_inc(S["p_L"], 1)
                dve.wait_ge(S["p_L"], p + 1)
                dve.tensor_tensor(dl[:], L[:], dl[:], ALU.subtract).then_inc(S["p_Lx"], 1)
                mixed(3 + 3 * p)
                dve.tensor_scalar(kk[:], k_, col("k_k", p), None, ALU.mult).then_inc(S["p_kkraw"], 1)
                dve.wait_ge(S["p_a"], p + 1)
                link(dve.tensor_scalar(bst[:], ap_[:], col("k_a", p), oka[:, p:p + 1], ALU.mult, ALU.add) if not p else
                     _after(dve, b_out, 16 * p).tensor_scalar(bst[:], ap_[:], col("k_a", p), oka[:, p:p + 1], ALU.mult, ALU.add))
                link(dve.tensor_tensor(k_, k_, bst[:], ALU.mult))
                mixed(4 + 3 * p)
                dve.scalar_tensor_tensor(out=dz[:], in0=r_, scalar=col("r_k", p), in1=k_, op0=ALU.mult, op1=ALU.mult).then_inc(S["p_b1"], 1)
                dve.wait_ge(S["p_nrm"], p + 1)
                link(dve.tensor_scalar(t1[:], t1[:], 1e-12, None, ALU.max))
                link(dve.reciprocal(t1[:], t1[:]))
                link(dve.tensor_tensor(kk[:], kk[:], t1[:], ALU.mult))
                dve.wait_ge(S["p_ex"], p + 1)
                dve.scalar_tensor_tensor(out=at[:, p, :], in0=kk[:], scalar=-1.0, in1=dl[:], op0=ALU.mult, op1=ALU.mult).then_inc(S["p_at"], 1)
                link(dve.tensor_tensor(t1[:], kk[:], ap_[:], ALU.mult))
                dve.wait_ge(S["p_en"], p + 1)
                dve.tensor_tensor(bt[:, p, :], t1[:], L[:], ALU.mult).then_inc(S["p_bt"], 1)
                dve.tensor_tensor(k_, k_, L[:], ALU.mult).then_inc(S["p_kt"], 1)
                dve.wait_ge(S["p_bs_mm"], p + 1)
                dve.tensor_tensor(bst[:], banks(4), v_, ALU.mult).then_inc(S["p_bonus"], 1)
                dve.wait_ge(S["p_kt"], p + 1)


def _after(eng, s, value):
    eng.wait_ge(s, value)
    return eng


def run_recurrence(sb, env, gates_d):
    nc, a, ps, k, col, row, bank, banks, sem = (env[n] for n in ("nc", "a", "ps", "k", "col", "row", "bank", "banks", "sem"))
    hT, ring, rt, at, bt, kt, vt, pc = (env[n] for n in ("hT", "ring", "rt", "at", "bt", "kt", "vt", "pc"))
    m = {n: sb("m_" + n, [P, NP, P]) for n in "abd bbd kbd rbd vbd bhbd khbd x2 X o8 o16 o32 Y RB AK RK y2 x4 R V BH KH S".split()}
    xraw, Tt, Z, U0, U, SPC = m["x2"], m["x2"], m["y2"], m["x4"], m["Y"], m["X"]
    gst = sb("gst2", [P, 2, 512])
    names = ("abd bbd kbd rbd vbd bhbd khbd y0_mm x0_mm rb_mm ak_mm rk_mm v_tr bh_tr kh_tr xraw X offs Y R1 RB AK RK V BH KH x2_mm y2_mm x2 y2 "
             "x4_mm r2_mm x4 R2 r4_mm R4 T_mm Z_mm T Z rz_mm R u0_mm U0 u_mm U sp_mm y_mm SPC S yout gate_mm gate_sig init").split()
    S = {n: sem("c_" + n) for n in names}
    gw = [sem("c_gw0"), sem("c_gw1")]
    g_out = [sem("c_g_out0"), sem("c_g_out1")]
    NI = NC // 2

    def quads(b):
        return ps[:, b, :].rearrange("p (q n) -> p q n", q=NP)

    def mask(name):
        return k[name].unsqueeze(1).to_broadcast([P, NP, P])

    def diag(t, h):
        return t[64 * h:64 * h + 64, :, 64 * h:64 * h + 64]

    def chunk(t, c, h):
        return t[64 * h:64 * h + 64, :, ds(c * C, C)]

    def decay(c, h):
        return pc[64 * h:64 * h + 64, :, ds(c, 1)].to_broadcast([64, NP, C])

    with nc.Block() as block:
        @block.sync
        def _(sp):
            def load(c, q):
                sp.dma_start(ring[:, q, 0].rearrange("p k n -> p (k n)"), a["w_in"][ds(c + Z_GATE, 1)].rearrange("c p n -> p (c n)")).then_inc(gw[q], 16)

            def store(c):
                for h in range(2):
                    sp.wait_ge(S["gate_sig"], 2 * c + h + 1)
                    sp.dma_start(gates_d[ds(c, 1), :, h * 512:(h + 1) * 512].rearrange("c p n -> p (c n)"), gst[:, h, :]).then_inc(g_out[h], 16)

            load(0, 0)
            load(1, 1)
            with sp.Fori(0, NI - 1) as i:
                for q in range(2):
                    store(2 * i + q)
                    load(2 * i + q + 2, q)
            store(NC - 2)
            store(NC - 1)
            for h in range(2):
                sp.wait_ge(g_out[h], 16 * NC)

        @block.gpsimd
        def _(pool):
            for n in "abd bbd kbd rbd vbd bhbd khbd S".split():
                ins = pool.memset(m[n][:], 0.0)
            ins.then_inc(S["init"], 1)
            pool.wait_ge(S["init"], 1)

            def body(c):
                pool.wait_ge(S["u0_mm"], c)
                pool.wait_ge(S["SPC"], c)
                for h in range(2):
                    ins = pool.tensor_copy(diag(m["abd"], h), chunk(at, c, h))
                ins.then_inc(S["abd"], 1)
                pool.wait_ge(S["abd"], c + 1)
                pool.wait_ge(S["v_tr"], c)
                for h in range(2):
                    ins = pool.tensor_copy(diag(m["vbd"], h), chunk(vt, c, h))
                ins.then_inc(S["vbd"], 1)
                pool.wait_ge(S["vbd"], c + 1)
                pool.wait_ge(S["init"], 1)
                pool.wait_ge(S["bh_tr"], c)
                for h in range(2):
                    ins = pool.tensor_tensor(diag(m["bhbd"], h), chunk(bt, c, h), decay(c, h), ALU.mult)
                ins.then_inc(S["bhbd"], 1)
                pool.wait_ge(S["bhbd"], c + 1)
                pool.wait_ge(S["xraw"], c + 1)
                pool.wait_ge(S["Z_mm"], 3 * c)
                for n in ("o8", "o16", "o32"):
                    ins = pool.tensor_tensor(m[n][:], xraw[:], mask(n), ALU.mult)
                ins.then_inc(S["offs"], 1)
                pool.wait_ge(S["init"], 1)
                pool.wait_ge(S["S"], c)
                pool.wait_ge(S["R2"], c + 1)
                pool.tensor_tensor(SPC[:], m["S"][:], pc[:, :, ds(c, 1)].to_broadcast([P, NP, P]), ALU.mult).then_inc(S["SPC"], 1)

            with pool.Fori(0, NC) as c:
                body(c)

        @block.scalar
        def _(act):
            act.wait_ge(S["init"], 1)

            def sigmoid(c, h):
                act.wait_ge(S["gate_mm"], 2 * c + h + 1)
                act.wait_ge(g_out[h], 16 * c)
                act.activation(gst[:, h, :], bank(6 + h), ACT.Sigmoid).then_inc(S["gate_sig"], 1)

            def body(c):
                for n, src, last, at_ in (("kbd", kt, "rk_mm", c), ("rbd", rt, "y_mm", c)):
                    act.wait_ge(S["init"], 1)
                    act.wait_ge(S[last], at_)
                    for h in range(2):
                        ins = act.copy(diag(m[n], h), chunk(src, c, h))
                    ins.then_inc(S[n], 1)

                def evac(b, ready, value, dst, done):
                    act.wait_ge(S[ready], value)
                    act.copy(dst[:], quads(b)).then_inc(S[done], 1)

                act.wait_ge(S["rz_mm"], 3 * c)
                evac(1, "x0_mm", c + 1, xraw, "xraw")
                act.wait_ge(S["y_mm"], c)
                evac(4, "v_tr", c + 1, m["V"], "V")
                act.wait_ge(S["sp_mm"], c)
                evac(0, "bh_tr", c + 1, m["BH"], "BH")
                evac(1, "kh_tr", c + 1, m["KH"], "KH")
                act.wait_ge(S["X"], c + 1)
                act.wait_ge(S["offs"], c + 1)
                evac(2, "x2_mm", c + 1, m["x2"], "x2")
                act.wait_ge(S["u_mm"], c)
                evac(4, "x4_mm", c + 1, m["x4"], "x4")
                for j in range(3):
                    if j == 0:
                        act.wait_ge(S["r2_mm"], c + 1)
                        act.wait_ge(S["x4_mm"], c + 1)
                    evac(1, "T_mm", 3 * c + j + 1, Tt, "T")
                    if j == 0:
                        sigmoid(c, 0)
                act.wait_ge(S["r4_mm"], c + 1)
                evac(4, "u0_mm", c + 1, U0, "U0")
                evac(5, "u_mm", c + 1, U, "U")
                sigmoid(c, 1)
                act.wait_ge(S["init"], 1)
                act.wait_ge(S["y_mm"], c + 1)
                for h in range(2):
                    ins = act.copy(chunk(rt, c, h), quads(4)[64 * h:64 * h + 64, :, 64 * h:64 * h + 64])
                ins.then_inc(S["yout"], 1)

            with act.Fori(0, NC) as c:
                body(c)

        @block.vector
        def _(dve):
            dve.wait_ge(S["init"], 1)

            def body(c):
                dve.wait_ge(S["rb_mm"], c)
                for h in range(2):
                    ins = dve.tensor_copy(diag(m["bbd"], h), chunk(bt, c, h))
                ins.then_inc(S["bbd"], 1)
                dve.wait_ge(S["kh_tr"], c)
                for h in range(2):
                    ins = dve.tensor_tensor(diag(m["khbd"], h), chunk(kt, c, h), decay(c, h), ALU.mult)
                ins.then_inc(S["khbd"], 1)

                def masked(b, ready, dst, name, done):
                    dve.wait_ge(S[ready], c + 1)
                    dve.tensor_tensor(dst[:], quads(b), mask(name), ALU.mult).then_inc(S[done], 1)

                dve.wait_ge(S["y_mm"], c)
                masked(0, "y0_mm", m["Y"], "y8", "Y")
                dve.wait_ge(S["Y"], c + 1)
                dve.wait_ge(S["u_mm"], c)
                dve.tensor_tensor(m["R"][:], m["Y"][:], mask("ident"), ALU.add).then_inc(S["R1"], 1)
                dve.wait_ge(S["xraw"], c + 1)
                dve.tensor_tensor(m["X"][:], xraw[:], mask("x8"), ALU.mult).then_inc(S["X"], 1)
                masked(2, "rb_mm", m["RB"], "upinc", "RB")
                masked(3, "ak_mm", m["AK"], "up", "AK")
                masked(5, "rk_mm", m["RK"], "upinc", "RK")
                dve.wait_ge(S["y2_mm"], c + 1)
                dve.wait_ge(S["rz_mm"], 3 * c)
                dve.tensor_copy(m["y2"][:], quads(3)).then_inc(S["y2"], 1)
                dve.wait_ge(S["r2_mm"], c + 1)
                dve.wait_ge(S["R1"], c + 1)
                dve.tensor_tensor(m["R"][:], m["R"][:], quads(5), ALU.add).then_inc(S["R2"], 1)
                dve.wait_ge(S["r4_mm"], c + 1)
                dve.wait_ge(S["R2"], c + 1)
                dve.tensor_tensor(m["R"][:], m["R"][:], quads(0), ALU.add).then_inc(S["R4"], 1)
                dve.wait_ge(S["R4"], c + 1)
                for j in range(3):
                    dve.wait_ge(S["Z_mm"], 3 * c + j + 1)
                    dve.wait_ge(S["x4_mm"], c + 1)
                    dve.tensor_copy(Z[:], quads(2)).then_inc(S["Z"], 1)
                    dve.wait_ge(S["rz_mm"], 3 * c + j + 1)
                    dve.tensor_tensor(m["R"][:], m["R"][:], quads(3), ALU.add).then_inc(S["R"], 1)
                    dve.wait_ge(S["R"], 3 * c + j + 1)
                dve.wait_ge(S["SPC"], c + 1)
                dve.wait_ge(S["y_mm"], c + 1)
                dve.wait_ge(S["sp_mm"], c + 1)
                dve.tensor_tensor(m["S"][:], SPC[:], quads(0), ALU.add).then_inc(S["S"], 1)

            with dve.Fori(0, NC) as c:
                body(c)

        @block.tensor
        def _(pe):
            pe.wait_ge(S["init"], 1)

            def each(b, pairs, done, transpose=False):
                for p in range(NP):
                    dst = ps[:, b, p * P:(p + 1) * P]
                    for n, (x, y) in enumerate(pairs):
                        if transpose:
                            ins = pe.transpose(dst, m[x][:, p, :], k["ident"])
                        else:
                            xt, yt = (m[x] if isinstance(x, str) else x), (m[y] if isinstance(y, str) else y)
                            ins = pe.matmul(dst, xt[:, p, :], yt[:, p, :], start=(n == 0), stop=(n == len(pairs) - 1))
                ins.then_inc(S[done], 1)

            def body(c, q):
                def gate_products():
                    pe.wait_ge(gw[q], 16 * turns[0])
                    for h in range(2):
                        for kc in range(KC):
                            if kc == 0:
                                pe.wait_ge(S["gate_sig"], 2 * c)
                            ins = pe.matmul(bank(6 + h), ring[:, q, 0, kc, :], hT[:, kc, h * 512:(h + 1) * 512], start=(kc == 0), stop=(kc == KC - 1))
                            if kc == KC - 1:
                                ins.then_inc(S["gate_mm"], 1)
                            yield

                work = gate_products()

                def fill(n=1):
                    for _ in range(n):
                        next(work, None)

                def need(**waits):
                    for n, v in waits.items():
                        pe.wait_ge(S[n], v)

                fill(1)
                need(abd=c + 1, bbd=c + 1, S=c)
                each(0, [("bbd", "abd")], "y0_mm")
                need(T=3 * c)
                each(1, [("abd", "bbd")], "x0_mm")
                need(kbd=c + 1, rbd=c + 1, Z=3 * c, R=3 * c)
                each(2, [("bbd", "rbd")], "rb_mm")
                each(3, [("kbd", "abd")], "ak_mm")
                need(U=c)
                each(5, [("kbd", "rbd")], "rk_mm")
                need(vbd=c + 1, yout=c)
                each(4, [("vbd", None)], "v_tr", transpose=True)
                need(bhbd=c + 1, Y=c + 1)
                each(0, [("bhbd", None)], "bh_tr", transpose=True)
                need(khbd=c + 1, xraw=c + 1)
                each(1, [("khbd", None)], "kh_tr", transpose=True)
                fill(1)
                need(X=c + 1, RB=c + 1, AK=c + 1)
                each(2, [("Y", "X")], "x2_mm")
                each(3, [("X", "Y")], "y2_mm")
                fill(2)
                need(x2=c + 1, R1=c + 1, RK=c + 1)
                each(5, [("x2", "R")], "r2_mm")
                need(y2=c + 1, V=c + 1)
                each(4, [("y2", "x2")], "x4_mm")
                fill(1)
                need(x4=c + 1, R2=c + 1, BH=c + 1)
                each(0, [("x4", "R")], "r4_mm")
                fill(1)
                need(offs=c + 1, KH=c + 1)
                for j, off in enumerate(("o8", "o16", "o32")):
                    need(R4=c + 1) if j == 0 else need(R=3 * c + j)
                    each(1, [("R", None)], "T_mm", transpose=True)
                    each(2, [(off, "R")], "Z_mm")
                    fill(1)
                    need(T=3 * c + j + 1, Z=3 * c + j + 1)
                    each(3, [(Tt, Z)], "rz_mm")
                    fill(1)
                need(S=c)
                each(4, [("abd", "S"), ("AK", "V")], "u0_mm")
                fill(2)
                need(U0=c + 1, R=3 * c + 3)
                each(5, [("R", U0)], "u_mm")
                fill(2)
                need(U=c + 1)
                each(0, [("BH", U), ("KH", "V")], "sp_mm")
                each(4, [("S", "rbd"), (U, "RB"), ("V", "RK")], "y_mm")
                fill(16)

            turns = [None]
            with pe.Fori(0, NI) as i:
                turns[0] = i + 1
                for q in range(2):
                    body(2 * i + q, q)


def mix_branches(sb, env, x1, logits, g_d, bonus_d, yb_d, gates_d, n2_d):
    nc, a, ps, k, col, row, bank, banks, sem = (env[n] for n in ("nc", "a", "ps", "k", "col", "row", "bank", "banks", "sem"))
    rt, modc, gate1b = env["rt"], env["modc"], env["gate1b"]
    yb = sb("yb2", [P, NP, T])
    mixed = sb("mixed", [P, KC, T])
    wab = sb("wab", [P, NP, D])
    wob = sb("wob", [P, KC, D // 2])
    gs = sb("gs", [P, 2, T])
    gg = sb("gg", [P, T])
    bo = sb("bo", [P, T])
    yc = sb("yc", [P, T])
    sq = sb("sq", [P, T])
    tmp = sb("tmp", [P, T])
    names = ("w_b w_a w_o yb_in gg_in bo_in mean_mm var_mm yc sq var sd gn ya pb_mm pa_mm mb ma mixed chain pchain "
             "gin0 gin1 eps").split()
    S = {n: sem("x_" + n) for n in names}
    with nc.Block() as block:
        @block.sync
        def _(sp):
            sp.dma_start(wab[:], a["w_branch_b"].rearrange("(k p) n -> p k n", p=P)).then_inc(S["w_b"], 16)
            sp.dma_start(yb[:], yb_d.rearrange("q p t -> p q t")).then_inc(S["yb_in"], 16)
            for n in range(2 * KC):
                if n >= 2:
                    sp.wait_ge(S["mb"], min(n - 1, KC))
                if n >= KC + 2:
                    sp.wait_ge(S["ma"], n - 1 - KC)
                sp.dma_start(gs[:, n % 2, :], gates_d[n]).then_inc(S[f"gin{n % 2}"], 16)
                if n == KC - 1:
                    sp.wait_ge(S["pb_mm"], KC)
                    sp.dma_start(wab[:], a["w_branch_a"].rearrange("(k p) n -> p k n", p=P)).then_inc(S["w_a"], 16)

        @block.scalar
        def _(act):
            for p in range(NP):
                if p:
                    act.wait_ge(S["ya"], p)
                act.dma_start(gg[:], g_d[p]).then_inc(S["gg_in"], 16)
                act.dma_start(bo[:], bonus_d[p]).then_inc(S["bo_in"], 16)
                act.wait_ge(S["var"], p + 1)
                act.activation(sq[:], sq[:], ACT.Sqrt).then_inc(S["sd"], 1)

        @block.gpsimd
        def _(pool):
            for p in range(NP):
                pool.wait_ge(S["yc"], p + 1)
                if p:
                    pool.wait_ge(S["gn"], p)
                pool.tensor_tensor(sq[:], yc[:], yc[:], ALU.mult).then_inc(S["sq"], 1)
                pool.wait_ge(S["gn"], p + 1)
                pool.wait_ge(S["bo_in"], 16 * (p + 1))
                pool.wait_ge(S["gg_in"], 16 * (p + 1))
                pool.tensor_tensor(yc[:], yc[:], bo[:], ALU.add).then_inc(S["pchain"], 1)
                pool.wait_ge(S["pchain"], p + 1)
                pool.tensor_tensor(rt[:, p, :], yc[:], gg[:], ALU.mult).then_inc(S["ya"], 1)

        @block.vector
        def _(dve):
            chain = [0]

            def link(ins):
                chain[0] += 1
                ins.then_inc(S["chain"], 1)
                dve.wait_ge(S["chain"], chain[0])

            def branch_b(j):
                dve.wait_ge(S["pb_mm"], j + 1)
                dve.wait_ge(S[f"gin{j % 2}"], 16 * (j // 2 + 1))
                dve.tensor_tensor(mixed[:, j, :], banks(4 + 2 * (j % 2)), gs[:, j % 2, :], ALU.mult).then_inc(S["mb"], 1)

            for p in range(NP):
                dve.wait_ge(S["mean_mm"], p + 1)
                if p:
                    dve.wait_ge(S["ya"], p)
                dve.tensor_tensor(yc[:], rt[:, p, :], banks(0), ALU.subtract).then_inc(S["yc"], 1)
                branch_b(2 * p)
                dve.wait_ge(S["var_mm"], p + 1)
                dve.tensor_scalar(sq[:], banks(2), GN_EPS, None, ALU.add).then_inc(S["var"], 1)
                branch_b(2 * p + 1)
                dve.wait_ge(S["sd"], p + 1)
                link(dve.reciprocal(sq[:], sq[:]))
                link(dve.tensor_tensor(yc[:], yc[:], sq[:], ALU.mult))
                dve.tensor_scalar(yc[:], yc[:], col("gn_g", p), col("gn_b", p), ALU.mult, ALU.add).then_inc(S["gn"], 1)
            for j in range(KC):
                dve.wait_ge(S["pa_mm"], j + 1)
                dve.wait_ge(S[f"gin{j % 2}"], 16 * ((KC + j) // 2 + 1))
                dve.tensor_tensor(tmp[:], banks(4 + 2 * (j % 2)), gs[:, j % 2, :], ALU.mult).then_inc(S["ma"], 1)
                dve.wait_ge(S["ma"], j + 1)
                dve.wait_ge(S["mb"], KC)
                link(dve.tensor_tensor(mixed[:, j, :], mixed[:, j, :], tmp[:], ALU.add))

        @block.tensor
        def _(pe):
            def heads(b, src, done):
                for h in range(2):
                    ins = pe.matmul(bank(b + h), k["headmean"], src[:, h * 512:(h + 1) * 512], start=True, stop=True)
                ins.then_inc(S[done], 1)

            def project(j, src, done):
                for h in range(2):
                    for q in range(NP):
                        ins = pe.matmul(bank(4 + 2 * (j % 2) + h), wab[:, q, j * P:(j + 1) * P], src[:, q, h * 512:(h + 1) * 512], start=(q == 0), stop=(q == NP - 1))
                ins.then_inc(S[done], 1)

            pe.wait_ge(S["w_b"], 16)
            pe.wait_ge(S["yb_in"], 16)
            for j in range(KC):
                p = j // 2
                if j % 2 == 0:
                    if p:
                        pe.wait_ge(S["yc"], p)
                    heads(0, rt[:, p, :], "mean_mm")
                if j >= 2:
                    pe.wait_ge(S["mb"], j - 1)
                project(j, yb, "pb_mm")
                if j % 2 == 0:
                    pe.wait_ge(S["sq"], p + 1)
                    if p:
                        pe.wait_ge(S["var"], p)
                    heads(2, sq[:], "var_mm")
            pe.wait_ge(S["w_a"], 16)
            pe.wait_ge(S["ya"], NP)
            for j in range(KC):
                if j < 2:
                    pe.wait_ge(S["mb"], KC)
                else:
                    pe.wait_ge(S["ma"], j - 1)
                project(j, rt, "pa_mm")

    env["phase_ends"]()
    rows = sb("rows", [P, 2, D])
    xs = sb("xs2", [P, D])
    n2 = sb("n2", [P, D])
    h2 = sb("h2", [P, KC, P])
    rw = sb("rw", [P, KC, E])
    st = sb("st", [P, 4, 6])
    mv = sb("mv2", [P, 2, 2])
    names = "x_in rows_in rw_in o_in o2_in o_mm stat sd lin x1r x1s x1 stat2 sd2 n2 n2_out n2_tr h2 r_mm chain res o_read".split()
    Q = {n: sem("o_" + n) for n in names}
    wo2 = yb
    wo_hi = yb[:].rearrange("p q (a n) -> p (q a) n", a=2)
    with nc.Block() as block:
        @block.sync
        def _(sp):
            w = a["w_out"].rearrange("(k p) n -> p k n", p=P)
            sp.dma_start(wob[:], w[:, :, 0:512]).then_inc(Q["o_in"], 16)
            sp.dma_start(wo_hi, w[:, :, 512:1024]).then_inc(Q["o2_in"], 16)
            sp.dma_start(rows[:, 0, :], row("ln1_g")).then_inc(Q["rows_in"], 16)
            sp.dma_start(rows[:, 1, :], row("ln1_b")).then_inc(Q["rows_in"], 16)
            sp.dma_start(rw[:], a["router_w"].rearrange("(k p) n -> p k n", p=P)).then_inc(Q["rw_in"], 16)
            for i in range(NT):
                if i:
                    sp.wait_ge(Q["res"], i)
                sp.dma_start(xs[:], a["x"][i * P:(i + 1) * P, :]).then_inc(Q["x_in"], 16)
                if i:
                    sp.wait_ge(Q["n2"], i)
                    sp.dma_start(n2_d[(i - 1) * P:i * P, :], n2[:]).then_inc(Q["n2_out"], 16)
            sp.wait_ge(Q["n2"], NT)
            sp.dma_start(n2_d[(NT - 1) * P:, :], n2[:]).then_inc(Q["n2_out"], 16)
            sp.wait_ge(Q["n2_out"], 16 * NT)

        @block.scalar
        def _(act):
            for i in range(NT):
                act.wait_ge(Q["stat"], i + 1)
                act.activation(mv[:, 0, 1:2], mv[:, 0, 1:2], ACT.Sqrt).then_inc(Q["sd"], 1)
                act.wait_ge(Q["stat2"], i + 1)
                act.activation(mv[:, 1, 1:2], mv[:, 1, 1:2], ACT.Sqrt).then_inc(Q["sd2"], 1)
                act.wait_ge(Q["n2_tr"], i + 1)
                if i:
                    act.wait_ge(Q["r_mm"], i)
                for kc in range(KC):
                    ins = act.activation(h2[:, kc, :], ps[:, 4 + kc // 4, (kc % 4) * P:(kc % 4 + 1) * P], ACT.Identity,
                                         bias=modc[:, 2, kc:kc + 1], scale=modc[:, 3, kc:kc + 1])
                ins.then_inc(Q["h2"], 1)

        @block.gpsimd
        def _(pool):
            pool.wait_ge(Q["rows_in"], 32)
            for i in range(NT):
                pool.wait_ge(Q["x1r"], i + 1)
                pool.tensor_tensor(x1[:, i, :], x1[:, i, :], rows[:, 0, :], ALU.mult).then_inc(Q["x1s"], 1)
                pool.wait_ge(Q["x1s"], i + 1)
                pool.tensor_tensor(x1[:, i, :], x1[:, i, :], rows[:, 1, :], ALU.add).then_inc(Q["x1"], 1)

        @block.vector
        def _(dve):
            chain = [0]

            def link(ins):
                chain[0] += 1
                ins.then_inc(Q["chain"], 1)
                dve.wait_ge(Q["chain"], chain[0])

            def norm(src, dst, w, stat, sd, i, done):
                for h in range(2):
                    ins = dve.bn_stats(st[:, 2 * w + h, :], src[:, h * 512:(h + 1) * 512])
                link(ins)
                link(dve.bn_aggr(mv[:, w, :], st[:, 2 * w:2 * w + 2, :].rearrange("p a b -> p (a b)")))
                dve.tensor_scalar(mv[:, w, 1:2], mv[:, w, 1:2], LN_EPS, None, ALU.add).then_inc(Q[stat], 1)
                dve.wait_ge(Q[sd], i + 1)
                link(dve.reciprocal(mv[:, w, 1:2], mv[:, w, 1:2]))
                return dve.tensor_scalar(dst, src, mv[:, w, 0:1], mv[:, w, 1:2], ALU.subtract, ALU.mult).then_inc(Q[done], 1)

            for i in range(NT):
                dve.wait_ge(Q["o_mm"], i + 1)
                dve.tensor_tensor(tmp[:], banks(2 * (i % 2)), gate1b[:], ALU.mult).then_inc(Q["o_read"], 1)
                dve.wait_ge(Q["o_read"], i + 1)
                dve.wait_ge(Q["x_in"], 16 * (i + 1))
                dve.scalar_tensor_tensor(out=tmp[:], in0=xs[:], scalar=ALPHA, in1=tmp[:], op0=ALU.mult, op1=ALU.add).then_inc(Q["res"], 1)
                dve.wait_ge(Q["res"], i + 1)
                norm(tmp[:], x1[:, i, :], 0, "stat", "sd", i, "x1r")
                dve.wait_ge(Q["x1"], i + 1)
                if i:
                    dve.wait_ge(Q["n2_out"], 16 * i)
                    dve.wait_ge(Q["n2_tr"], i)
                norm(x1[:, i, :], n2[:], 1, "stat2", "sd2", i, "n2")
            dve.wait_ge(Q["r_mm"], NT)
            link(dve.tensor_copy(logits[:].rearrange("p i e -> p (i e)"), bank(6, NT * E)))

        @block.tensor
        def _(pe):
            pe.wait_ge(Q["o_in"], 16)
            pe.wait_ge(Q["o2_in"], 16)

            def out_tile(i):
                if i >= 2:
                    pe.wait_ge(Q["o_read"], i - 1)
                for h, w in enumerate((wob[:], wo_hi)):
                    for kc in range(KC):
                        ins = pe.matmul(bank(2 * (i % 2) + h), mixed[:, kc, i * P:(i + 1) * P], w[:, kc, :], start=(kc == 0), stop=(kc == KC - 1))
                ins.then_inc(Q["o_mm"], 1)

            def router(i):
                pe.wait_ge(Q["n2"], i + 1)
                if i:
                    pe.wait_ge(Q["h2"], i)
                else:
                    pe.wait_ge(Q["rw_in"], 16)
                for kc in range(KC):
                    ins = pe.transpose(ps[:, 4 + kc // 4, (kc % 4) * P:(kc % 4 + 1) * P], n2[:, kc * P:(kc + 1) * P], k["ident"])
                ins.then_inc(Q["n2_tr"], 1)
                pe.wait_ge(Q["h2"], i + 1)
                for kc in range(KC):
                    ins = pe.matmul(ps[:, 6, i * E:(i + 1) * E], h2[:, kc, :], rw[:, kc, :], start=(kc == 0), stop=(kc == KC - 1))
                ins.then_inc(Q["r_mm"], 1)

            out_tile(0)
            for i in range(NT):
                if i + 1 < NT:
                    out_tile(i + 1)
                router(i)


def route(sb, env, logits, dest, wts, blocks, slot_d):
    nc, a, ps, k, row, sem, small = (env[n] for n in ("nc", "a", "ps", "k", "row", "sem", "small"))
    NE = NT * E
    t = {n: sb("r_" + n, [P, NE]) for n in "score sel gs eq eq2 masked M1 M2 M wk tot".split()}
    pair = sb("r_pair", [P, NT * EG, 3])
    base = sb("r_base", [P, NT + 1, E])
    nblk = sb("r_nblk", [P, E])
    bend = sb("r_bend", [P, E])
    bst = sb("r_bst", [P, E])
    one = sb("r_one", [P, E])
    gq = {n: sb("r_g" + n, [P, NT * EG]) for n in "abcd"}
    c8 = {n: sb("r_c" + n, [P, NT]) for n in "abc"}
    rb = sb("r_rb", [P, E])
    cmp_ = sb("r_cmp", [1, NB, E])
    bl = sb("r_bl", [1, NB])
    tok = sb("r_tok", [P, NT], I32)
    zero = sb("r_zero", [P, NB], I32)
    names = "score rb_in tok_in slots_zeroed M_ready rank_mm chain dest zero scatter blocks".split()
    S = {n: sem("r_" + n) for n in names}
    prio_g, prio_e, iota_b = small[:, 0:EG], small[:, EG:EG + E], small[0:1, 32:32 + NB]

    def ie(x):
        return x[:].rearrange("p (i e) -> p i e", e=E)

    def ig(x):
        return x[:].rearrange("p (i g) -> p i g", g=EG)

    with nc.Block() as block:
        @block.sync
        def _(sp):
            sp.dma_start(rb[:], row("router_b")).then_inc(S["rb_in"], 16)
            sp.dma_start(tok[:], a["token"]).then_inc(S["tok_in"], 16)
            sp.wait_ge(S["zero"], 1)
            sp.dma_start(slot_d.rearrange("(p n) o -> p (n o)", p=P), zero[:]).then_inc(S["slots_zeroed"], 16)

        @block.scalar
        def _(act):
            act.activation(t["score"][:], logits[:].rearrange("p i e -> p (i e)"), ACT.Sigmoid).then_inc(S["score"], 1)

        @block.tensor
        def _(pe):
            pe.wait_ge(S["M_ready"], 1)
            pe.matmul(ps[:, 0, 0:NE], k["upfull"], t["M"][:], start=True, stop=True)
            pe.matmul(ps[:, 1, 0:NE], k["ones"], t["M"][:], start=True, stop=True).then_inc(S["rank_mm"], 1)

        @block.gpsimd
        def _(pool):
            pool.memset(zero[:], 0).then_inc(S["zero"], 1)
            pool.wait_ge(S["dest"], 1)
            pool.wait_ge(S["tok_in"], 16)
            pool.wait_ge(S["slots_zeroed"], 16)
            for c in range(2):
                for i in range(NT):
                    pool.indirect_dma_start(out=slot_d, out_offset=bass.IndirectOffsetOnAxis(ap=dest[:, c, i:i + 1].bitcast(U32), axis=0),
                                            in_=tok[:, i:i + 1], in_offset=None).then_inc(S["scatter"], 16)
            pool.wait_ge(S["scatter"], 32 * NT)

        @block.vector
        def _(dve):
            chain = [0]

            def link(ins):
                chain[0] += 1
                ins.then_inc(S["chain"], 1)
                dve.wait_ge(S["chain"], chain[0])

            def tt(o, x, y, op):
                link(dve.tensor_tensor(o, x, y, op))

            dve.wait_ge(S["score"], 1)
            dve.wait_ge(S["rb_in"], 16)
            tt(ie(t["sel"]), ie(t["score"]), rb[:].unsqueeze(1).to_broadcast([P, NT, E]), ALU.add)
            x4 = t["sel"][:].rearrange("p (m e) -> p m e", e=4)
            ga, gb = gq["a"][:].unsqueeze(2), gq["b"][:]
            tt(pair[:], x4[:, :, 0:3], x4[:, :, 1:4], ALU.add)
            link(dve.tensor_reduce(gb, pair[:], AX.X, ALU.max))
            tt(pair[:, :, 0:2], x4[:, :, 0:2], x4[:, :, 2:4], ALU.add)
            tt(pair[:, :, 2:3], x4[:, :, 0:1], x4[:, :, 3:4], ALU.add)
            link(dve.tensor_reduce(gq["a"][:], pair[:], AX.X, ALU.max))
            tt(gb, gb, gq["a"][:], ALU.max)
            link(dve.tensor_reduce(c8["a"][:], ig(gq["b"]), AX.X, ALU.max))
            tt(ig(gq["c"]), ig(gq["b"]), c8["a"][:].unsqueeze(2).to_broadcast([P, NT, EG]), ALU.is_equal)
            tt(ig(gq["c"]), ig(gq["c"]), prio_g.unsqueeze(1).to_broadcast([P, NT, EG]), ALU.mult)
            link(dve.tensor_reduce(c8["a"][:], ig(gq["c"]), AX.X, ALU.max))
            tt(ig(gq["c"]), ig(gq["c"]), c8["a"][:].unsqueeze(2).to_broadcast([P, NT, EG]), ALU.is_equal)
            link(dve.tensor_scalar(gq["d"][:], gq["c"][:], -1.0, BIG, ALU.add, ALU.mult))
            tt(t["masked"][:].rearrange("p (m e) -> p m e", e=4), x4, gq["d"][:].unsqueeze(2).to_broadcast([P, NT * EG, 4]), ALU.add)
            for n, M in enumerate(("M1", "M2")):
                link(dve.tensor_reduce(c8["a"][:], ie(t["masked"]), AX.X, ALU.max))
                tt(ie(t["eq"]), ie(t["masked"]), c8["a"][:].unsqueeze(2).to_broadcast([P, NT, E]), ALU.is_equal)
                tt(ie(t["eq"]), ie(t["eq"]), prio_e.unsqueeze(1).to_broadcast([P, NT, E]), ALU.mult)
                link(dve.tensor_reduce(c8["a"][:], ie(t["eq"]), AX.X, ALU.max))
                tt(ie(t[M]), ie(t["eq"]), c8["a"][:].unsqueeze(2).to_broadcast([P, NT, E]), ALU.is_equal)
                if n == 0:
                    link(dve.scalar_tensor_tensor(out=t["masked"][:], in0=t[M][:], scalar=-BIG, in1=t["masked"][:], op0=ALU.mult, op1=ALU.add))
            dve.tensor_tensor(t["M"][:], t["M1"][:], t["M2"][:], ALU.add).then_inc(S["M_ready"], 1)
            for n, M in enumerate(("M1", "M2")):
                tt(t["wk"][:], t["score"][:], t[M][:], ALU.mult)
                link(dve.tensor_reduce(wts[:, n, :], ie(t["wk"]), AX.X, ALU.add))
            tt(c8["b"][:], wts[:, 0, :], wts[:, 1, :], ALU.add)
            link(dve.reciprocal(c8["b"][:], c8["b"][:]))
            for n in range(2):
                tt(wts[:, n, :], wts[:, n, :], c8["b"][:], ALU.mult)
            link(dve.memset(base[:, 0, :], 0.0))
            link(dve.memset(one[:], 1.0))
            link(dve.memset(nblk[:], 0.0))
            dve.wait_ge(S["rank_mm"], 1)
            for i in range(NT):
                tt(base[:, i + 1, :], base[:, i, :], ps[:, 1, i * E:(i + 1) * E], ALU.add)
            for j in range(T // P):
                link(dve.scalar_tensor_tensor(out=nblk[:], in0=base[:, NT, :], scalar=float(P * j), in1=nblk[:], op0=ALU.is_gt, op1=ALU.add))
            link(dve.tensor_tensor_scan(bend[:], one[:], nblk[:], 0.0, ALU.mult, ALU.add))
            tt(bst[:], bend[:], nblk[:], ALU.subtract)
            link(dve.tensor_scalar(bst[:], bst[:], float(P), None, ALU.mult))
            tt(ie(t["wk"]), ps[:, 0, 0:NE].rearrange("p (i e) -> p i e", e=E), base[:, 0:NT, :], ALU.add)
            tt(ie(t["wk"]), ie(t["wk"]), bst[:].unsqueeze(1).to_broadcast([P, NT, E]), ALU.add)
            for n, M in enumerate(("M1", "M2")):
                tt(t["eq"][:], t["wk"][:], t[M][:], ALU.mult)
                link(dve.tensor_reduce(c8["c"][:], ie(t["eq"]), AX.X, ALU.add))
                ins = dve.tensor_copy(dest[:, n, :], c8["c"][:])
                if n == 0:
                    link(ins)
            ins.then_inc(S["dest"], 1)
            tt(cmp_[:], bend[0:1, :].unsqueeze(1).to_broadcast([1, NB, E]), iota_b.unsqueeze(2).to_broadcast([1, NB, E]), ALU.is_le)
            link(dve.tensor_reduce(bl[:], cmp_[:], AX.X, ALU.add))
            link(dve.tensor_scalar(bl[:], bl[:], float(E - 1), None, ALU.min))
            link(dve.tensor_copy(blocks[:], bl[:]))


def run_experts(sb, env, blocks, slot_d, n2_d, ys_d):
    nc, a, ps, k, bank, banks, sem, modc = (env[n] for n in ("nc", "a", "ps", "k", "bank", "banks", "sem", "modc"))
    wg = [sb(f"wg{i}", [P, KC, F]) for i in range(2)]
    wu = [sb(f"wu{i}", [P, KC, F]) for i in range(2)]
    wd = [sb(f"wd{i}", [P, FC, D]) for i in range(2)]
    idx = sb("idx", [P, 2], I32)
    xg = sb("xg", [P, D])
    xT = [sb(f"xT{i}", [P, KC, P]) for i in range(2)]
    sil = sb("sil", [P, F])
    hid = sb("hid", [P, F])
    hidT = sb("hidT", [P, FC, P])
    yst = sb("yst", [P, D])
    names = "idx xg xt_mm xT gu_mm sil hid ht_mm hidT d_mm y yout".split()
    S = {n: sem("e_" + n) for n in names}
    full = [[sem(f"e_w{n}{i}") for n in "gud"] for i in range(2)]
    NI = NB // 2

    with nc.Block() as block:
        @block.sync
        def _(sp):
            def load(b, q):
                e = sp.value_load(blocks[0:1, ds(b, 1)], min_val=0, max_val=E - 1)
                sp.dma_start(wg[q][:], a["e_gate"][ds(e, 1)].rearrange("e (k p) f -> p (e k) f", p=P)).then_inc(full[q][0], 16)
                sp.dma_start(wu[q][:], a["e_up"][ds(e, 1)].rearrange("e (k p) f -> p (e k) f", p=P)).then_inc(full[q][1], 16)
                sp.dma_start(wd[q][:], a["e_down"][ds(e, 1)].rearrange("e (k p) f -> p (e k) f", p=P)).then_inc(full[q][2], 16)

            def store(b):
                sp.wait_ge(S["y"], b + 1)
                sp.dma_start(ys_d.rearrange("(b p) n -> b p n", p=P)[ds(b, 1)].rearrange("b p n -> p (b n)"), yst[:]).then_inc(S["yout"], 16)

            load(0, 0)
            load(1, 1)
            with sp.Fori(1, NI) as i:
                for q in range(2):
                    sp.wait_ge(S["d_mm"], 2 * i + q - 1)
                    load(2 * i + q, q)
                    store(2 * i + q - 2)
            store(NB - 2)
            store(NB - 1)
            sp.wait_ge(S["yout"], 16 * NB)

        @block.gpsimd
        def _(pool):
            slots = slot_d.rearrange("(b p) o -> b p o", p=P)
            for b in range(NB):
                if b:
                    pool.wait_ge(S["xt_mm"], b)
                pool.dma_start(idx[:, 0:1], slots[b], allow_slow_non_contiguous=True).then_inc(S["idx"], 16)
                pool.wait_ge(S["idx"], 16 * b + 16)
                pool.indirect_dma_start(out=xg[:], out_offset=None, in_=n2_d,
                                        in_offset=bass.IndirectOffsetOnAxis(ap=idx[:, 0:1].bitcast(U32), axis=0)).then_inc(S["xg"], 16)

        @block.scalar
        def _(act):
            with act.Fori(0, NI) as i:
                for q in range(2):
                    b = 2 * i + q
                    act.wait_ge(S["xt_mm"], b + 1)
                    act.wait_ge(S["gu_mm"], b)
                    for kc in range(KC):
                        ins = act.activation(xT[q][:, kc, :], ps[:, 2 + kc // 4, (kc % 4) * P:(kc % 4 + 1) * P], ACT.Identity,
                                             bias=modc[:, 2, kc:kc + 1], scale=modc[:, 3, kc:kc + 1])
                    ins.then_inc(S["xT"], 1)
                    act.wait_ge(S["gu_mm"], b + 1)
                    act.wait_ge(S["hid"], b)
                    act.activation(sil[:], bank(0), ACT.Silu).then_inc(S["sil"], 1)

        @block.vector
        def _(dve):
            def out_rows(b):
                dve.wait_ge(S["d_mm"], b + 1)
                dve.wait_ge(S["yout"], 16 * b)
                dve.tensor_copy(yst[:], banks(6)).then_inc(S["y"], 1)

            def hidden(b):
                dve.wait_ge(S["sil"], b + 1)
                dve.wait_ge(S["ht_mm"], b)
                dve.tensor_tensor(hid[:], sil[:], bank(1), ALU.mult).then_inc(S["hid"], 1)
                dve.wait_ge(S["ht_mm"], b + 1)
                dve.wait_ge(S["d_mm"], b)
                dve.tensor_copy(hidT[:].rearrange("p k t -> p (k t)"), bank(4)).then_inc(S["hidT"], 1)

            hidden(0)
            with dve.Fori(1, NB) as b:
                out_rows(b - 1)
                hidden(b)
            out_rows(NB - 1)

        @block.tensor
        def _(pe):
            def turn(b):
                pe.wait_ge(S["xg"], 16 * b + 16)
                pe.wait_ge(S["xT"], b)
                for kc in range(KC):
                    ins = pe.transpose(ps[:, 2 + kc // 4, (kc % 4) * P:(kc % 4 + 1) * P], xg[:, kc * P:(kc + 1) * P], k["ident"])
                ins.then_inc(S["xt_mm"], 1)

            def gate_up(b, q, n):
                pe.wait_ge(S["xT"], b + 1)
                pe.wait_ge(full[q][0], 16 * n)
                pe.wait_ge(S["hid"], b)
                for kc in range(KC):
                    pe.matmul(bank(0), xT[q][:, kc, :], wg[q][:, kc, :], start=(kc == 0), stop=(kc == KC - 1))
                pe.wait_ge(full[q][1], 16 * n)
                for kc in range(KC):
                    ins = pe.matmul(bank(1), xT[q][:, kc, :], wu[q][:, kc, :], start=(kc == 0), stop=(kc == KC - 1))
                ins.then_inc(S["gu_mm"], 1)

            def turn_hidden(b):
                pe.wait_ge(S["hid"], b + 1)
                for kc in range(FC):
                    ins = pe.transpose(ps[:, 4, kc * P:(kc + 1) * P], hid[:, kc * P:(kc + 1) * P], k["ident"])
                ins.then_inc(S["ht_mm"], 1)

            def down(b, q, n):
                pe.wait_ge(S["hidT"], b + 1)
                pe.wait_ge(full[q][2], 16 * n)
                pe.wait_ge(S["y"], b)
                for h in range(2):
                    for kc in range(FC):
                        ins = pe.matmul(bank(6 + h), hidT[:, kc, :], wd[q][:, kc, h * 512:(h + 1) * 512], start=(kc == 0), stop=(kc == FC - 1))
                ins.then_inc(S["d_mm"], 1)

            turn(0)
            gate_up(0, 0, 1)
            turn(1)
            turn_hidden(0)
            gate_up(1, 1, 1)
            turn(2)
            down(0, 0, 1)
            turn_hidden(1)
            def two_blocks(i, last=False):
                gate_up(2 * i, 0, i + 1)
                turn(2 * i + 1)
                down(2 * i - 1, 1, i)
                turn_hidden(2 * i)
                gate_up(2 * i + 1, 1, i + 1)
                if not last:
                    turn(2 * i + 2)
                down(2 * i, 0, i + 1)
                turn_hidden(2 * i + 1)

            with pe.Fori(1, NI - 1) as i:
                two_blocks(i)
            two_blocks(NI - 1, last=True)
            down(NB - 1, 1, NI)


def combine(sb, env, x1, dest, wts, ys_d, gate2_d, out):
    nc, a, row, sem = (env[n] for n in ("nc", "a", "row", "sem"))
    ya = [sb(f"ya{i}", [P, D]) for i in range(2)]
    yb = [sb(f"ybb{i}", [P, D]) for i in range(2)]
    f = sb("f", [P, 2, D])
    rows = sb("rows3", [P, 2, D])
    gate2b = sb("gate2b2", [P, D])
    st = sb("st3", [P, 2, 6])
    mv = sb("mv3", [P, 2])
    names = "rows_in g_in fetched0 fetched1 sum stat sd chain n s1 fin out0 out1".split()
    S = {n: sem("f_" + n) for n in names}
    with nc.Block() as block:
        @block.sync
        def _(sp):
            sp.dma_start(rows[:, 0, :], row("ln2_g")).then_inc(S["rows_in"], 16)
            sp.dma_start(rows[:, 1, :], row("ln2_b")).then_inc(S["rows_in"], 16)
            sp.dma_start(gate2b[:], gate2_d).then_inc(S["g_in"], 16)
            for i in range(NT):
                sp.wait_ge(S["fin"], i + 1)
                sp.dma_start(out[i * P:(i + 1) * P, :], f[:, i % 2, :]).then_inc(S[f"out{i % 2}"], 16)
            for q in range(2):
                sp.wait_ge(S[f"out{q}"], 16 * NT // 2)

        @block.gpsimd
        def _(pool):
            pool.wait_ge(S["rows_in"], 32)

            def fetch(i):
                if i >= 2:
                    pool.wait_ge(S["n"], i - 1)
                for c, t in enumerate((ya[i % 2], yb[i % 2])):
                    pool.indirect_dma_start(out=t[:], out_offset=None, in_=ys_d,
                                            in_offset=bass.IndirectOffsetOnAxis(ap=dest[:, c, i:i + 1].bitcast(U32), axis=0)) \
                        .then_inc(S[f"fetched{i % 2}"], 16)

            fetch(0)
            for i in range(NT):
                if i + 1 < NT:
                    fetch(i + 1)
                pool.wait_ge(S["n"], i + 1)
                pool.tensor_tensor(f[:, i % 2, :], f[:, i % 2, :], rows[:, 0, :], ALU.mult).then_inc(S["s1"], 1)
                pool.wait_ge(S["s1"], i + 1)
                pool.tensor_tensor(f[:, i % 2, :], f[:, i % 2, :], rows[:, 1, :], ALU.add).then_inc(S["fin"], 1)

        @block.scalar
        def _(act):
            for i in range(NT):
                act.wait_ge(S["stat"], i + 1)
                act.activation(mv[:, 1:2], mv[:, 1:2], ACT.Sqrt).then_inc(S["sd"], 1)

        @block.vector
        def _(dve):
            chain = [0]

            def link(ins):
                chain[0] += 1
                ins.then_inc(S["chain"], 1)
                dve.wait_ge(S["chain"], chain[0])

            dve.wait_ge(S["g_in"], 16)
            for i in range(NT):
                q = i % 2
                dve.wait_ge(S[f"fetched{q}"], 32 * (i // 2 + 1))
                link(dve.tensor_scalar(ya[q][:], ya[q][:], wts[:, 0, i:i + 1], None, ALU.mult))
                link(dve.scalar_tensor_tensor(out=ya[q][:], in0=yb[q][:], scalar=wts[:, 1, i:i + 1], in1=ya[q][:], op0=ALU.mult, op1=ALU.add))
                link(dve.tensor_tensor(ya[q][:], ya[q][:], gate2b[:], ALU.mult))
                link(dve.scalar_tensor_tensor(out=ya[q][:], in0=x1[:, i, :], scalar=ALPHA, in1=ya[q][:], op0=ALU.mult, op1=ALU.add))
                for h in range(2):
                    ins = dve.bn_stats(st[:, h, :], ya[q][:, h * 512:(h + 1) * 512])
                link(ins)
                link(dve.bn_aggr(mv[:], st[:].rearrange("p a b -> p (a b)")))
                dve.tensor_scalar(mv[:, 1:2], mv[:, 1:2], LN_EPS, None, ALU.add).then_inc(S["stat"], 1)
                dve.wait_ge(S["sd"], i + 1)
                link(dve.reciprocal(mv[:, 1:2], mv[:, 1:2]))
                if i >= 2:
                    dve.wait_ge(S[f"out{q}"], 16 * (i // 2))
                dve.tensor_scalar(f[:, q, :], ya[q][:], mv[:, 0:1], mv[:, 1:2], ALU.subtract, ALU.mult).then_inc(S["n"], 1)
                dve.wait_ge(S["n"], i + 1)


def kernel(**inputs):
    import concourse.bacc as _bacc
    from concourse.bass_utils import run_bass_kernel_spmd as _run

    v = {n: np.asarray(x) for n, x in inputs.items()}

    def chunks(w):
        return np.ascontiguousarray(w.reshape(KC, P, -1, P).transpose(2, 1, 0, 3)).reshape(-1, P, KC * P)

    def cols(x):
        return x.reshape(-1, P).T

    b_mod = v["b_mod"][0].reshape(6, D)
    col_of = {"mu": v["rwkv_mu"][0], "w0": v["w0"][0], "a0": v["a0"][0], "k_k": v["k_k"][0], "k_a": v["k_a"][0],
              "r_k": v["r_k"][0].reshape(-1), "gn_g": v["gn_g"][0], "gn_b": v["gn_b"][0], "shift1": b_mod[0],
              "scale1": b_mod[1], "shift2": b_mod[3], "scale2": b_mod[4], "c": v["c"][0]}
    row_of = {"sg_ln_g": v["sg_ln_g"][0], "sg_ln_b": v["sg_ln_b"][0], "gate1": b_mod[2], "gate2": b_mod[5],
              "ln1_g": v["ln1_g"][0], "ln1_b": v["ln1_b"][0], "ln2_g": v["ln2_g"][0], "ln2_b": v["ln2_b"][0],
              "router_b": v["router_b"]}
    table, chunk_start, small, token = constants()
    arrays = {
        "x": v["x"][0], "w_mod": chunks(v["w_mod"][0]), "w_in": chunks(v["w_in"][0])[Z_ORDER],
        "cols": np.concatenate([cols(col_of[n]) for n in COLS], axis=1),
        "rows": np.concatenate([row_of[n] for n in ROWS]),
        "table": table, "chunk_start": chunk_start, "small": small, "token": token,
        "w2": v["w2"][0], "a2": v["a2"][0], "g2": v["g2"][0],
        "w_s": v["w_s"][0].transpose(2, 0, 1), "b_s": v["b_s"][0],
        "w_branch_a": v["w_branch_a"][0], "w_branch_b": v["w_branch_b"][0], "w_out": v["w_out"][0],
        "router_w": v["router_w"], "e_gate": v["e_gate"][0], "e_up": v["e_up"][0], "e_down": v["e_down"][0],
    }
    arrays = {f"{n}_dram": np.ascontiguousarray(x) for n, x in arrays.items()}
    nc = _bacc.Bacc("TRN2", target_bir_lowering=False, num_devices=1)
    a = {n[:-5]: nc.dram_tensor(n, x.shape, mybir.dt.from_np(x.dtype), kind="ExternalInput").ap() for n, x in arrays.items()}
    out = nc.dram_tensor("out_dram", (T, D), F32, kind="ExternalOutput").ap()
    build(nc, a, out)
    r = _run(nc, [arrays], core_ids=[0])
    return r.results[0]["out_dram"].reshape(1, T, D)
```

```python
from contextlib import ExitStack

import numpy as np
import concourse.bass as bass
from concourse import mybir

F32 = mybir.dt.float32
F32R = mybir.dt.float32r
I32 = mybir.dt.int32
U32 = mybir.dt.uint32
ALU = mybir.AluOpType
ACT = mybir.ActivationFunctionType
AX = mybir.AxisListType
ds = bass.ds

P = 128
D = 1024
T = 1024
KC = D // P
NT = T // P
W = 512
NP = W // P
C = 64
NC = T // C
E = 16
EG = 4
F = 512
FC = F // P
NB = 2 * T // P + E
DECAY = float(np.exp(-0.5))
ALPHA = 2.0 ** 0.25
LN_EPS = 1e-5
GN_EPS = 64e-5
BIG = 1e30

CONSTS = ["ident", "up", "upinc", "upfull", "y8", "x8", "o8", "o16", "o32", "headones", "headmean", "ones", "causal"]
COLS = {}
for _name, _n in (("mu", 14), ("w0", 4), ("a0", 4), ("k_k", 4), ("k_a", 4), ("r_k", 4), ("gn_g", 4), ("gn_b", 4),
                  ("shift1", 8), ("scale1", 8), ("shift2", 8), ("scale2", 8), ("c", 8)):
    COLS[_name] = (sum(n for _, n in COLS.values()), _n)
NCOL = sum(n for _, n in COLS.values())
ROWS = {}
for _name, _n in (("sg_ln_g", W), ("sg_ln_b", W), ("gate1", D), ("gate2", D), ("ln1_g", D), ("ln1_b", D),
                  ("ln2_g", D), ("ln2_b", D), ("router_b", E)):
    ROWS[_name] = (sum(n for _, n in ROWS.values()), _n)
NROW = sum(n for _, n in ROWS.values())
Z_ORDER = [12, 13] + [p + 4 * s for p in range(NP) for s in range(3)] + [18, 19, 20, 21] + [14, 15, 16, 17] \
    + list(range(30, 38)) + list(range(22, 30))
Z_V, Z_U, Z_GATE = 14, 18, 22


def constants():
    i = np.arange(P)
    row, col = i[:, None], i[None, :]
    same = lambda n: row // n == col // n
    m = {
        "ident": row == col,
        "up": (row < col) & same(C),
        "upinc": (row <= col) & same(C),
        "upfull": row < col,
        "y8": (row < col) & same(8),
        "x8": (row > col) & same(8),
        "o8": (row > col) & same(16) & ~same(8),
        "o16": (row > col) & same(32) & ~same(16),
        "o32": (row > col) & same(64) & ~same(32),
        "headones": same(64),
        "headmean": same(64) / 64.0,
        "ones": np.ones((P, P)),
        "causal": row <= col,
    }
    table = np.concatenate([np.asarray(m[n], np.float32) for n in CONSTS], axis=1)
    chunk_start = np.ones((P, T), np.float32)
    chunk_start[:, ::C] = 0.0
    small = np.zeros((P, 96), np.float32)
    small[:, 0:EG] = EG - np.arange(EG)
    small[:, EG:EG + E] = E - np.arange(E)
    token = np.arange(T, dtype=np.int32).reshape(NT, P).T.copy()
    return table, chunk_start, small, token


def build(nc, a, out):
    g_d = nc.dram_tensor("g_scratch", (NP, P, T), F32, kind="Internal").ap()
    bonus_d = nc.dram_tensor("bonus_scratch", (NP, P, T), F32, kind="Internal").ap()
    yb_d = nc.dram_tensor("yb_scratch", (NP, P, T), F32, kind="Internal").ap()
    gates_d = nc.dram_tensor("gates_scratch", (2 * KC, P, T), F32, kind="Internal").ap()
    x1_d = nc.dram_tensor("x1_scratch", (T // 2, D), F32, kind="Internal").ap()
    n2_d = nc.dram_tensor("n2_scratch", (T, D), F32, kind="Internal").ap()
    slot_d = nc.dram_tensor("slot_scratch", ((NB + 2) * P, 1), I32, kind="Internal").ap()
    ys_d = nc.dram_tensor("ys_scratch", ((NB + 1) * P, D), F32, kind="Internal").ap()

    with ExitStack() as top:
        sems = {}

        def sem(name):
            if name not in sems:
                sems[name] = nc.alloc_semaphore(name=name)
            return sems[name]

        def phase_ends(keep=()):
            nc.clear_and_free_semaphores([x for n, x in sems.items() if n not in keep])
            for n in [n for n in sems if n not in keep]:
                del sems[n]
            nc.all_engine_barrier()

        def tiles(stack):
            def sb(name, shape, dt=F32):
                return stack.enter_context(nc.sbuf_tensor(name, shape, dt))
            return sb

        sb = tiles(top)
        ps = top.enter_context(nc.psum_tensor("ps", [P, 8, 512], F32))
        consts = sb("consts", [P, len(CONSTS), P])
        cols = sb("cols", [P, NCOL])
        small = sb("small", [P, 96])
        modc = sb("modc", [P, 4, KC])
        k = {n: consts[:, i, :] for i, n in enumerate(CONSTS)}

        def col(name, i):
            return cols[:, COLS[name][0] + i:COLS[name][0] + i + 1]

        def row(name):
            s, n = ROWS[name]
            return a["rows"][s:s + n].partition_broadcast(P)

        def bank(b, n=512):
            return ps[:, b, 0:n]

        def banks(b):
            return ps[:, b:b + 2, :].rearrange("p a n -> p (a n)")

        with ExitStack() as mixer:
            msb = tiles(mixer)
            gate1b = msb("gate1b", [P, D])
            env = dict(nc=nc, a=a, ps=ps, k=k, cols=cols, col=col, row=row, bank=bank, banks=banks, sem=sem,
                       modc=modc, small=small, consts=consts, gate1b=gate1b, tiles=tiles, phase_ends=phase_ends)
            gate2_d = nc.dram_tensor("gate2_scratch", (P, D), F32, kind="Internal").ap()
            with ExitStack() as early:
                esb = tiles(early)
                rt = msb("rt", [P, NP, T])
                at, bt, kt, vt = (esb(n, [P, NP, T]) for n in ("at", "bt", "kt", "vt"))
                pc = esb("pc", [P, NP, NC])
                hT = esb("hT", [P, KC, T])
                ring = esb("ring", [P, 3, 2, KC, P])
                env.update(hT=hT, ring=ring, rt=rt, at=at, bt=bt, kt=kt, vt=vt, pc=pc)
                with ExitStack() as s:
                    project_and_gate(tiles(s), env, yb_d, gate2_d)
                    phase_ends()
                with ExitStack() as s:
                    prepare_recurrence(tiles(s), env, g_d, bonus_d)
                    phase_ends()
                with ExitStack() as s:
                    run_recurrence(tiles(s), env, gates_d, ys_d)
                    phase_ends()
            logits = msb("logits", [P, NT, E])
            with ExitStack() as s:
                x1b = tiles(s)("x1b", [P, NT // 2, D])
                x1 = [rt[:, i, :] if i < NT // 2 else x1b[:, i - NT // 2, :] for i in range(NT)]
                mix_branches(tiles(s), env, x1, x1_d, logits, g_d, bonus_d, yb_d, gates_d, n2_d)
                phase_ends()
            dest = msb("dest", [P, 2, NT], I32)
            wts = msb("wts", [P, 2, NT])
            bounds = msb("bounds", [1, 2 * E], I32)
            with ExitStack() as e:
                env["weights"] = expert_weights(tiles(e), env)
                with ExitStack() as s:
                    route(tiles(s), env, logits, dest, wts, bounds, slot_d)
                    phase_ends(keep=[n for n in sems if n.startswith("e_w")])
                with ExitStack() as s:
                    run_experts(tiles(s), env, bounds, slot_d, n2_d, ys_d, gate2_d)
                    phase_ends()
            with ExitStack() as s:
                combine(tiles(s), env, rt, x1_d, dest, wts, ys_d, out)
                phase_ends()


def project_and_gate(sb, env, yb_d, gate2_d):
    nc, a, ps, k, col, row, bank, banks, sem = (env[n] for n in ("nc", "a", "ps", "k", "col", "row", "bank", "banks", "sem"))
    modc, hT, ring, gate1b = env["modc"], env["hT"], env["ring"], env["gate1b"]
    rt, at, bt, kt, vt = (env[n] for n in ("rt", "at", "bt", "kt", "vt"))
    xs, xn = kt[:, 0:2, :], kt[:, 2:4, :]
    gateb, gate2b = vt[:, 0, :], vt[:, 1, :]
    vg = rt[:].rearrange("p q (a n) -> p (q a) n", n=W)
    u, yb = at[:, 0:2, :], bt[:, 0:2, :]
    macc = [x.rearrange("p a t -> p (a t)") for x in (at[:, 2:4, :], kt[:, 0:2, :], bt[:, 2:4, :])]
    stats = sb("stats", [P, NT, 2, 6])
    mv = sb("mv", [P, NT, 2])
    cond = sb("cond", [P, KC])
    mod_w = sb("mod_w", [P, 3, 2 * D])
    last_w = sb("last_w", [P, 2, KC, P])
    vstats = sb("vstats", [P, NT, 6])
    vmv = sb("vmv", [P, NT, 2])
    lng = sb("lng", [P, W])
    lnb = sb("lnb", [P, W])
    wst = sb("wst", [P, 8, P])
    bsb = sb("bsb", [P, NP, P])

    consts_in, x_in, x_norm, x_turned = sem("consts_in"), [sem("x_in0"), sem("x_in1")], sem("x_norm"), sem("x_turned")
    x_stats, x_rstd, h_evac, h_ready = sem("x_stats"), sem("x_rstd"), sem("h_evac"), sem("h_ready")
    w_in_slot = [sem(f"w_slot{i}") for i in range(4)]
    mod_slot = [sem(f"mod_slot{i}") for i in range(3)]
    cond_ready, mod_acc, mod_mm, mod_ready = sem("cond_ready"), sem("mod_acc"), sem("mod_mm"), sem("mod_ready")
    v_mm, v_gelu, v_var, v_rstd, v_norm, v_scaled = (sem(n) for n in ("v_mm", "v_gelu", "v_var", "v_rstd", "v_norm", "v_scaled"))
    u_mm, u_gelu, s_mm, s_read, yb_ready = (sem(n) for n in ("u_mm", "u_gelu", "s_mm", "s_read", "yb_ready"))
    yb_out, dve_chain, pool_chain, gate2_out = [sem("yb_out0"), sem("yb_out1")], sem("dve_chain0"), sem("pool_chain0"), sem("gate2_out")
    rows_in = sem("rows_in")
    z_w = [ring[:, 0], ring[:, 1], ring[:, 2], last_w[:]]

    def weights_here(eng, n):
        eng.wait_ge(w_in_slot[n], 16)

    with nc.Block() as block:
        @block.sync
        def _(sp):
            sp.dma_start(env["consts"][:], a["table"].rearrange("p (n q) -> p n q", q=P)).then_inc(consts_in, 16)
            sp.dma_start(env["cols"][:], a["cols"]).then_inc(consts_in, 16)
            sp.dma_start(env["small"][:], a["small"]).then_inc(consts_in, 16)

            def load_mod(n):
                if n >= 3:
                    sp.wait_ge(mod_acc, n - 2)
                j, kc = divmod(n, KC)
                sp.dma_start(mod_w[:, n % 3, :], a["w_mod"][kc * P:(kc + 1) * P, j * 2 * D:(j + 1) * 2 * D]).then_inc(mod_slot[n % 3], 16)

            for n in range(KC):
                load_mod(n)
            for n, g in enumerate((Z_V, Z_V + 2, Z_U, Z_U + 2)):
                sp.dma_start(z_w[n].rearrange("p c k n -> p c (k n)"), a["w_in"][g:g + 2].rearrange("c p n -> p c n")).then_inc(w_in_slot[n], 16)
            for n in range(KC, 3 * KC):
                load_mod(n)
            for i in range(2):
                sp.wait_ge(yb_out[i], 32)
            sp.wait_ge(gate2_out, 16)

        @block.scalar
        def _(act):
            for i in range(NT):
                if i >= 2:
                    act.wait_ge(x_norm, i - 1)
                act.dma_start(xs[:, i % 2, :], a["x"][i * P:(i + 1) * P, :]).then_inc(x_in[i % 2], 16)
                if i == 0:
                    act.dma_start(gateb, row("gate1")).then_inc(rows_in, 16)
                    act.dma_start(gate2b, row("gate2")).then_inc(rows_in, 16)
                    act.dma_start(lng[:], row("sg_ln_g")).then_inc(rows_in, 16)
                    act.dma_start(lnb[:], row("sg_ln_b")).then_inc(rows_in, 16)
                    act.dma_start(wst[:], a["w_s"]).then_inc(rows_in, 16)
                    for h in range(2):
                        act.dma_start(bsb[64 * h:64 * h + 64], a["b_s"].rearrange("(g h) t -> h g t", h=2)[h].partition_broadcast(64)).then_inc(rows_in, 16)
                    act.wait_ge(consts_in, 48)
                    act.activation(cond[:], env["cols"][:, COLS["c"][0]:COLS["c"][0] + KC], ACT.Silu).then_inc(cond_ready, 1)
                act.wait_ge(x_stats, i + 1)
                act.activation(mv[:, i, 1:2], mv[:, i, 1:2], ACT.Sqrt).then_inc(x_rstd, 1)
                if i >= 1:
                    act.wait_ge(x_turned, i)
                    act.copy(hT[:, :, (i - 1) * P:i * P], banks(2 * ((i - 1) % 2)).rearrange("p (k t) -> p k t", k=KC)).then_inc(h_evac, 1)
            act.wait_ge(x_turned, NT)
            act.copy(hT[:, :, (NT - 1) * P:], banks(2 * ((NT - 1) % 2)).rearrange("p (k t) -> p k t", k=KC)).then_inc(h_evac, 1)
            act.wait_ge(mod_ready, 1)
            act.wait_ge(h_evac, NT)
            for kc in range(1, KC, 2):
                act.activation(hT[:, kc, :], hT[:, kc, :], ACT.Identity, bias=modc[:, 0, kc:kc + 1], scale=modc[:, 1, kc:kc + 1]).then_inc(h_ready, 1)
            for i in range(NT):
                act.wait_ge(v_mm, i + 1)
                act.activation(vg[:, i, :], bank(i % 4), ACT.Gelu_apprx_tanh).then_inc(v_gelu, 1)
            for p in range(NP):
                if p >= 2:
                    act.wait_ge(yb_ready, p - 1)
                for h in range(2):
                    act.wait_ge(u_mm, 2 * p + h + 1)
                    act.activation(u[:, p % 2, h * 512:(h + 1) * 512], bank((2 * p + h) % 4), ACT.Gelu_apprx_tanh).then_inc(u_gelu, 1)
                if p == 0:
                    act.wait_ge(v_var, 1)
                    act.activation(vmv[:, :, 1:2], vmv[:, :, 1:2], ACT.Sqrt).then_inc(v_rstd, 1)
            for p in range(NP):
                act.wait_ge(yb_ready, p + 1)
                act.dma_start(yb_d[p], yb[:, p % 2, :]).then_inc(yb_out[p % 2], 16)
            act.wait_ge(mod_ready, 2)
            act.dma_start(gate2_d, gate2b).then_inc(gate2_out, 16)

        @block.vector
        def _(dve):
            chain = [0]

            def link(ins):
                chain[0] += 1
                ins.then_inc(dve_chain, 1)
                dve.wait_ge(dve_chain, chain[0])

            def mod_row(n):
                j, kc = divmod(n, KC)
                dve.wait_ge(mod_slot[n % 3], 16 * (n // 3 + 1))
                if kc == 0:
                    dve.tensor_scalar(macc[j], mod_w[:, n % 3, :], cond[:, kc:kc + 1], None, ALU.mult).then_inc(mod_acc, 1)
                else:
                    dve.wait_ge(mod_acc, n)
                    dve.scalar_tensor_tensor(out=macc[j], in0=mod_w[:, n % 3, :], scalar=cond[:, kc:kc + 1], in1=macc[j],
                                             op0=ALU.mult, op1=ALU.add).then_inc(mod_acc, 1)

            def mod_column(i, name, plus, src):
                return dve.scalar_tensor_tensor(out=modc[:, i, :], in0=src, scalar=plus,
                                                in1=env["cols"][:, COLS[name][0]:COLS[name][0] + KC], op0=ALU.add, op1=ALU.add)

            dve.wait_ge(cond_ready, 1)
            for i in range(NT):
                dve.wait_ge(x_in[i % 2], 16 * (i // 2 + 1))
                for h in range(2):
                    ins = dve.bn_stats(stats[:, i, h, :], xs[:, i % 2, h * 512:(h + 1) * 512])
                link(ins)
                link(dve.bn_aggr(mv[:, i, :], stats[:, i, :, :].rearrange("p a b -> p (a b)")))
                dve.tensor_scalar(mv[:, i, 1:2], mv[:, i, 1:2], LN_EPS, None, ALU.add).then_inc(x_stats, 1)
                dve.wait_ge(x_rstd, i + 1)
                link(dve.reciprocal(mv[:, i, 1:2], mv[:, i, 1:2]))
                if i >= 2:
                    dve.wait_ge(x_turned, i - 1)
                dve.tensor_scalar(xn[:, i % 2, :], xs[:, i % 2, :], mv[:, i, 0:1], mv[:, i, 1:2], ALU.subtract, ALU.mult).then_inc(x_norm, 1)
                mod_row(i)
            dve.wait_ge(mod_mm, 1)
            mod_column(0, "shift1", 0.0, ps[:, 4, 0:KC])
            mod_column(1, "scale1", 1.0, ps[:, 4, KC:2 * KC]).then_inc(mod_ready, 1)
            dve.wait_ge(mod_ready, 1)
            dve.wait_ge(h_evac, NT)
            for kc in range(0, KC, 2):
                dve.tensor_scalar(hT[:, kc, :], hT[:, kc, :], modc[:, 1, kc:kc + 1], modc[:, 0, kc:kc + 1], ALU.mult, ALU.add).then_inc(h_ready, 1)
            for i in range(NT):
                dve.wait_ge(v_gelu, i + 1)
                ins = dve.bn_stats(vstats[:, i, :], vg[:, i, :])
                if i == NT - 1:
                    link(ins)
                mod_row(KC + i)
            for i in range(NT):
                ins = dve.bn_aggr(vmv[:, i, :], vstats[:, i, :])
            link(ins)
            dve.tensor_scalar(vmv[:, :, 1:2], vmv[:, :, 1:2], LN_EPS, None, ALU.add).then_inc(v_var, 1)
            dve.wait_ge(v_rstd, 1)
            link(dve.reciprocal(vmv[:, :, 1:2], vmv[:, :, 1:2]))
            for i in range(NT):
                dve.tensor_scalar(vg[:, i, :], vg[:, i, :], vmv[:, i, 0:1], vmv[:, i, 1:2], ALU.subtract, ALU.mult).then_inc(v_norm, 1)
            for n in range(2 * KC, 3 * KC):
                mod_row(n)
            for p in range(NP):
                dve.wait_ge(s_mm, p + 1)
                if p >= 2:
                    dve.wait_ge(yb_out[p % 2], 16)
                dve.wait_ge(rows_in, 112)
                dve.tensor_tensor(yb[:, p % 2, :].rearrange("p (n t) -> p n t", t=P), banks(4 + 2 * (p % 2)).rearrange("p (n t) -> p n t", t=P),
                                  bsb[:, p, :].unsqueeze(1).to_broadcast([P, NT, P]), ALU.add).then_inc(s_read, 1)
                dve.wait_ge(s_read, p + 1)
                dve.wait_ge(u_gelu, 2 * p + 2)
                dve.tensor_tensor(yb[:, p % 2, :], yb[:, p % 2, :], u[:, p % 2, :], ALU.mult).then_inc(yb_ready, 1)
            dve.wait_ge(mod_mm, 2)
            dve.scalar_tensor_tensor(out=gate1b[:], in0=banks(4), scalar=1.0, in1=gateb, op0=ALU.add, op1=ALU.add)
            dve.scalar_tensor_tensor(out=gate2b, in0=banks(0), scalar=1.0, in1=gate2b, op0=ALU.add, op1=ALU.add)
            mod_column(2, "shift2", 0.0, ps[:, 6, 0:KC])
            mod_column(3, "scale2", 1.0, ps[:, 6, KC:2 * KC]).then_inc(mod_ready, 1)
            dve.wait_ge(mod_ready, 2)

        @block.gpsimd
        def _(pool):
            pool.wait_ge(rows_in, 112)
            pool.wait_ge(consts_in, 48)
            pool.tensor_tensor(wst[:], wst[:], k["causal"].unsqueeze(1).to_broadcast([P, 8, P]), ALU.mult)
            for i in range(NT):
                pool.wait_ge(v_norm, i + 1)
                pool.tensor_tensor(vg[:, i, :], vg[:, i, :], lng[:], ALU.mult).then_inc(pool_chain, 1)
                pool.wait_ge(pool_chain, i + 1)
                pool.tensor_tensor(vg[:, i, :], vg[:, i, :], lnb[:], ALU.add).then_inc(v_scaled, 1)

        @block.tensor
        def _(pe):
            pe.wait_ge(consts_in, 48)
            for i in range(NT):
                pe.wait_ge(x_norm, i + 1)
                if i >= 2:
                    pe.wait_ge(h_evac, i - 1)
                for kc in range(KC):
                    b = 2 * (i % 2) + kc // 4
                    ins = pe.transpose(ps[:, b, (kc % 4) * P:(kc % 4 + 1) * P], xn[:, i % 2, kc * P:(kc + 1) * P], k["ident"])
                ins.then_inc(x_turned, 1)

            def mod_columns(j, at_, b, c0):
                for c in range(KC):
                    ins = pe.matmul(ps[:, b, c0 + c:c0 + c + 1], macc[j][:, at_ + c * P:at_ + (c + 1) * P], k["ones"][:, 0:1], start=True, stop=True)
                return ins

            def mod_row(j, at_, b):
                for h in range(2):
                    ins = pe.matmul(bank(b + h), k["ones"], macc[j][:, at_ + h * 512:at_ + (h + 1) * 512], start=True, stop=True)
                return ins

            pe.wait_ge(mod_acc, KC)
            mod_columns(0, 0, 4, 0)
            mod_columns(0, D, 4, KC).then_inc(mod_mm, 1)
            pe.wait_ge(h_ready, KC)
            weights_here(pe, 0)
            weights_here(pe, 1)
            pe.wait_ge(h_evac, NT)
            for i in range(NT):
                if i >= 4:
                    pe.wait_ge(v_gelu, i - 3)
                for half in range(2):
                    for kc in range(KC):
                        ins = pe.matmul(ps[:, i % 4, half * 256:half * 256 + 256], hT[:, kc, i * P:(i + 1) * P], z_w[half][:, :, kc, :],
                                        start=(kc == 0), stop=(kc == KC - 1))
                ins.then_inc(v_mm, 1)

            def mix(p):
                pe.wait_ge(v_scaled, NT)
                pe.wait_ge(rows_in, 112)
                if p >= 2:
                    pe.wait_ge(s_read, p - 1)
                if p < 2:
                    pe.wait_ge(mod_ready, 1)
                for i in range(NT):
                    for h in range(2):
                        g = 2 * p + h
                        ins = pe.matmul(ps[64 * h:64 * h + 64, 4 + 2 * (p % 2) + i // 4, (i % 4) * P:(i % 4 + 1) * P],
                                        vg[:, i, 64 * g:64 * g + 64], wst[:, g, :], start=True, stop=True)
                ins.then_inc(s_mm, 1)

            for p in range(NP):
                n = 2 + p // 2
                weights_here(pe, n)
                for h in range(2):
                    m = 2 * p + h
                    pe.wait_ge(v_gelu, NT)
                    if m >= 4:
                        pe.wait_ge(u_gelu, m - 3)
                    for kc in range(KC):
                        ins = pe.matmul(bank(m % 4), z_w[n][:, p % 2, kc, :], hT[:, kc, h * 512:(h + 1) * 512], start=(kc == 0), stop=(kc == KC - 1))
                    ins.then_inc(u_mm, 1)
            for p in range(NP):
                mix(p)
            pe.wait_ge(mod_acc, 3 * KC)
            pe.wait_ge(s_read, NP)
            pe.wait_ge(u_gelu, 2 * NP)
            mod_row(1, 0, 4)
            mod_row(2, D, 0)
            mod_columns(1, D, 6, 0)
            mod_columns(2, 0, 6, KC).then_inc(mod_mm, 1)


def prepare_recurrence(sb, env, g_d, bonus_d):
    nc, a, ps, k, col, row, bank, banks, sem = (env[n] for n in ("nc", "a", "ps", "k", "col", "row", "bank", "banks", "sem"))
    hT, ring, rt, at, bt, kt, vt, pc = (env[n] for n in ("hT", "ring", "rt", "at", "bt", "kt", "vt", "pc"))
    reset = sb("reset", [P, T])
    zraw = sb("zraw", [P, 2, T + 1])
    dz = sb("dz", [P, T])
    wa = sb("wa", [P, T])
    sg = sb("sg", [P, T])
    lora = sb("lora", [P, W])
    g2 = sb("g2", [P, W])
    L = sb("L", [P, T])
    kk = sb("kk", [P, T])
    t1 = sb("t1", [P, T])
    ein = sb("ein", [P, T])
    gst = sb("gst", [P, T])
    bst = sb("bst", [P, T])
    oka = sb("oka", [P, NP])
    names = ("p_reset_in p_lora_in p_z_mm p_z_evac p_z_mixed p_thw p_sg p_q_mm p_a_mm p_g_mm p_ss_mm p_bs_mm p_dl p_a p_L p_Lx p_ein p_en p_ex "
             "p_g_evac p_kkraw p_sq p_nrm p_kkn p_t1 p_b1 p_bonus p_at p_bt p_kt p_rt p_bta p_zero p_chain p_kmod").split()
    S = {n: sem(n) for n in names}
    w_slot = [sem(f"p_w_slot{i}") for i in range(3)]
    g_out, b_out = sem("p_g_out"), sem("p_b_out")
    NZ = 14
    dst_of = [None, None] + [t for p in range(NP) for t in ((rt, p), (kt, p), (vt, p))]

    with nc.Block() as block:
        @block.sync
        def _(sp):
            sp.dma_start(reset[:], a["chunk_start"]).then_inc(S["p_reset_in"], 16)
            sp.dma_start(lora[0:64, :], a["w2"]).then_inc(S["p_lora_in"], 16)
            sp.dma_start(lora[64:128, :], a["a2"]).then_inc(S["p_lora_in"], 16)
            sp.dma_start(g2[:], a["g2"]).then_inc(S["p_lora_in"], 16)
            for n in range(NZ // 2):
                if n >= 3:
                    sp.wait_ge(S["p_z_mm"], 4 * (n - 2))
                sp.dma_start(ring[:, n % 3].rearrange("p c k n -> p c (k n)"), a["w_in"][2 * n:2 * n + 2].rearrange("c p n -> p c n")).then_inc(w_slot[n % 3], 16)
            for p in range(NP):
                sp.wait_ge(S["p_g_evac"], p + 1)
                sp.dma_start(g_d[p], gst[:]).then_inc(g_out, 16)
                sp.wait_ge(S["p_bonus"], p + 1)
                sp.dma_start(bonus_d[p], bst[:]).then_inc(b_out, 16)
            sp.wait_ge(g_out, 16 * NP)
            sp.wait_ge(b_out, 16 * NP)

        @block.tensor
        def _(pe):
            def z(n):
                if n % 2 == 0:
                    pe.wait_ge(w_slot[n // 2 % 3], 16 * (n // 2 // 3 + 1))
                for h in range(2):
                    m = 2 * n + h
                    if m >= 4:
                        pe.wait_ge(S["p_z_evac"], m - 3)
                    for kc in range(KC):
                        ins = pe.matmul(bank(m % 4), ring[:, n // 2 % 3, n % 2, kc, :], hT[:, kc, h * 512:(h + 1) * 512], start=(kc == 0), stop=(kc == KC - 1))
                    ins.then_inc(S["p_z_mm"], 1)

            def both(b, lhsT, rhs, done):
                for h in range(2):
                    ins = pe.matmul(bank(b + h), lhsT, rhs[:, h * 512:(h + 1) * 512], start=True, stop=True)
                ins.then_inc(S[done], 1)

            z(0)
            z(1)
            z(2)
            for p in range(NP):
                if p == 0:
                    pe.wait_ge(S["p_thw"], 1)
                    pe.wait_ge(S["p_z_mixed"], 2)
                    pe.wait_ge(S["p_lora_in"], 48)
                if p >= 1:
                    pe.wait_ge(S["p_bonus"], p)
                    pe.wait_ge(S["p_g_evac"], p)
                both(4, lora[0:64, p * P:(p + 1) * P], wa[0:64, :], "p_q_mm")
                both(6, lora[64:128, p * P:(p + 1) * P], wa[64:128, :], "p_a_mm")
                z(3 + 3 * p)
                pe.wait_ge(S["p_sg"], 1)
                pe.wait_ge(S["p_a"], p + 1)
                both(6, g2[:, p * P:(p + 1) * P], sg[:], "p_g_mm")
                z(4 + 3 * p)
                pe.wait_ge(S["p_dl"], p + 1)
                pe.wait_ge(S["p_sq"], p + 1)
                both(4, k["headones"], t1[:], "p_ss_mm")
                if p + 1 < NP:
                    z(5 + 3 * p)
                pe.wait_ge(S["p_b1"], p + 1)
                pe.wait_ge(S["p_nrm"], p + 1)
                both(4, k["headones"], dz[:], "p_bs_mm")

        @block.scalar
        def _(act):
            def evac(n):
                if n >= 2:
                    act.wait_ge(S["p_z_mixed"], n - 1)
                if n == 0:
                    act.wait_ge(S["p_zero"], 1)
                for h in range(2):
                    act.wait_ge(S["p_z_mm"], 2 * n + h + 1)
                    act.copy(zraw[:, n % 2, 1 + h * 512:1 + (h + 1) * 512], bank((2 * n + h) % 4)).then_inc(S["p_z_evac"], 1)

            evac(0)
            evac(1)
            act.wait_ge(S["p_z_mixed"], 1)
            act.activation(wa[0:64, :], wa[0:64, :], ACT.Tanh).then_inc(S["p_thw"], 1)
            act.wait_ge(S["p_z_mixed"], 2)
            act.activation(sg[:], sg[:], ACT.Sigmoid).then_inc(S["p_sg"], 1)
            evac(2)
            for p in range(NP):
                dl, ap_ = at[:, p, :], bt[:, p, :]
                act.wait_ge(S["p_q_mm"], p + 1)
                act.activation(dl, banks(4), ACT.Sigmoid, bias=col("w0", p)).then_inc(S["p_dl"], 1)
                act.wait_ge(S["p_a_mm"], p + 1)
                act.activation(ap_, banks(6), ACT.Sigmoid, bias=col("a0", p)).then_inc(S["p_a"], 1)
                act.wait_ge(S["p_L"], p + 1)
                if p:
                    act.wait_ge(S["p_rt"], p)
                act.activation(ein[:], L[:], ACT.Exp, scale=-DECAY).then_inc(S["p_ein"], 1)
                evac(3 + 3 * p)
                act.wait_ge(S["p_g_mm"], p + 1)
                if p:
                    act.wait_ge(g_out, 16 * p)
                act.copy(gst[:], banks(6)).then_inc(S["p_g_evac"], 1)
                act.wait_ge(S["p_Lx"], p + 1)
                act.activation(dl, dl, ACT.Exp, scale=-DECAY).then_inc(S["p_ex"], 1)
                act.wait_ge(S["p_ein"], p + 1)
                act.activation(L[:], L[:], ACT.Exp, scale=DECAY).then_inc(S["p_en"], 1)
                evac(4 + 3 * p)
                act.wait_ge(S["p_ss_mm"], p + 1)
                act.activation(t1[:], banks(4), ACT.Sqrt).then_inc(S["p_nrm"], 1)
                if p + 1 < NP:
                    evac(5 + 3 * p)

        @block.gpsimd
        def _(pool):
            for p in range(NP):
                pool.wait_ge(S["p_kkraw"], p + 1)
                if p:
                    pool.wait_ge(S["p_kt"], p)
                    pool.wait_ge(S["p_bt"], p)
                pool.tensor_tensor(t1[:], kk[:], kk[:], ALU.mult).then_inc(S["p_sq"], 1)
                pool.wait_ge(S["p_b1"], p + 1)
                pool.wait_ge(S["p_ein"], p + 1)
                pool.tensor_tensor(rt[:, p, :], rt[:, p, :], ein[:], ALU.mult)
                pool.tensor_copy(pc[:, p, :], ein[:, C - 1::C]).then_inc(S["p_rt"], 1)

        @block.vector
        def _(dve):
            chain = [0]

            def link(ins):
                chain[0] += 1
                ins.then_inc(S["p_chain"], 1)
                dve.wait_ge(S["p_chain"], chain[0])

            dve.memset(zraw[:, :, 0:1], 0.0).then_inc(S["p_zero"], 1)
            link(dve.tensor_scalar(oka[:], env["cols"][:, COLS["k_a"][0]:COLS["k_a"][0] + NP], -1.0, 1.0, ALU.mult, ALU.add))

            def mixed(n):
                dve.wait_ge(S["p_z_evac"], 2 * n + 2)
                c = Z_ORDER[n]
                dst = (wa[:], sg[:])[n] if n < 2 else dst_of[n][0][:, dst_of[n][1], :]
                link(dve.tensor_tensor(dz[:], zraw[:, n % 2, 0:T], zraw[:, n % 2, 1:T + 1], ALU.subtract))
                dve.scalar_tensor_tensor(out=dst, in0=dz[:], scalar=col("mu", c), in1=zraw[:, n % 2, 1:T + 1], op0=ALU.mult, op1=ALU.add) \
                    .then_inc(S["p_z_mixed"], 1)
                dve.wait_ge(S["p_z_mixed"], n + 1)

            dve.wait_ge(S["p_zero"], 1)
            mixed(0)
            mixed(1)
            dve.wait_ge(S["p_reset_in"], 16)
            for p in range(NP):
                r_, k_, v_ = rt[:, p, :], kt[:, p, :], vt[:, p, :]
                dl, ap_ = at[:, p, :], bt[:, p, :]
                if p:
                    dve.wait_ge(S["p_bs_mm"], p)
                mixed(2 + 3 * p)
                dve.wait_ge(S["p_dl"], p + 1)
                dve.tensor_tensor_scan(L[:], reset[:], dl, 0.0, ALU.mult, ALU.add).then_inc(S["p_L"], 1)
                dve.wait_ge(S["p_L"], p + 1)
                dve.tensor_tensor(dl, L[:], dl, ALU.subtract).then_inc(S["p_Lx"], 1)
                mixed(3 + 3 * p)
                dve.tensor_scalar(kk[:], k_, col("k_k", p), None, ALU.mult).then_inc(S["p_kkraw"], 1)
                dve.wait_ge(S["p_a"], p + 1)
                link(dve.tensor_scalar(bst[:], ap_, col("k_a", p), oka[:, p:p + 1], ALU.mult, ALU.add) if not p else
                     _after(dve, b_out, 16 * p).tensor_scalar(bst[:], ap_, col("k_a", p), oka[:, p:p + 1], ALU.mult, ALU.add))
                link(dve.tensor_tensor(k_, k_, bst[:], ALU.mult))
                mixed(4 + 3 * p)
                dve.scalar_tensor_tensor(out=dz[:], in0=r_, scalar=col("r_k", p), in1=k_, op0=ALU.mult, op1=ALU.mult).then_inc(S["p_b1"], 1)
                dve.wait_ge(S["p_nrm"], p + 1)
                link(dve.tensor_scalar(t1[:], t1[:], 1e-12, None, ALU.max))
                link(dve.reciprocal(t1[:], t1[:]))
                link(dve.tensor_tensor(kk[:], kk[:], t1[:], ALU.mult))
                dve.wait_ge(S["p_ex"], p + 1)
                dve.scalar_tensor_tensor(out=at[:, p, :], in0=kk[:], scalar=-1.0, in1=dl, op0=ALU.mult, op1=ALU.mult).then_inc(S["p_at"], 1)
                link(dve.tensor_tensor(t1[:], kk[:], ap_, ALU.mult))
                dve.wait_ge(S["p_bs_mm"], p + 1)
                dve.tensor_tensor(bst[:], banks(4), v_, ALU.mult).then_inc(S["p_bonus"], 1)
                dve.wait_ge(S["p_en"], p + 1)
                dve.tensor_tensor(bt[:, p, :], t1[:], L[:], ALU.mult).then_inc(S["p_bt"], 1)
                dve.tensor_tensor(k_, k_, L[:], ALU.mult).then_inc(S["p_kt"], 1)
                dve.wait_ge(S["p_kt"], p + 1)


def _after(eng, s, value):
    eng.wait_ge(s, value)
    return eng


def run_recurrence(sb, env, gates_d, ys_d):
    nc, a, ps, k, col, row, bank, banks, sem = (env[n] for n in ("nc", "a", "ps", "k", "col", "row", "bank", "banks", "sem"))
    hT, ring, rt, at, bt, kt, vt, pc = (env[n] for n in ("hT", "ring", "rt", "at", "bt", "kt", "vt", "pc"))
    m = {n: sb("m_" + n, [P, NP, P]) for n in "abd bbd kbd rbd vbd bhbd khbd x2 X o8 o16 o32 Y RB AK RK y2 x4 R V BH KH S".split()}
    xraw, Tt, Z, U0, U, SPC = m["x2"], m["x2"], m["y2"], m["x4"], m["Y"], m["X"]
    gst = sb("gst2", [P, 2, 512])
    nought = sb("nought", [P, P])
    names = ("abd bbd kbd rbd vbd bhbd khbd y0_mm x0_mm rb_mm ak_mm rk_mm v_tr bh_tr kh_tr xraw X offs Y R1 RB AK RK V BH KH x2_mm y2_mm x2 y2 "
             "x4_mm r2_mm x4 R2 r4_mm R4 T_mm Z_mm T Z rz_mm R u0_mm U0 u_mm U sp_mm y_mm SPC S yout gate_mm gate_sig init").split()
    S = {n: sem("c_" + n) for n in names}
    gw = [sem("c_gw0"), sem("c_gw1")]
    g_out = [sem("c_g_out0"), sem("c_g_out1")]
    nought_ready, zeros_out = sem("c_nought"), sem("c_zeros_out")
    NI = NC // 2

    signals = {
        "sync": (),
        "gpsimd": "abd vbd bhbd offs SPC".split(),
        "scalar": "kbd rbd xraw V BH KH x2 x4 T U0 U yout gate_sig".split(),
        "vector": "bbd khbd Y R1 X RB AK RK y2 R2 R4 Z R S".split(),
        "tensor": [n for n in names if n.endswith("_mm") or n.endswith("_tr")],
    }

    def start_at_one(eng, which):
        for n in signals[which]:
            eng.sem_inc(S[n], 1)

    def quads(b):
        return ps[:, b, :].rearrange("p (q n) -> p q n", q=NP)

    def mask(name):
        return k[name].unsqueeze(1).to_broadcast([P, NP, P])

    def diag(t, h):
        return t[64 * h:64 * h + 64, :, 64 * h:64 * h + 64]

    def chunk(t, c, h):
        return t[64 * h:64 * h + 64, :, ds(c * C, C)]

    def decay(c, h):
        return pc[64 * h:64 * h + 64, :, ds(c, 1)].to_broadcast([64, NP, C])

    with nc.Block() as block:
        @block.sync
        def _(sp):
            for h in range(2):
                sp.sem_inc(g_out[h], 16)
            def load(c, q):
                sp.dma_start(ring[:, q, 0].rearrange("p k n -> p (k n)"), a["w_in"][ds(c + Z_GATE, 1)].rearrange("c p n -> p (c n)")).then_inc(gw[q], 16)

            def store(c):
                for h in range(2):
                    sp.wait_ge(S["gate_sig"], 2 * c + h + 2)
                    sp.dma_start(gates_d[ds(c, 1), :, h * 512:(h + 1) * 512].rearrange("c p n -> p (c n)"), gst[:, h, :]).then_inc(g_out[h], 16)

            load(0, 0)
            load(1, 1)
            sp.wait_ge(nought_ready, 1)
            sp.dma_start(ys_d[E * P:, :].rearrange("(p b) (n c) -> p (b n) c", p=P, c=P),
                         nought[:].unsqueeze(1).to_broadcast([P, (NB + 1 - E) * KC, P])).then_inc(zeros_out, 16)
            with sp.Fori(0, NI - 1) as i:
                for q in range(2):
                    store(2 * i + q)
                    load(2 * i + q + 2, q)
            store(NC - 2)
            store(NC - 1)
            for h in range(2):
                sp.wait_ge(g_out[h], 16 * NC + 16)
            sp.wait_ge(zeros_out, 16)

        @block.gpsimd
        def _(pool):
            start_at_one(pool, "gpsimd")
            pool.memset(nought[:], 0.0).then_inc(nought_ready, 1)
            for n in "abd bbd kbd rbd vbd bhbd khbd S".split():
                ins = pool.memset(m[n][:], 0.0)
            ins.then_inc(S["init"], 1)
            pool.wait_ge(S["init"], 1)

            def body(c):
                pool.wait_ge(S["u0_mm"], c + 1)
                pool.wait_ge(S["SPC"], c + 1)
                for h in range(2):
                    ins = pool.tensor_copy(diag(m["abd"], h), chunk(at, c, h))
                ins.then_inc(S["abd"], 1)
                pool.wait_ge(S["abd"], c + 2)
                pool.wait_ge(S["v_tr"], c + 1)
                for h in range(2):
                    ins = pool.tensor_copy(diag(m["vbd"], h), chunk(vt, c, h))
                ins.then_inc(S["vbd"], 1)
                pool.wait_ge(S["vbd"], c + 2)
                pool.wait_ge(S["init"], 1)
                pool.wait_ge(S["bh_tr"], c + 1)
                for h in range(2):
                    ins = pool.tensor_tensor(diag(m["bhbd"], h), chunk(bt, c, h), decay(c, h), ALU.mult)
                ins.then_inc(S["bhbd"], 1)
                pool.wait_ge(S["bhbd"], c + 2)
                pool.wait_ge(S["xraw"], c + 2)
                pool.wait_ge(S["Z_mm"], 3 * c + 1)
                for n in ("o8", "o16", "o32"):
                    ins = pool.tensor_tensor(m[n][:], xraw[:], mask(n), ALU.mult)
                ins.then_inc(S["offs"], 1)
                pool.wait_ge(S["init"], 1)
                pool.wait_ge(S["S"], c + 1)
                pool.wait_ge(S["R2"], c + 2)
                pool.tensor_tensor(SPC[:], m["S"][:], pc[:, :, ds(c, 1)].to_broadcast([P, NP, P]), ALU.mult).then_inc(S["SPC"], 1)

            with pool.Fori(0, NC) as c:
                body(c)

        @block.scalar
        def _(act):
            start_at_one(act, "scalar")
            act.wait_ge(S["init"], 1)

            def sigmoid(c, h):
                act.wait_ge(S["gate_mm"], 2 * c + h + 2)
                act.wait_ge(g_out[h], 16 * c + 16)
                act.activation(gst[:, h, :], bank(6 + h), ACT.Sigmoid).then_inc(S["gate_sig"], 1)

            def body(c):
                for n, src, last, at_ in (("kbd", kt, "rk_mm", c), ("rbd", rt, "y_mm", c)):
                    act.wait_ge(S["init"], 1)
                    act.wait_ge(S[last], at_ + 1)
                    for h in range(2):
                        ins = act.copy(diag(m[n], h), chunk(src, c, h))
                    ins.then_inc(S[n], 1)

                def evac(b, ready, value, dst, done):
                    act.wait_ge(S[ready], value + 1)
                    act.copy(dst[:], quads(b)).then_inc(S[done], 1)

                act.wait_ge(S["rz_mm"], 3 * c + 1)
                evac(1, "x0_mm", c + 1, xraw, "xraw")
                act.wait_ge(S["y_mm"], c + 1)
                evac(4, "v_tr", c + 1, m["V"], "V")
                act.wait_ge(S["sp_mm"], c + 1)
                evac(0, "bh_tr", c + 1, m["BH"], "BH")
                evac(1, "kh_tr", c + 1, m["KH"], "KH")
                act.wait_ge(S["X"], c + 2)
                act.wait_ge(S["offs"], c + 2)
                evac(2, "x2_mm", c + 1, m["x2"], "x2")
                act.wait_ge(S["u_mm"], c + 1)
                evac(4, "x4_mm", c + 1, m["x4"], "x4")
                for j in range(3):
                    if j == 0:
                        act.wait_ge(S["r2_mm"], c + 2)
                        act.wait_ge(S["x4_mm"], c + 2)
                    evac(1, "T_mm", 3 * c + j + 1, Tt, "T")
                    if j == 0:
                        sigmoid(c, 0)
                act.wait_ge(S["r4_mm"], c + 2)
                evac(4, "u0_mm", c + 1, U0, "U0")
                evac(5, "u_mm", c + 1, U, "U")
                sigmoid(c, 1)
                act.wait_ge(S["init"], 1)
                act.wait_ge(S["y_mm"], c + 2)
                for h in range(2):
                    ins = act.copy(chunk(rt, c, h), quads(4)[64 * h:64 * h + 64, :, 64 * h:64 * h + 64])
                ins.then_inc(S["yout"], 1)

            with act.Fori(0, NC) as c:
                body(c)

        @block.vector
        def _(dve):
            start_at_one(dve, "vector")
            dve.wait_ge(S["init"], 1)

            def body(c):
                dve.wait_ge(S["rb_mm"], c + 1)
                for h in range(2):
                    ins = dve.tensor_copy(diag(m["bbd"], h), chunk(bt, c, h))
                ins.then_inc(S["bbd"], 1)
                dve.wait_ge(S["kh_tr"], c + 1)
                for h in range(2):
                    ins = dve.tensor_tensor(diag(m["khbd"], h), chunk(kt, c, h), decay(c, h), ALU.mult)
                ins.then_inc(S["khbd"], 1)

                def masked(b, ready, dst, name, done):
                    dve.wait_ge(S[ready], c + 2)
                    dve.tensor_tensor(dst[:], quads(b), mask(name), ALU.mult).then_inc(S[done], 1)

                dve.wait_ge(S["y_mm"], c + 1)
                masked(0, "y0_mm", m["Y"], "y8", "Y")
                dve.wait_ge(S["Y"], c + 2)
                dve.wait_ge(S["u_mm"], c + 1)
                dve.tensor_tensor(m["R"][:], m["Y"][:], mask("ident"), ALU.add).then_inc(S["R1"], 1)
                dve.wait_ge(S["xraw"], c + 2)
                dve.tensor_tensor(m["X"][:], xraw[:], mask("x8"), ALU.mult).then_inc(S["X"], 1)
                masked(2, "rb_mm", m["RB"], "upinc", "RB")
                masked(3, "ak_mm", m["AK"], "up", "AK")
                masked(5, "rk_mm", m["RK"], "upinc", "RK")
                dve.wait_ge(S["y2_mm"], c + 2)
                dve.wait_ge(S["rz_mm"], 3 * c + 1)
                dve.tensor_copy(m["y2"][:], quads(3)).then_inc(S["y2"], 1)
                dve.wait_ge(S["r2_mm"], c + 2)
                dve.wait_ge(S["R1"], c + 2)
                dve.tensor_tensor(m["R"][:], m["R"][:], quads(5), ALU.add).then_inc(S["R2"], 1)
                dve.wait_ge(S["r4_mm"], c + 2)
                dve.wait_ge(S["R2"], c + 2)
                dve.tensor_tensor(m["R"][:], m["R"][:], quads(0), ALU.add).then_inc(S["R4"], 1)
                dve.wait_ge(S["R4"], c + 2)
                for j in range(3):
                    dve.wait_ge(S["Z_mm"], 3 * c + j + 2)
                    dve.wait_ge(S["x4_mm"], c + 2)
                    dve.tensor_copy(Z[:], quads(2)).then_inc(S["Z"], 1)
                    dve.wait_ge(S["rz_mm"], 3 * c + j + 2)
                    dve.tensor_tensor(m["R"][:], m["R"][:], quads(3), ALU.add).then_inc(S["R"], 1)
                    dve.wait_ge(S["R"], 3 * c + j + 2)
                dve.wait_ge(S["SPC"], c + 2)
                dve.wait_ge(S["y_mm"], c + 2)
                dve.wait_ge(S["sp_mm"], c + 2)
                dve.tensor_tensor(m["S"][:], SPC[:], quads(0), ALU.add).then_inc(S["S"], 1)

            with dve.Fori(0, NC) as c:
                body(c)

        @block.tensor
        def _(pe):
            start_at_one(pe, "tensor")
            pe.wait_ge(S["init"], 1)

            def each(b, pairs, done, transpose=False):
                for p in range(NP):
                    dst = ps[:, b, p * P:(p + 1) * P]
                    for n, (x, y) in enumerate(pairs):
                        if transpose:
                            ins = pe.transpose(dst, m[x][:, p, :], k["ident"])
                        else:
                            xt, yt = (m[x] if isinstance(x, str) else x), (m[y] if isinstance(y, str) else y)
                            ins = pe.matmul(dst, xt[:, p, :], yt[:, p, :], start=(n == 0), stop=(n == len(pairs) - 1))
                ins.then_inc(S[done], 1)

            def body(c, q):
                def gate_products():
                    pe.wait_ge(gw[q], 16 * turns[0])
                    for h in range(2):
                        for kc in range(KC):
                            if kc == 0:
                                pe.wait_ge(S["gate_sig"], 2 * c + 1)
                            ins = pe.matmul(bank(6 + h), ring[:, q, 0, kc, :], hT[:, kc, h * 512:(h + 1) * 512], start=(kc == 0), stop=(kc == KC - 1))
                            if kc == KC - 1:
                                ins.then_inc(S["gate_mm"], 1)
                            yield

                work = gate_products()

                def fill(n=1):
                    for _ in range(n):
                        next(work, None)

                def need(**waits):
                    for n, v in waits.items():
                        pe.wait_ge(S[n], v + 1)

                fill(1)
                need(abd=c + 1, bbd=c + 1, S=c)
                each(0, [("bbd", "abd")], "y0_mm")
                need(T=3 * c)
                each(1, [("abd", "bbd")], "x0_mm")
                need(kbd=c + 1, rbd=c + 1, Z=3 * c, R=3 * c)
                each(2, [("bbd", "rbd")], "rb_mm")
                each(3, [("kbd", "abd")], "ak_mm")
                need(U=c)
                each(5, [("kbd", "rbd")], "rk_mm")
                need(vbd=c + 1, yout=c)
                each(4, [("vbd", None)], "v_tr", transpose=True)
                need(bhbd=c + 1, Y=c + 1)
                each(0, [("bhbd", None)], "bh_tr", transpose=True)
                need(khbd=c + 1, xraw=c + 1)
                each(1, [("khbd", None)], "kh_tr", transpose=True)
                fill(1)
                need(X=c + 1, RB=c + 1, AK=c + 1)
                each(2, [("Y", "X")], "x2_mm")
                each(3, [("X", "Y")], "y2_mm")
                fill(2)
                need(x2=c + 1, R1=c + 1, RK=c + 1)
                each(5, [("x2", "R")], "r2_mm")
                need(y2=c + 1, V=c + 1)
                each(4, [("y2", "x2")], "x4_mm")
                fill(1)
                need(x4=c + 1, R2=c + 1, BH=c + 1)
                each(0, [("x4", "R")], "r4_mm")
                fill(1)
                need(offs=c + 1, KH=c + 1)
                for j, off in enumerate(("o8", "o16", "o32")):
                    need(R4=c + 1) if j == 0 else need(R=3 * c + j)
                    each(1, [("R", None)], "T_mm", transpose=True)
                    each(2, [(off, "R")], "Z_mm")
                    fill(1)
                    need(T=3 * c + j + 1, Z=3 * c + j + 1)
                    each(3, [(Tt, Z)], "rz_mm")
                    fill(1)
                need(S=c)
                each(4, [("abd", "S"), ("AK", "V")], "u0_mm")
                fill(2)
                need(U0=c + 1, R=3 * c + 3)
                each(5, [("R", U0)], "u_mm")
                fill(2)
                need(U=c + 1)
                each(0, [("BH", U), ("KH", "V")], "sp_mm")
                each(4, [("S", "rbd"), (U, "RB"), ("V", "RK")], "y_mm")
                fill(16)

            turns = [None]
            with pe.Fori(0, NI) as i:
                turns[0] = i + 1
                for q in range(2):
                    body(2 * i + q, q)


def mix_branches(sb, env, x1, x1_d, logits, g_d, bonus_d, yb_d, gates_d, n2_d):
    nc, a, ps, k, col, row, bank, banks, sem = (env[n] for n in ("nc", "a", "ps", "k", "col", "row", "bank", "banks", "sem"))
    rt, modc, gate1b = env["rt"], env["modc"], env["gate1b"]
    yb = sb("yb2", [P, NP, T])
    mixed = sb("mixed", [P, KC, T])
    wab = sb("wab", [P, NP, D])
    wob = sb("wob", [P, KC, D // 2])
    gs = sb("gs", [P, 2, T])
    gg = sb("gg", [P, T])
    bo = sb("bo", [P, T])
    yc = sb("yc", [P, T])
    sq = sb("sq", [P, T])
    tmp = sb("tmp", [P, T])
    names = ("w_b w_a w_o yb_in gg_in bo_in mean_mm var_mm yc sq var sd gn ya pb_mm pa_mm mb ma mixed chain pchain "
             "gin0 gin1 eps").split()
    S = {n: sem("x_" + n) for n in names}
    with nc.Block() as block:
        @block.sync
        def _(sp):
            sp.dma_start(wab[:], a["w_branch_b"].rearrange("(k p) n -> p k n", p=P)).then_inc(S["w_b"], 16)
            sp.dma_start(yb[:], yb_d.rearrange("q p t -> p q t")).then_inc(S["yb_in"], 16)
            for n in range(2 * KC):
                if n >= 2:
                    sp.wait_ge(S["mb"], min(n - 1, KC))
                if n >= KC + 2:
                    sp.wait_ge(S["ma"], n - 1 - KC)
                sp.dma_start(gs[:, n % 2, :], gates_d[n]).then_inc(S[f"gin{n % 2}"], 16)
                if n == KC - 1:
                    sp.wait_ge(S["pb_mm"], KC)
                    sp.dma_start(wab[:], a["w_branch_a"].rearrange("(k p) n -> p k n", p=P)).then_inc(S["w_a"], 16)

        @block.scalar
        def _(act):
            for p in range(NP):
                if p:
                    act.wait_ge(S["ya"], p)
                act.dma_start(gg[:], g_d[p]).then_inc(S["gg_in"], 16)
                act.dma_start(bo[:], bonus_d[p]).then_inc(S["bo_in"], 16)
                act.wait_ge(S["var"], p + 1)
                act.activation(sq[:], sq[:], ACT.Sqrt).then_inc(S["sd"], 1)

        @block.gpsimd
        def _(pool):
            for p in range(NP):
                pool.wait_ge(S["yc"], p + 1)
                if p:
                    pool.wait_ge(S["gn"], p)
                pool.tensor_tensor(sq[:], yc[:], yc[:], ALU.mult).then_inc(S["sq"], 1)
                pool.wait_ge(S["gn"], p + 1)
                pool.wait_ge(S["bo_in"], 16 * (p + 1))
                pool.wait_ge(S["gg_in"], 16 * (p + 1))
                pool.tensor_tensor(yc[:], yc[:], bo[:], ALU.add).then_inc(S["pchain"], 1)
                pool.wait_ge(S["pchain"], p + 1)
                pool.tensor_tensor(rt[:, p, :], yc[:], gg[:], ALU.mult).then_inc(S["ya"], 1)

        @block.vector
        def _(dve):
            chain = [0]

            def link(ins):
                chain[0] += 1
                ins.then_inc(S["chain"], 1)
                dve.wait_ge(S["chain"], chain[0])

            def branch_b(j):
                dve.wait_ge(S["pb_mm"], j + 1)
                dve.wait_ge(S[f"gin{j % 2}"], 16 * (j // 2 + 1))
                dve.tensor_tensor(mixed[:, j, :], banks(4 + 2 * (j % 2)), gs[:, j % 2, :], ALU.mult).then_inc(S["mb"], 1)

            for p in range(NP):
                dve.wait_ge(S["mean_mm"], p + 1)
                if p:
                    dve.wait_ge(S["ya"], p)
                dve.tensor_tensor(yc[:], rt[:, p, :], banks(0), ALU.subtract).then_inc(S["yc"], 1)
                branch_b(2 * p)
                dve.wait_ge(S["var_mm"], p + 1)
                dve.tensor_scalar(sq[:], banks(2), GN_EPS, None, ALU.add).then_inc(S["var"], 1)
                branch_b(2 * p + 1)
                dve.wait_ge(S["sd"], p + 1)
                link(dve.reciprocal(sq[:], sq[:]))
                link(dve.tensor_tensor(yc[:], yc[:], sq[:], ALU.mult))
                dve.tensor_scalar(yc[:], yc[:], col("gn_g", p), col("gn_b", p), ALU.mult, ALU.add).then_inc(S["gn"], 1)
            for j in range(KC):
                dve.wait_ge(S["pa_mm"], j + 1)
                dve.wait_ge(S[f"gin{j % 2}"], 16 * ((KC + j) // 2 + 1))
                dve.tensor_tensor(tmp[:], banks(4 + 2 * (j % 2)), gs[:, j % 2, :], ALU.mult).then_inc(S["ma"], 1)
                dve.wait_ge(S["ma"], j + 1)
                dve.wait_ge(S["mb"], KC)
                link(dve.tensor_tensor(mixed[:, j, :], mixed[:, j, :], tmp[:], ALU.add))

        @block.tensor
        def _(pe):
            def heads(b, src, done):
                for h in range(2):
                    ins = pe.matmul(bank(b + h), k["headmean"], src[:, h * 512:(h + 1) * 512], start=True, stop=True)
                ins.then_inc(S[done], 1)

            def project(j, src, done):
                for h in range(2):
                    for q in range(NP):
                        ins = pe.matmul(bank(4 + 2 * (j % 2) + h), wab[:, q, j * P:(j + 1) * P], src[:, q, h * 512:(h + 1) * 512], start=(q == 0), stop=(q == NP - 1))
                ins.then_inc(S[done], 1)

            pe.wait_ge(S["w_b"], 16)
            pe.wait_ge(S["yb_in"], 16)
            for j in range(KC):
                p = j // 2
                if j % 2 == 0:
                    if p:
                        pe.wait_ge(S["yc"], p)
                    heads(0, rt[:, p, :], "mean_mm")
                if j >= 2:
                    pe.wait_ge(S["mb"], j - 1)
                project(j, yb, "pb_mm")
                if j % 2 == 0:
                    pe.wait_ge(S["sq"], p + 1)
                    if p:
                        pe.wait_ge(S["var"], p)
                    heads(2, sq[:], "var_mm")
            pe.wait_ge(S["w_a"], 16)
            pe.wait_ge(S["ya"], NP)
            for j in range(KC):
                if j < 2:
                    pe.wait_ge(S["mb"], KC)
                else:
                    pe.wait_ge(S["ma"], j - 1)
                project(j, rt, "pa_mm")

    env["phase_ends"]()
    rows = sb("rows", [P, 2, D])
    xs = sb("xs2", [P, D])
    n2 = sb("n2", [P, D])
    h2 = sb("h2", [P, KC, P])
    rw = sb("rw", [P, KC, E])
    st = sb("st", [P, 4, 6])
    mv = sb("mv2", [P, 2, 2])
    names = "x_in rows_in rw_in o_in o2_in o_mm stat sd lin x1r x1s x1 stat2 sd2 n2 n2_out n2_tr h2 r_mm chain res o_read x1_out".split()
    Q = {n: sem("o_" + n) for n in names}
    wo2 = yb
    wo_hi = yb[:].rearrange("p q (a n) -> p (q a) n", a=2)
    with nc.Block() as block:
        @block.sync
        def _(sp):
            w = a["w_out"].rearrange("(k p) n -> p k n", p=P)
            sp.dma_start(wob[:], w[:, :, 0:512]).then_inc(Q["o_in"], 16)
            sp.dma_start(wo_hi, w[:, :, 512:1024]).then_inc(Q["o2_in"], 16)
            sp.dma_start(rows[:, 0, :], row("ln1_g")).then_inc(Q["rows_in"], 16)
            sp.dma_start(rows[:, 1, :], row("ln1_b")).then_inc(Q["rows_in"], 16)
            sp.dma_start(rw[:], a["router_w"].rearrange("(k p) n -> p k n", p=P)).then_inc(Q["rw_in"], 16)
            for i in range(NT):
                if i:
                    sp.wait_ge(Q["res"], i)
                sp.dma_start(xs[:], a["x"][i * P:(i + 1) * P, :]).then_inc(Q["x_in"], 16)
                if i:
                    sp.wait_ge(Q["n2"], i)
                    sp.dma_start(n2_d[(i - 1) * P:i * P, :], n2[:]).then_inc(Q["n2_out"], 16)
                if i > NT // 2:
                    j = i - 1 - NT // 2
                    sp.dma_start(x1_d[j * P:(j + 1) * P, :], x1[i - 1]).then_inc(Q["x1_out"], 16)
            sp.wait_ge(Q["n2"], NT)
            sp.dma_start(n2_d[(NT - 1) * P:, :], n2[:]).then_inc(Q["n2_out"], 16)
            sp.dma_start(x1_d[(NT // 2 - 1) * P:, :], x1[NT - 1]).then_inc(Q["x1_out"], 16)
            sp.wait_ge(Q["x1_out"], 16 * (NT // 2))
            sp.wait_ge(Q["n2_out"], 16 * NT)

        @block.scalar
        def _(act):
            for i in range(NT):
                act.wait_ge(Q["stat"], i + 1)
                act.activation(mv[:, 0, 1:2], mv[:, 0, 1:2], ACT.Sqrt).then_inc(Q["sd"], 1)
                act.wait_ge(Q["stat2"], i + 1)
                act.activation(mv[:, 1, 1:2], mv[:, 1, 1:2], ACT.Sqrt).then_inc(Q["sd2"], 1)
                act.wait_ge(Q["n2_tr"], i + 1)
                if i:
                    act.wait_ge(Q["r_mm"], i)
                for kc in range(KC):
                    ins = act.activation(h2[:, kc, :], ps[:, 4 + kc // 4, (kc % 4) * P:(kc % 4 + 1) * P], ACT.Identity,
                                         bias=modc[:, 2, kc:kc + 1], scale=modc[:, 3, kc:kc + 1])
                ins.then_inc(Q["h2"], 1)

        @block.gpsimd
        def _(pool):
            pool.wait_ge(Q["rows_in"], 32)
            for i in range(NT):
                pool.wait_ge(Q["x1r"], i + 1)
                pool.tensor_tensor(x1[i], x1[i], rows[:, 0, :], ALU.mult).then_inc(Q["x1s"], 1)
                pool.wait_ge(Q["x1s"], i + 1)
                pool.tensor_tensor(x1[i], x1[i], rows[:, 1, :], ALU.add).then_inc(Q["x1"], 1)

        @block.vector
        def _(dve):
            chain = [0]

            def link(ins):
                chain[0] += 1
                ins.then_inc(Q["chain"], 1)
                dve.wait_ge(Q["chain"], chain[0])

            def norm(src, dst, w, stat, sd, i, done):
                for h in range(2):
                    ins = dve.bn_stats(st[:, 2 * w + h, :], src[:, h * 512:(h + 1) * 512])
                link(ins)
                link(dve.bn_aggr(mv[:, w, :], st[:, 2 * w:2 * w + 2, :].rearrange("p a b -> p (a b)")))
                dve.tensor_scalar(mv[:, w, 1:2], mv[:, w, 1:2], LN_EPS, None, ALU.add).then_inc(Q[stat], 1)
                dve.wait_ge(Q[sd], i + 1)
                link(dve.reciprocal(mv[:, w, 1:2], mv[:, w, 1:2]))
                return dve.tensor_scalar(dst, src, mv[:, w, 0:1], mv[:, w, 1:2], ALU.subtract, ALU.mult).then_inc(Q[done], 1)

            for i in range(NT):
                dve.wait_ge(Q["o_mm"], i + 1)
                dve.tensor_tensor(tmp[:], banks(2 * (i % 2)), gate1b[:], ALU.mult).then_inc(Q["o_read"], 1)
                dve.wait_ge(Q["o_read"], i + 1)
                dve.wait_ge(Q["x_in"], 16 * (i + 1))
                dve.scalar_tensor_tensor(out=tmp[:], in0=xs[:], scalar=ALPHA, in1=tmp[:], op0=ALU.mult, op1=ALU.add).then_inc(Q["res"], 1)
                dve.wait_ge(Q["res"], i + 1)
                norm(tmp[:], x1[i], 0, "stat", "sd", i, "x1r")
                dve.wait_ge(Q["x1"], i + 1)
                if i:
                    dve.wait_ge(Q["n2_out"], 16 * i)
                    dve.wait_ge(Q["n2_tr"], i)
                norm(x1[i], n2[:], 1, "stat2", "sd2", i, "n2")
            dve.wait_ge(Q["r_mm"], NT)
            link(dve.tensor_copy(logits[:].rearrange("p i e -> p (i e)"), bank(6, NT * E)))

        @block.tensor
        def _(pe):
            pe.wait_ge(Q["o_in"], 16)
            pe.wait_ge(Q["o2_in"], 16)

            def out_tile(i):
                if i >= 2:
                    pe.wait_ge(Q["o_read"], i - 1)
                for h, w in enumerate((wob[:], wo_hi)):
                    for kc in range(KC):
                        ins = pe.matmul(bank(2 * (i % 2) + h), mixed[:, kc, i * P:(i + 1) * P], w[:, kc, :], start=(kc == 0), stop=(kc == KC - 1))
                ins.then_inc(Q["o_mm"], 1)

            def turn(i):
                pe.wait_ge(Q["n2"], i + 1)
                if i:
                    pe.wait_ge(Q["h2"], i)
                else:
                    pe.wait_ge(Q["rw_in"], 16)
                for kc in range(KC):
                    ins = pe.transpose(ps[:, 4 + kc // 4, (kc % 4) * P:(kc % 4 + 1) * P], n2[:, kc * P:(kc + 1) * P], k["ident"])
                ins.then_inc(Q["n2_tr"], 1)

            def router(i):
                pe.wait_ge(Q["h2"], i + 1)
                for kc in range(KC):
                    ins = pe.matmul(ps[:, 6, i * E:(i + 1) * E], h2[:, kc, :], rw[:, kc, :], start=(kc == 0), stop=(kc == KC - 1))
                ins.then_inc(Q["r_mm"], 1)

            out_tile(0)
            out_tile(1)
            for i in range(NT):
                turn(i)
                if i + 2 < NT:
                    out_tile(i + 2)
                router(i)


def expert_weights(sb, env):
    nc, a = env["nc"], env["a"]
    w = [sb(f"w{n}", [P, KC, F] if n != "d" else [P, FC, D]) for n in "gud"]
    full = [env["sem"](f"e_w{n}") for n in "gud"]

    def load(sp, e, n):
        name = ("e_gate", "e_up", "e_down")[n]
        sp.dma_start(w[n][:], a[name][ds(e, 1)].rearrange("e (k p) f -> p (e k) f", p=P)).then_inc(full[n], 16)

    return w, full, load


def route(sb, env, logits, dest, wts, bounds, slot_d):
    nc, a, ps, k, row, sem, small = (env[n] for n in ("nc", "a", "ps", "k", "row", "sem", "small"))
    NE = NT * E
    t = {n: sb("r_" + n, [P, NE]) for n in "score sel gs eq eq2 masked M1 M2 M wk tot".split()}
    pair = sb("r_pair", [P, NT * EG, 3])
    base = sb("r_base", [P, NT + 1, E])
    nblk = sb("r_nblk", [P, E])
    bend = sb("r_bend", [P, E])
    bst = sb("r_bst", [P, E])
    first = sb("r_first", [P, E])
    one = sb("r_one", [P, E])
    gq = {n: sb("r_g" + n, [P, NT * EG]) for n in "abcd"}
    c8 = {n: sb("r_c" + n, [P, NT]) for n in "abc"}
    rb = sb("r_rb", [P, E])
    tok = sb("r_tok", [P, NT], I32)
    zero = sb("r_zero", [P, NB + 2], I32)
    names = "score rb_in tok_in slots_zeroed M_ready rank_mm chain dest zero scatter blocks".split()
    S = {n: sem("r_" + n) for n in names}
    prio_g, prio_e = small[:, 0:EG], small[:, EG:EG + E]

    def ie(x):
        return x[:].rearrange("p (i e) -> p i e", e=E)

    def ig(x):
        return x[:].rearrange("p (i g) -> p i g", g=EG)

    with nc.Block() as block:
        @block.sync
        def _(sp):
            sp.dma_start(rb[:], row("router_b")).then_inc(S["rb_in"], 16)
            sp.dma_start(tok[:], a["token"]).then_inc(S["tok_in"], 16)
            sp.wait_ge(S["zero"], 1)
            sp.dma_start(slot_d.rearrange("(p n) o -> p (n o)", p=P), zero[:]).then_inc(S["slots_zeroed"], 16)
            for n in range(3):
                env["weights"][2](sp, 0, n)

        @block.scalar
        def _(act):
            act.activation(t["score"][:], logits[:].rearrange("p i e -> p (i e)"), ACT.Sigmoid).then_inc(S["score"], 1)

        @block.tensor
        def _(pe):
            pe.wait_ge(S["M_ready"], 1)
            pe.matmul(ps[:, 0, 0:NE], k["upfull"], t["M"][:], start=True, stop=True)
            pe.matmul(ps[:, 1, 0:NE], k["ones"], t["M"][:], start=True, stop=True).then_inc(S["rank_mm"], 1)

        @block.gpsimd
        def _(pool):
            pool.memset(zero[:], 0).then_inc(S["zero"], 1)
            pool.wait_ge(S["dest"], 1)
            pool.wait_ge(S["tok_in"], 16)
            pool.wait_ge(S["slots_zeroed"], 16)
            for c in range(2):
                for i in range(NT):
                    pool.indirect_dma_start(out=slot_d, out_offset=bass.IndirectOffsetOnAxis(ap=dest[:, c, i:i + 1].bitcast(U32), axis=0),
                                            in_=tok[:, i:i + 1], in_offset=None).then_inc(S["scatter"], 16)
            pool.wait_ge(S["scatter"], 32 * NT)

        @block.vector
        def _(dve):
            chain = [0]

            def link(ins):
                chain[0] += 1
                ins.then_inc(S["chain"], 1)
                dve.wait_ge(S["chain"], chain[0])

            def tt(o, x, y, op):
                link(dve.tensor_tensor(o, x, y, op))

            dve.wait_ge(S["score"], 1)
            dve.wait_ge(S["rb_in"], 16)
            tt(ie(t["sel"]), ie(t["score"]), rb[:].unsqueeze(1).to_broadcast([P, NT, E]), ALU.add)
            x4 = t["sel"][:].rearrange("p (m e) -> p m e", e=4)
            ga, gb = gq["a"][:].unsqueeze(2), gq["b"][:]
            tt(pair[:], x4[:, :, 0:3], x4[:, :, 1:4], ALU.add)
            link(dve.tensor_reduce(gb, pair[:], AX.X, ALU.max))
            tt(pair[:, :, 0:2], x4[:, :, 0:2], x4[:, :, 2:4], ALU.add)
            tt(pair[:, :, 2:3], x4[:, :, 0:1], x4[:, :, 3:4], ALU.add)
            link(dve.tensor_reduce(gq["a"][:], pair[:], AX.X, ALU.max))
            tt(gb, gb, gq["a"][:], ALU.max)
            link(dve.tensor_reduce(c8["a"][:], ig(gq["b"]), AX.X, ALU.max))
            tt(ig(gq["c"]), ig(gq["b"]), c8["a"][:].unsqueeze(2).to_broadcast([P, NT, EG]), ALU.is_equal)
            tt(ig(gq["c"]), ig(gq["c"]), prio_g.unsqueeze(1).to_broadcast([P, NT, EG]), ALU.mult)
            link(dve.tensor_reduce(c8["a"][:], ig(gq["c"]), AX.X, ALU.max))
            tt(ig(gq["c"]), ig(gq["c"]), c8["a"][:].unsqueeze(2).to_broadcast([P, NT, EG]), ALU.is_equal)
            link(dve.tensor_scalar(gq["d"][:], gq["c"][:], -1.0, BIG, ALU.add, ALU.mult))
            tt(t["masked"][:].rearrange("p (m e) -> p m e", e=4), x4, gq["d"][:].unsqueeze(2).to_broadcast([P, NT * EG, 4]), ALU.add)
            for n, M in enumerate(("M1", "M2")):
                link(dve.tensor_reduce(c8["a"][:], ie(t["masked"]), AX.X, ALU.max))
                tt(ie(t["eq"]), ie(t["masked"]), c8["a"][:].unsqueeze(2).to_broadcast([P, NT, E]), ALU.is_equal)
                tt(ie(t["eq"]), ie(t["eq"]), prio_e.unsqueeze(1).to_broadcast([P, NT, E]), ALU.mult)
                link(dve.tensor_reduce(c8["a"][:], ie(t["eq"]), AX.X, ALU.max))
                tt(ie(t[M]), ie(t["eq"]), c8["a"][:].unsqueeze(2).to_broadcast([P, NT, E]), ALU.is_equal)
                if n == 0:
                    link(dve.scalar_tensor_tensor(out=t["masked"][:], in0=t[M][:], scalar=-BIG, in1=t["masked"][:], op0=ALU.mult, op1=ALU.add))
            dve.tensor_tensor(t["M"][:], t["M1"][:], t["M2"][:], ALU.add).then_inc(S["M_ready"], 1)
            for n, M in enumerate(("M1", "M2")):
                tt(t["wk"][:], t["score"][:], t[M][:], ALU.mult)
                link(dve.tensor_reduce(wts[:, n, :], ie(t["wk"]), AX.X, ALU.add))
            tt(c8["b"][:], wts[:, 0, :], wts[:, 1, :], ALU.add)
            link(dve.reciprocal(c8["b"][:], c8["b"][:]))
            for n in range(2):
                tt(wts[:, n, :], wts[:, n, :], c8["b"][:], ALU.mult)
            link(dve.memset(base[:, 0, :], 0.0))
            link(dve.memset(one[:], 1.0))
            link(dve.memset(nblk[:], 0.0))
            dve.wait_ge(S["rank_mm"], 1)
            for i in range(NT):
                tt(base[:, i + 1, :], base[:, i, :], ps[:, 1, i * E:(i + 1) * E], ALU.add)
            link(dve.tensor_scalar(nblk[:], nblk[:], 1.0, None, ALU.add))
            for j in range(1, T // P):
                link(dve.scalar_tensor_tensor(out=nblk[:], in0=base[:, NT, :], scalar=float(P * j), in1=nblk[:], op0=ALU.is_gt, op1=ALU.add))
            link(dve.tensor_tensor_scan(bend[:], one[:], nblk[:], 0.0, ALU.mult, ALU.add))
            tt(first[:], bend[:], nblk[:], ALU.subtract)
            link(dve.tensor_scalar(bst[:], first[:], float(P), None, ALU.mult))
            tt(ie(t["wk"]), ps[:, 0, 0:NE].rearrange("p (i e) -> p i e", e=E), base[:, 0:NT, :], ALU.add)
            tt(ie(t["wk"]), ie(t["wk"]), bst[:].unsqueeze(1).to_broadcast([P, NT, E]), ALU.add)
            for n, M in enumerate(("M1", "M2")):
                tt(t["eq"][:], t["wk"][:], t[M][:], ALU.mult)
                link(dve.tensor_reduce(c8["c"][:], ie(t["eq"]), AX.X, ALU.add))
                ins = dve.tensor_copy(dest[:, n, :], c8["c"][:])
                if n == 0:
                    link(ins)
            ins.then_inc(S["dest"], 1)
            link(dve.tensor_copy(bounds[:, 0:E], first[0:1, :]))
            link(dve.tensor_scalar(bend[:], bend[:], -1.0, None, ALU.add))
            link(dve.tensor_copy(bounds[:, E:], bend[0:1, :]))


def run_experts(sb, env, bounds, slot_d, n2_d, ys_d, gate2_d):
    nc, a, ps, k, bank, banks, sem, modc = (env[n] for n in ("nc", "a", "ps", "k", "bank", "banks", "sem", "modc"))
    raw, full, load = env["weights"]
    hi, lo = ([sb(f"w{n}_{part}", [P, KC, F] if n != "d" else [P, FC, D], F32R) for n in "gud"] for part in ("hi", "lo"))
    GATE, UP, DOWN = range(3)
    HI, LO = ("wg_hi", "wu_hi", "wd_hi"), ("wg_lo", "wu_lo", "wd_lo")
    FIRST, LAST = range(2)
    gate2b = env["gate1b"]
    slots = sb("slots", [P, NB + 2], I32)
    idx = sb("idx", [P, 1], I32)
    xg = sb("xg", [P, D])
    xT = sb("xT", [P, KC, P])
    x_hi, x_lo = (sb(f"x_{n}", [P, KC, P], F32R) for n in ("hi", "lo"))
    sil = sb("sil", [P, F])
    hid = sb("hid", [P, F])
    h_hi, h_lo = (sb(f"h_{n}", [P, FC, P], F32R) for n in ("hi", "lo"))
    yst = sb("yst", [P, D])
    signals = {"tensor": "xt_mm g_mm gu_mm ht_mm d_mm", "scalar": "xT x_hi sil h_hi wg_hi wu_hi wd_hi",
               "vector": "x_lo hid h_lo y wg_lo wu_lo wd_lo", "gpsimd": "idx xg", "sync": "yout"}
    S = {n: sem("e_" + n) for names in signals.values() for n in names.split()}
    g_in, slots_in = sem("e_gate2"), sem("e_slots")

    by_dma = ("xg", "yout")
    starts = {n: 0 if n in ("idx", "xg") else 16 if n == "yout" else 1 for n in S}
    ys_rows = ys_d.rearrange("(b p) n -> b p n", p=P)

    def start_above_zero(eng, which):
        for n in signals[which].split():
            if starts[n]:
                eng.sem_inc(S[n], starts[n])

    def need(eng, **counts):
        for n, count in counts.items():
            eng.wait_ge(S[n], (16 * count if n in by_dma else count) + starts[n])

    def bound(eng, e, which):
        return eng.value_load(bounds[0:1, ds(e + E * which, 1)], min_val=0, max_val=NB - 1)

    def total(eng):
        return bound(eng, E - 1, LAST) + 1

    def over_blocks(eng, steps):
        def expert(e, following):
            first, last = bound(eng, e, FIRST), bound(eng, e, LAST)
            with eng.If(first < last):
                with eng.Fori(first, last) as b:
                    steps(b, e, None)
            steps(last, e, following)

        with eng.Fori(0, E - 1) as e:
            expert(e, e + 1)
        expert(E - 1, None)

    def half(t, h):
        n = t.shape[1] // 2
        return t[:, h * n:(h + 1) * n, :]

    with nc.Block() as block:
        @block.sync
        def _(sp):
            start_above_zero(sp, "sync")
            sp.dma_start(slots[:], slot_d.rearrange("(b p) o -> p (b o)", p=P), allow_slow_non_contiguous=True).then_inc(slots_in, 16)
            sp.dma_start(gate2b[:], gate2_d).then_inc(g_in, 16)
            with sp.Fori(1, E) as e:
                for n in range(3):
                    sp.wait_ge(S[LO[n]], 2 * e + 1)
                    load(sp, e, n)

        @block.gpsimd
        def _(pool):
            start_above_zero(pool, "gpsimd")
            pool.wait_ge(slots_in, 16)
            with pool.Fori(1, total(pool) + 2) as n:
                pool.wait_ge(slots_in, 16)
                pool.wait_ge(S["xt_mm"], n)
                pool.tensor_copy(idx[:], slots[:, ds(n - 1, 1)]).then_inc(S["idx"], 1)
                pool.wait_ge(slots_in, 16)
                pool.wait_ge(S["idx"], n)
                pool.indirect_dma_start(out=xg[:], out_offset=None, in_=n2_d,
                                        in_offset=bass.IndirectOffsetOnAxis(ap=idx[:].bitcast(U32), axis=0)).then_inc(S["xg"], 16)
            need(pool, yout=total(pool))

        @block.scalar
        def _(act):
            start_above_zero(act, "scalar")

            def inputs(b, used):
                need(act, xt_mm=b + 1, gu_mm=used, x_lo=used)
                for kc in range(KC):
                    ins = act.activation(xT[:, kc, :], ps[:, 2 + kc // 4, (kc % 4) * P:(kc % 4 + 1) * P], ACT.Identity,
                                         bias=modc[:, 2, kc:kc + 1], scale=modc[:, 3, kc:kc + 1])
                ins.then_inc(S["xT"], 1)
                need(act, xT=b + 1)
                act.copy(x_hi[:], xT[:]).then_inc(S["x_hi"], 1)

            def split(e, n, used):
                act.wait_ge(full[n], 16 * (e + 1))
                need(act, **{("g_mm", "gu_mm", "d_mm")[n]: used})
                for h in range(2):
                    act.copy(half(hi[n], h), half(raw[n], h)).then_inc(S[HI[n]], 1)

            def steps(b, e, following):
                need(act, g_mm=b + 1, hid=b)
                act.activation(sil[:], bank(0), ACT.Silu).then_inc(S["sil"], 1)
                if following is not None:
                    split(following, GATE, b + 1)
                need(act, ht_mm=b + 1, d_mm=b)
                act.copy(h_hi[:].rearrange("p k t -> p (k t)"), bank(4)).then_inc(S["h_hi"], 1)
                inputs(b + 1, b + 1)
                if following is not None:
                    split(following, UP, b + 1)
                need(act, y=b + 1)
                act.dma_start(ys_rows[ds(b, 1)].rearrange("b p n -> p (b n)"), yst[:]).then_inc(S["yout"], 16)
                if following is not None:
                    split(following, DOWN, b + 1)

            split(0, GATE, 0)
            inputs(0, 0)
            split(0, UP, 0)
            split(0, DOWN, 0)
            over_blocks(act, steps)

        @block.vector
        def _(dve):
            start_above_zero(dve, "vector")

            def split(e, n):
                for h in range(2):
                    dve.wait_ge(S[HI[n]], 2 * e + h + 2)
                    dve.tensor_tensor(half(lo[n], h), half(raw[n], h), half(hi[n], h).bitcast(F32), ALU.subtract).then_inc(S[LO[n]], 1)

            def inputs(b, used):
                need(dve, x_hi=b + 1, gu_mm=used)
                dve.tensor_tensor(x_lo[:], xT[:], x_hi[:].bitcast(F32), ALU.subtract).then_inc(S["x_lo"], 1)

            def steps(b, e, following):
                need(dve, sil=b + 1, gu_mm=b + 1, ht_mm=b)
                dve.tensor_tensor(hid[:], sil[:], bank(1), ALU.mult).then_inc(S["hid"], 1)
                need(dve, h_hi=b + 1, d_mm=b)
                dve.tensor_tensor(h_lo[:].rearrange("p k t -> p (k t)"), bank(4), h_hi[:].bitcast(F32).rearrange("p k t -> p (k t)"), ALU.subtract) \
                    .then_inc(S["h_lo"], 1)
                if following is not None:
                    split(following, GATE)
                inputs(b + 1, b + 1)
                if following is not None:
                    split(following, UP)
                need(dve, d_mm=b + 1, yout=b)
                dve.tensor_tensor(yst[:], banks(6), gate2b[:], ALU.mult).then_inc(S["y"], 1)
                if following is not None:
                    split(following, DOWN)

            dve.wait_ge(g_in, 16)
            split(0, GATE)
            inputs(0, 0)
            split(0, UP)
            split(0, DOWN)
            over_blocks(dve, steps)

        @block.tensor
        def _(pe):
            start_above_zero(pe, "tensor")

            def split_product(out, x, w, chunks, n, e, x_lo_ready):
                terms = ((x[0], w[0]), (x[0], w[1]), (x[1], w[0]))
                for m, (xx, ww) in enumerate(terms):
                    if m < 2:
                        pe.wait_ge(S[(HI, LO)[m][n]], 2 * e + 3)
                    else:
                        x_lo_ready()
                    for kc in range(chunks):
                        ins = pe.matmul(out, xx[:, kc, :], ww(kc), start=(m == 0 and kc == 0), stop=(m == 2 and kc == chunks - 1))
                return ins

            def turn(b, used):
                need(pe, xg=b + 1, xT=used)
                for kc in range(KC):
                    ins = pe.transpose(ps[:, 2 + kc // 4, (kc % 4) * P:(kc % 4 + 1) * P], xg[:, kc * P:(kc + 1) * P], k["ident"])
                ins.then_inc(S["xt_mm"], 1)

            def steps(b, e, _):
                need(pe, x_hi=b + 1, hid=b)
                for n, done in ((GATE, "g_mm"), (UP, "gu_mm")):
                    w = [lambda kc, t=t: t[:, kc, :] for t in (hi[n], lo[n])]
                    split_product(bank(n), (x_hi, x_lo), w, KC, n, e, lambda: need(pe, x_lo=b + 1)).then_inc(S[done], 1)
                turn(b + 1, b + 1)
                need(pe, hid=b + 1, h_hi=b, h_lo=b)
                for kc in range(FC):
                    ins = pe.transpose(ps[:, 4, kc * P:(kc + 1) * P], hid[:, kc * P:(kc + 1) * P], k["ident"])
                ins.then_inc(S["ht_mm"], 1)
                need(pe, h_hi=b + 1, y=b)
                for h in range(2):
                    w = [lambda kc, t=t: t[:, kc, h * 512:(h + 1) * 512] for t in (hi[DOWN], lo[DOWN])]
                    ins = split_product(bank(6 + h), (h_hi, h_lo), w, FC, DOWN, e, lambda: need(pe, h_lo=b + 1))
                ins.then_inc(S["d_mm"], 1)

            turn(0, 0)
            over_blocks(pe, steps)


def combine(sb, env, rt, x1_d, dest, wts, ys_d, out):
    nc, a, row, sem = (env[n] for n in ("nc", "a", "row", "sem"))
    R = 3
    ya = [sb(f"ya{i}", [P, D]) for i in range(R)]
    yb = [sb(f"ybb{i}", [P, D]) for i in range(R)]
    f = sb("f", [P, R, D])
    x1b = sb("x1_back", [P, NT // 2, D])
    x1 = [rt[:, i, :] if i < NT // 2 else x1b[:, i - NT // 2, :] for i in range(NT)]
    rows = sb("rows3", [P, 2, D])
    st = sb("st3", [P, R, 2, 6])
    mv = sb("mv3", [P, R, 3])
    names = "rows_in x1_in first stat sd chain shift n s1 fin".split()
    S = {n: sem("f_" + n) for n in names}
    fetched, stored = ([sem(f"f_{n}{i}") for i in range(R)] for n in ("fetched", "stored"))
    with nc.Block() as block:
        @block.sync
        def _(sp):
            sp.dma_start(rows[:, 0, :], row("ln2_g")).then_inc(S["rows_in"], 16)
            sp.dma_start(rows[:, 1, :], row("ln2_b")).then_inc(S["rows_in"], 16)
            sp.dma_start(x1b[:], x1_d.rearrange("(i p) n -> p i n", p=P)).then_inc(S["x1_in"], 16)
            for i in range(NT):
                sp.wait_ge(S["fin"], i + 1)
                sp.dma_start(out[i * P:(i + 1) * P, :], f[:, i % R, :]).then_inc(stored[i % R], 16)
            for q in range(R):
                sp.wait_ge(stored[q], 16 * len(range(q, NT, R)))

        @block.gpsimd
        def _(pool):
            def fetch(i):
                if i >= R:
                    pool.wait_ge(S["n"], i - R + 1)
                for c, t in enumerate((ya[i % R], yb[i % R])):
                    pool.indirect_dma_start(out=t[:], out_offset=None, in_=ys_d,
                                            in_offset=bass.IndirectOffsetOnAxis(ap=dest[:, c, i:i + 1].bitcast(U32), axis=0)) \
                        .then_inc(fetched[i % R], 16)

            for i in range(R):
                fetch(i)
            pool.wait_ge(S["rows_in"], 32)
            for i in range(NT):
                if i + R < NT:
                    fetch(i + R)
                pool.wait_ge(S["s1"], i + 1)
                pool.tensor_tensor(f[:, i % R, :], f[:, i % R, :], rows[:, 1, :], ALU.add).then_inc(S["fin"], 1)

        @block.scalar
        def _(act):
            for i in range(NT + 2):
                if i < NT:
                    act.wait_ge(fetched[i % R], 32 * (i // R + 1))
                    act.activation(ya[i % R][:], ya[i % R][:], ACT.Identity, scale=wts[:, 0, i:i + 1]).then_inc(S["first"], 1)
                if 1 <= i <= NT:
                    act.wait_ge(S["stat"], i)
                    act.activation(mv[:, (i - 1) % R, 1:2], mv[:, (i - 1) % R, 1:2], ACT.Sqrt).then_inc(S["sd"], 1)
                if i >= 2:
                    j, q = i - 2, (i - 2) % R
                    act.wait_ge(S["shift"], j + 1)
                    if j >= R:
                        act.wait_ge(stored[q], 16 * (j // R))
                    act.activation(f[:, q, :], ya[q][:], ACT.Identity, bias=mv[:, q, 2:3], scale=mv[:, q, 1:2]).then_inc(S["n"], 1)

        @block.vector
        def _(dve):
            chain = [0]

            def link(ins):
                chain[0] += 1
                ins.then_inc(S["chain"], 1)
                dve.wait_ge(S["chain"], chain[0])

            def add_up(i, q):
                dve.wait_ge(S["first"], i + 1)
                if i == NT // 2:
                    dve.wait_ge(S["x1_in"], 16)
                dve.wait_ge(fetched[q], 32 * (i // R + 1))
                link(dve.scalar_tensor_tensor(out=ya[q][:], in0=x1[i], scalar=ALPHA, in1=ya[q][:], op0=ALU.mult, op1=ALU.add))
                link(dve.scalar_tensor_tensor(out=ya[q][:], in0=yb[q][:], scalar=wts[:, 1, i:i + 1], in1=ya[q][:], op0=ALU.mult, op1=ALU.add))
                for h in range(2):
                    ins = dve.bn_stats(st[:, q, h, :], ya[q][:, h * 512:(h + 1) * 512])
                link(ins)
                link(dve.bn_aggr(mv[:, q, 0:2], st[:, q].rearrange("p a b -> p (a b)")))
                dve.tensor_scalar(mv[:, q, 1:2], mv[:, q, 1:2], LN_EPS, None, ALU.add).then_inc(S["stat"], 1)

            def scale_and_shift(i, q):
                dve.wait_ge(S["sd"], i + 1)
                link(dve.reciprocal(mv[:, q, 1:2], mv[:, q, 1:2]))
                dve.scalar_tensor_tensor(out=mv[:, q, 2:3], in0=mv[:, q, 0:1], scalar=-1.0, in1=mv[:, q, 1:2], op0=ALU.mult, op1=ALU.mult) \
                    .then_inc(S["shift"], 1)

            dve.wait_ge(S["rows_in"], 32)
            for i in range(NT + 2):
                if i < NT:
                    add_up(i, i % R)
                if 1 <= i <= NT:
                    scale_and_shift(i - 1, (i - 1) % R)
                if i >= 2:
                    q = (i - 2) % R
                    dve.wait_ge(S["n"], i - 1)
                    dve.tensor_tensor(f[:, q, :], f[:, q, :], rows[:, 0, :], ALU.mult).then_inc(S["s1"], 1)


def kernel(**inputs):
    import concourse.bacc as _bacc
    from concourse.bass_utils import run_bass_kernel_spmd as _run

    v = {n: np.asarray(x) for n, x in inputs.items()}

    def chunks(w):
        return np.ascontiguousarray(w.reshape(KC, P, -1, P).transpose(2, 1, 0, 3)).reshape(-1, P, KC * P)

    def cols(x):
        return x.reshape(-1, P).T

    b_mod = v["b_mod"][0].reshape(6, D)
    col_of = {"mu": v["rwkv_mu"][0], "w0": v["w0"][0], "a0": v["a0"][0], "k_k": v["k_k"][0], "k_a": v["k_a"][0],
              "r_k": v["r_k"][0].reshape(-1), "gn_g": v["gn_g"][0], "gn_b": v["gn_b"][0], "shift1": b_mod[0],
              "scale1": b_mod[1], "shift2": b_mod[3], "scale2": b_mod[4], "c": v["c"][0]}
    row_of = {"sg_ln_g": v["sg_ln_g"][0], "sg_ln_b": v["sg_ln_b"][0], "gate1": b_mod[2], "gate2": b_mod[5],
              "ln1_g": v["ln1_g"][0], "ln1_b": v["ln1_b"][0], "ln2_g": v["ln2_g"][0], "ln2_b": v["ln2_b"][0],
              "router_b": v["router_b"]}
    table, chunk_start, small, token = constants()
    arrays = {
        "x": v["x"][0], "w_mod": v["w_mod"][0], "w_in": chunks(v["w_in"][0])[Z_ORDER],
        "cols": np.concatenate([cols(col_of[n]) for n in COLS], axis=1),
        "rows": np.concatenate([row_of[n] for n in ROWS]),
        "table": table, "chunk_start": chunk_start, "small": small, "token": token,
        "w2": v["w2"][0], "a2": v["a2"][0], "g2": v["g2"][0],
        "w_s": v["w_s"][0].transpose(2, 0, 1), "b_s": v["b_s"][0],
        "w_branch_a": v["w_branch_a"][0], "w_branch_b": v["w_branch_b"][0], "w_out": v["w_out"][0],
        "router_w": v["router_w"], "e_gate": v["e_gate"][0], "e_up": v["e_up"][0], "e_down": v["e_down"][0],
    }
    arrays = {f"{n}_dram": np.ascontiguousarray(x) for n, x in arrays.items()}
    nc = _bacc.Bacc("TRN2", target_bir_lowering=False, num_devices=1)
    a = {n[:-5]: nc.dram_tensor(n, x.shape, mybir.dt.from_np(x.dtype), kind="ExternalInput").ap() for n, x in arrays.items()}
    out = nc.dram_tensor("out_dram", (T, D), F32, kind="ExternalOutput").ap()
    build(nc, a, out)
    r = _run(nc, [arrays], core_ids=[0])
    return r.results[0]["out_dram"].reshape(1, T, D)
```

```python
from contextlib import ExitStack

import numpy as np
import concourse.bass as bass
from concourse import mybir

F32 = mybir.dt.float32
F32R = mybir.dt.float32r
I32 = mybir.dt.int32
U32 = mybir.dt.uint32
ALU = mybir.AluOpType
ACT = mybir.ActivationFunctionType
AX = mybir.AxisListType
ds = bass.ds

P = 128
D = 1024
T = 1024
KC = D // P
NT = T // P
W = 512
NP = W // P
C = 64
NC = T // C
E = 16
EG = 4
F = 512
FC = F // P
NB = 2 * T // P + E
DECAY = float(np.exp(-0.5))
ALPHA = 2.0 ** 0.25
LN_EPS = 1e-5
GN_EPS = 64e-5
BIG = 1e30

COUNT = EG + E
TOKEN = COUNT + P
SMALL = TOKEN + NT

CONSTS = ["ident", "up", "upinc", "upfull", "y8", "x8", "o8", "o16", "o32", "headones", "headmean", "ones", "causal"]
COLS = {}
for _name, _n in (("mu", 14), ("w0", 4), ("a0", 4), ("k_k", 4), ("k_a", 4), ("r_k", 4), ("gn_g", 4), ("gn_b", 4),
                  ("shift1", 8), ("scale1", 8), ("shift2", 8), ("scale2", 8), ("c", 8)):
    COLS[_name] = (sum(n for _, n in COLS.values()), _n)
NCOL = sum(n for _, n in COLS.values())
ROWS = {}
for _name, _n in (("sg_ln_g", W), ("sg_ln_b", W), ("gate1", D), ("gate2", D), ("ln1_g", D), ("ln1_b", D),
                  ("ln2_g", D), ("ln2_b", D), ("router_b", E)):
    ROWS[_name] = (sum(n for _, n in ROWS.values()), _n)
NROW = sum(n for _, n in ROWS.values())
Z_ORDER = [12, 13] + [p + 4 * s for p in range(NP) for s in range(3)] + [18, 19, 20, 21] + [14, 15, 16, 17] \
    + list(range(30, 38)) + list(range(22, 30))
Z_V, Z_U, Z_GATE = 14, 18, 22


def constants():
    i = np.arange(P)
    row, col = i[:, None], i[None, :]
    same = lambda n: row // n == col // n
    m = {
        "ident": row == col,
        "up": (row < col) & same(C),
        "upinc": (row <= col) & same(C),
        "upfull": row < col,
        "y8": (row < col) & same(8),
        "x8": (row > col) & same(8),
        "o8": (row > col) & same(16) & ~same(8),
        "o16": (row > col) & same(32) & ~same(16),
        "o32": (row > col) & same(64) & ~same(32),
        "headones": same(64),
        "headmean": same(64) / 64.0,
        "ones": np.ones((P, P)),
        "causal": row <= col,
    }
    table = np.concatenate([np.asarray(m[n], np.float32) for n in CONSTS], axis=1)
    chunk_start = np.ones((P, T), np.float32)
    chunk_start[:, ::C] = 0.0
    small = np.zeros((P, SMALL), np.float32)
    small[:, 0:EG] = EG - np.arange(EG)
    small[:, EG:EG + E] = E - np.arange(E)
    small[:, COUNT:COUNT + P] = np.arange(P)
    small[:, TOKEN:TOKEN + NT] = np.arange(T).reshape(NT, P).T
    return table, chunk_start, small


def build(nc, a, out):
    g_d = nc.dram_tensor("g_scratch", (NP, P, T), F32, kind="Internal").ap()
    bonus_d = nc.dram_tensor("bonus_scratch", (NP, P, T), F32, kind="Internal").ap()
    yb_d = nc.dram_tensor("yb_scratch", (NP, P, T), F32, kind="Internal").ap()
    gates_d = nc.dram_tensor("gates_scratch", (2 * KC, P, T), F32, kind="Internal").ap()
    x1_d = nc.dram_tensor("x1_scratch", (T // 2, D), F32, kind="Internal").ap()
    n2_d = nc.dram_tensor("n2_scratch", (T, D), F32, kind="Internal").ap()
    ys_d = nc.dram_tensor("ys_scratch", ((NB + 1) * P, D), F32, kind="Internal").ap()

    with ExitStack() as top:
        sems = {}

        def sem(name):
            if name not in sems:
                sems[name] = nc.alloc_semaphore(name=name)
            return sems[name]

        def phase_ends(keep=()):
            nc.clear_and_free_semaphores([x for n, x in sems.items() if n not in keep])
            for n in [n for n in sems if n not in keep]:
                del sems[n]
            nc.all_engine_barrier()

        def tiles(stack):
            def sb(name, shape, dt=F32):
                return stack.enter_context(nc.sbuf_tensor(name, shape, dt))
            return sb

        sb = tiles(top)
        ps = top.enter_context(nc.psum_tensor("ps", [P, 8, 512], F32))
        consts = sb("consts", [P, len(CONSTS), P])
        cols = sb("cols", [P, NCOL])
        small = sb("small", [P, SMALL])
        modc = sb("modc", [P, 4, KC])
        k = {n: consts[:, i, :] for i, n in enumerate(CONSTS)}

        def col(name, i):
            return cols[:, COLS[name][0] + i:COLS[name][0] + i + 1]

        def row(name):
            s, n = ROWS[name]
            return a["rows"][s:s + n].partition_broadcast(P)

        def bank(b, n=512):
            return ps[:, b, 0:n]

        def banks(b):
            return ps[:, b:b + 2, :].rearrange("p a n -> p (a n)")

        with ExitStack() as mixer:
            msb = tiles(mixer)
            gate1b = msb("gate1b", [P, D])
            env = dict(nc=nc, a=a, ps=ps, k=k, cols=cols, col=col, row=row, bank=bank, banks=banks, sem=sem,
                       modc=modc, small=small, consts=consts, gate1b=gate1b, tiles=tiles, phase_ends=phase_ends)
            gate2_d = nc.dram_tensor("gate2_scratch", (P, D), F32, kind="Internal").ap()
            rt = msb("rt", [P, NP, T])
            logits = msb("logits", [P, NT, E])
            through = mixer.enter_context(ExitStack())
            ring = tiles(through)("ring", [P, 3, 2, KC, P])
            with ExitStack() as early:
                esb = tiles(early)
                at, bt, kt, vt = (esb(n, [P, NP, T]) for n in ("at", "bt", "kt", "vt"))
                pc = esb("pc", [P, NP, NC])
                hT = esb("hT", [P, KC, T])
                env.update(hT=hT, ring=ring, rt=rt, at=at, bt=bt, kt=kt, vt=vt, pc=pc)
                with ExitStack() as s:
                    project_and_gate(tiles(s), env, yb_d, gate2_d)
                    phase_ends(keep=["p_w_slot0", "p_w_slot1"])
                with ExitStack() as s:
                    prepare_recurrence(tiles(s), env, g_d, bonus_d)
                    phase_ends()
                with ExitStack() as s:
                    run_recurrence(tiles(s), env, gates_d, ys_d)
                    phase_ends(keep=["x_w_b"])
            with ExitStack() as s:
                x1b = tiles(s)("x1b", [P, NT // 2, D])
                x1 = [rt[:, i, :] if i < NT // 2 else x1b[:, i - NT // 2, :] for i in range(NT)]
                mix_branches(tiles(s), env, x1, x1_d, logits, g_d, bonus_d, yb_d, gates_d, n2_d)
                phase_ends()
            through.close()
            dest = msb("dest", [P, 2, NT], I32)
            wts = msb("wts", [P, 2, NT])
            bounds = msb("bounds", [1, 2 * E], I32)
            slots = msb("slots", [P, NB + 2], I32)
            with ExitStack() as e:
                env["weights"] = expert_weights(tiles(e), env)
                with ExitStack() as s:
                    route(tiles(s), env, logits, dest, wts, bounds, slots)
                    phase_ends(keep=[n for n in sems if n.startswith("e_w")])
                with ExitStack() as s:
                    run_experts(tiles(s), env, bounds, slots, n2_d, ys_d, gate2_d)
                    phase_ends()
            with ExitStack() as s:
                combine(tiles(s), env, rt, x1_d, dest, wts, ys_d, out)
                phase_ends()


def project_and_gate(sb, env, yb_d, gate2_d):
    nc, a, ps, k, col, row, bank, banks, sem = (env[n] for n in ("nc", "a", "ps", "k", "col", "row", "bank", "banks", "sem"))
    modc, hT, ring, gate1b = env["modc"], env["hT"], env["ring"], env["gate1b"]
    rt, at, bt, kt, vt = (env[n] for n in ("rt", "at", "bt", "kt", "vt"))
    xs, xn = kt[:, 0:2, :], kt[:, 2:4, :]
    gateb, gate2b = vt[:, 0, :], vt[:, 1, :]
    vg = rt[:].rearrange("p q (a n) -> p (q a) n", n=W)
    u, yb = at, bt[:, 0:2, :]
    macc = [x.rearrange("p a t -> p (a t)") for x in (at[:, 2:4, :], kt[:, 0:2, :], bt[:, 2:4, :])]
    stats = sb("stats", [P, NT, 2, 6])
    mv = sb("mv", [P, NT, 2])
    cond = sb("cond", [P, KC])
    mod_w = sb("mod_w", [P, 3, 2 * D])
    last_w = sb("last_w", [P, 2, KC, P])
    vstats = sb("vstats", [P, NT, 6])
    vmv = sb("vmv", [P, NT, 2])
    lng = sb("lng", [P, W])
    lnb = sb("lnb", [P, W])
    wst = sb("wst", [P, 8, P])
    bsb = sb("bsb", [P, NP, P])

    consts_in, x_in, x_norm, x_turned = sem("consts_in"), [sem("x_in0"), sem("x_in1")], sem("x_norm"), sem("x_turned")
    x_stats, x_rstd, h_evac, h_ready = sem("x_stats"), sem("x_rstd"), sem("h_evac"), sem("h_ready")
    w_in_slot = [sem(f"w_slot{i}") for i in range(4)]
    mod_slot = [sem(f"mod_slot{i}") for i in range(3)]
    cond_ready, mod_acc, mod_mm, mod_ready = sem("cond_ready"), sem("mod_acc"), sem("mod_mm"), sem("mod_ready")
    v_mm, v_gelu, v_var, v_rstd, v_norm, v_scaled = (sem(n) for n in ("v_mm", "v_gelu", "v_var", "v_rstd", "v_norm", "v_scaled"))
    u_mm, u_gelu, s_mm, s_read, yb_ready = (sem(n) for n in ("u_mm", "u_gelu", "s_mm", "s_read", "yb_ready"))
    yb_out, dve_chain, pool_chain, gate2_out = [sem("yb_out0"), sem("yb_out1")], sem("dve_chain0"), sem("pool_chain0"), sem("gate2_out")
    rows_in = sem("rows_in")
    z_w = [ring[:, 0], ring[:, 1], ring[:, 2], last_w[:]]

    def weights_here(eng, n):
        eng.wait_ge(w_in_slot[n], 16)

    with nc.Block() as block:
        @block.sync
        def _(sp):
            sp.dma_start(env["consts"][:], a["table"].rearrange("p (n q) -> p n q", q=P)).then_inc(consts_in, 16)
            sp.dma_start(env["cols"][:], a["cols"]).then_inc(consts_in, 16)
            sp.dma_start(env["small"][:], a["small"]).then_inc(consts_in, 16)

            def load_mod(n):
                if n >= 3:
                    sp.wait_ge(mod_acc, n - 2)
                j, kc = divmod(n, KC)
                sp.dma_start(mod_w[:, n % 3, :], a["w_mod"][kc * P:(kc + 1) * P, j * 2 * D:(j + 1) * 2 * D]).then_inc(mod_slot[n % 3], 16)

            for n in range(KC):
                load_mod(n)
            sp.wait_ge(x_in[(NT - 1) % 2], 16 * (NT // 2))
            for n, g in enumerate((Z_V, Z_V + 2, Z_U, Z_U + 2)):
                sp.dma_start(z_w[n].rearrange("p c k n -> p c (k n)"), a["w_in"][g:g + 2].rearrange("c p n -> p c n")).then_inc(w_in_slot[n], 16)
            for n in range(KC, 3 * KC):
                load_mod(n)
            sp.wait_ge(v_mm, NT)
            for n in range(2):
                sp.dma_start(ring[:, n].rearrange("p c k n -> p c (k n)"), a["w_in"][2 * n:2 * n + 2].rearrange("c p n -> p c n")).then_inc(sem(f"p_w_slot{n}"), 16)
            for i in range(2):
                sp.wait_ge(yb_out[i], 32)
            sp.wait_ge(gate2_out, 16)

        @block.scalar
        def _(act):
            def load_x(i):
                if i >= 2:
                    act.wait_ge(x_norm, i - 1)
                act.dma_start(xs[:, i % 2, :], a["x"][i * P:(i + 1) * P, :]).then_inc(x_in[i % 2], 16)

            load_x(0)
            load_x(1)
            act.wait_ge(consts_in, 48)
            act.activation(cond[:], env["cols"][:, COLS["c"][0]:COLS["c"][0] + KC], ACT.Silu).then_inc(cond_ready, 1)
            for i in range(NT):
                if i == 3:
                    act.dma_start(gateb, row("gate1")).then_inc(rows_in, 16)
                    act.dma_start(gate2b, row("gate2")).then_inc(rows_in, 16)
                    act.dma_start(lng[:], row("sg_ln_g")).then_inc(rows_in, 16)
                    act.dma_start(lnb[:], row("sg_ln_b")).then_inc(rows_in, 16)
                    act.dma_start(wst[:], a["w_s"]).then_inc(rows_in, 16)
                    for h in range(2):
                        act.dma_start(bsb[64 * h:64 * h + 64], a["b_s"].rearrange("(g h) t -> h g t", h=2)[h].partition_broadcast(64)).then_inc(rows_in, 16)
                act.wait_ge(x_stats, i + 1)
                act.activation(mv[:, i, 1:2], mv[:, i, 1:2], ACT.Sqrt).then_inc(x_rstd, 1)
                if i + 2 < NT:
                    load_x(i + 2)
                if i >= 1:
                    act.wait_ge(x_turned, i)
                    act.copy(hT[:, :, (i - 1) * P:i * P], banks(2 * ((i - 1) % 2)).rearrange("p (k t) -> p k t", k=KC)).then_inc(h_evac, 1)
            act.wait_ge(x_turned, NT)
            act.copy(hT[:, :, (NT - 1) * P:], banks(2 * ((NT - 1) % 2)).rearrange("p (k t) -> p k t", k=KC)).then_inc(h_evac, 1)
            act.wait_ge(mod_ready, 1)
            act.wait_ge(h_evac, NT)
            for kc in range(1, KC, 2):
                act.activation(hT[:, kc, :], hT[:, kc, :], ACT.Identity, bias=modc[:, 0, kc:kc + 1], scale=modc[:, 1, kc:kc + 1]).then_inc(h_ready, 1)
            for i in range(NT):
                act.wait_ge(v_mm, i + 1)
                act.activation(vg[:, i, :], bank(i % 4), ACT.Gelu_apprx_tanh).then_inc(v_gelu, 1)
            for p in range(NP):
                if p == 2:
                    act.wait_ge(mod_mm, 1)
                for h in range(2):
                    act.wait_ge(u_mm, 2 * p + h + 1)
                    act.activation(u[:, p, h * 512:(h + 1) * 512], bank((2 * p + h) % 4), ACT.Gelu_apprx_tanh).then_inc(u_gelu, 1)
                if p == 0:
                    act.wait_ge(v_var, 1)
                    act.activation(vmv[:, :, 1:2], vmv[:, :, 1:2], ACT.Sqrt).then_inc(v_rstd, 1)
            for p in range(NP):
                act.wait_ge(yb_ready, p + 1)
                act.dma_start(yb_d[p], yb[:, p % 2, :]).then_inc(yb_out[p % 2], 16)
            act.wait_ge(mod_ready, 2)
            act.dma_start(gate2_d, gate2b).then_inc(gate2_out, 16)

        @block.vector
        def _(dve):
            chain = [0]

            def link(ins):
                chain[0] += 1
                ins.then_inc(dve_chain, 1)
                dve.wait_ge(dve_chain, chain[0])

            def mod_row(n):
                j, kc = divmod(n, KC)
                dve.wait_ge(mod_slot[n % 3], 16 * (n // 3 + 1))
                if kc == 0:
                    dve.tensor_scalar(macc[j], mod_w[:, n % 3, :], cond[:, kc:kc + 1], None, ALU.mult).then_inc(mod_acc, 1)
                else:
                    dve.wait_ge(mod_acc, n)
                    dve.scalar_tensor_tensor(out=macc[j], in0=mod_w[:, n % 3, :], scalar=cond[:, kc:kc + 1], in1=macc[j],
                                             op0=ALU.mult, op1=ALU.add).then_inc(mod_acc, 1)

            def mod_column(i, name, plus, src):
                return dve.scalar_tensor_tensor(out=modc[:, i, :], in0=src, scalar=plus,
                                                in1=env["cols"][:, COLS[name][0]:COLS[name][0] + KC], op0=ALU.add, op1=ALU.add)

            dve.wait_ge(cond_ready, 1)
            for i in range(NT):
                dve.wait_ge(x_in[i % 2], 16 * (i // 2 + 1))
                for h in range(2):
                    ins = dve.bn_stats(stats[:, i, h, :], xs[:, i % 2, h * 512:(h + 1) * 512])
                link(ins)
                link(dve.bn_aggr(mv[:, i, :], stats[:, i, :, :].rearrange("p a b -> p (a b)")))
                dve.tensor_scalar(mv[:, i, 1:2], mv[:, i, 1:2], LN_EPS, None, ALU.add).then_inc(x_stats, 1)
                dve.wait_ge(x_rstd, i + 1)
                link(dve.reciprocal(mv[:, i, 1:2], mv[:, i, 1:2]))
                if i >= 2:
                    dve.wait_ge(x_turned, i - 1)
                dve.tensor_scalar(xn[:, i % 2, :], xs[:, i % 2, :], mv[:, i, 0:1], mv[:, i, 1:2], ALU.subtract, ALU.mult).then_inc(x_norm, 1)
                mod_row(i)
            dve.wait_ge(mod_mm, 1)
            mod_column(0, "shift1", 0.0, ps[:, 4, 0:KC])
            mod_column(1, "scale1", 1.0, ps[:, 4, KC:2 * KC]).then_inc(mod_ready, 1)
            dve.wait_ge(mod_ready, 1)
            dve.wait_ge(h_evac, NT)
            for kc in range(0, KC, 2):
                dve.tensor_scalar(hT[:, kc, :], hT[:, kc, :], modc[:, 1, kc:kc + 1], modc[:, 0, kc:kc + 1], ALU.mult, ALU.add).then_inc(h_ready, 1)
            for i in range(NT):
                dve.wait_ge(v_gelu, i + 1)
                ins = dve.bn_stats(vstats[:, i, :], vg[:, i, :])
                if i == NT - 1:
                    link(ins)
                mod_row(KC + i)
            for i in range(NT):
                ins = dve.bn_aggr(vmv[:, i, :], vstats[:, i, :])
            link(ins)
            dve.tensor_scalar(vmv[:, :, 1:2], vmv[:, :, 1:2], LN_EPS, None, ALU.add).then_inc(v_var, 1)
            dve.wait_ge(v_rstd, 1)
            link(dve.reciprocal(vmv[:, :, 1:2], vmv[:, :, 1:2]))
            for i in range(NT):
                dve.tensor_scalar(vg[:, i, :], vg[:, i, :], vmv[:, i, 0:1], vmv[:, i, 1:2], ALU.subtract, ALU.mult).then_inc(v_norm, 1)
            for n in range(2 * KC, 3 * KC):
                mod_row(n)
            dve.wait_ge(mod_mm, 2)
            dve.scalar_tensor_tensor(out=gate1b[:], in0=banks(0), scalar=1.0, in1=gateb, op0=ALU.add, op1=ALU.add)
            dve.scalar_tensor_tensor(out=gate2b, in0=banks(2), scalar=1.0, in1=gate2b, op0=ALU.add, op1=ALU.add)
            mod_column(2, "shift2", 0.0, ps[:, 7, 0:KC])
            mod_column(3, "scale2", 1.0, ps[:, 7, KC:2 * KC]).then_inc(mod_ready, 1)
            dve.wait_ge(mod_ready, 2)
            for p in range(NP):
                dve.wait_ge(s_mm, p + 1)
                if p >= 2:
                    dve.wait_ge(yb_out[p % 2], 16)
                dve.wait_ge(rows_in, 112)
                dve.tensor_tensor(yb[:, p % 2, :].rearrange("p (n t) -> p n t", t=P), banks(4 + 2 * (p % 2)).rearrange("p (n t) -> p n t", t=P),
                                  bsb[:, p, :].unsqueeze(1).to_broadcast([P, NT, P]), ALU.add).then_inc(s_read, 1)
                dve.wait_ge(s_read, p + 1)
                dve.wait_ge(u_gelu, 2 * p + 2)
                dve.tensor_tensor(yb[:, p % 2, :], yb[:, p % 2, :], u[:, p, :], ALU.mult).then_inc(yb_ready, 1)
        @block.gpsimd
        def _(pool):
            pool.wait_ge(rows_in, 112)
            pool.wait_ge(consts_in, 48)
            pool.tensor_tensor(wst[:], wst[:], k["causal"].unsqueeze(1).to_broadcast([P, 8, P]), ALU.mult)
            for i in range(NT):
                pool.wait_ge(v_norm, i + 1)
                pool.tensor_tensor(vg[:, i, :], vg[:, i, :], lng[:], ALU.mult).then_inc(pool_chain, 1)
                pool.wait_ge(pool_chain, i + 1)
                pool.tensor_tensor(vg[:, i, :], vg[:, i, :], lnb[:], ALU.add).then_inc(v_scaled, 1)

        @block.tensor
        def _(pe):
            pe.wait_ge(consts_in, 48)
            for i in range(NT):
                pe.wait_ge(x_norm, i + 1)
                if i >= 2:
                    pe.wait_ge(h_evac, i - 1)
                for kc in range(KC):
                    b = 2 * (i % 2) + kc // 4
                    ins = pe.transpose(ps[:, b, (kc % 4) * P:(kc % 4 + 1) * P], xn[:, i % 2, kc * P:(kc + 1) * P], k["ident"])
                ins.then_inc(x_turned, 1)

            def mod_columns(j, at_, b, c0):
                for c in range(KC):
                    ins = pe.matmul(ps[:, b, c0 + c:c0 + c + 1], macc[j][:, at_ + c * P:at_ + (c + 1) * P], k["ones"][:, 0:1], start=True, stop=True)
                return ins

            def mod_row(j, at_, b):
                for h in range(2):
                    ins = pe.matmul(bank(b + h), k["ones"], macc[j][:, at_ + h * 512:at_ + (h + 1) * 512], start=True, stop=True)
                return ins

            pe.wait_ge(mod_acc, KC)
            mod_columns(0, 0, 4, 0)
            mod_columns(0, D, 4, KC).then_inc(mod_mm, 1)
            pe.wait_ge(h_ready, KC)
            weights_here(pe, 0)
            weights_here(pe, 1)
            pe.wait_ge(h_evac, NT)
            for i in range(NT):
                if i >= 4:
                    pe.wait_ge(v_gelu, i - 3)
                for half in range(2):
                    for kc in range(KC):
                        ins = pe.matmul(ps[:, i % 4, half * 256:half * 256 + 256], hT[:, kc, i * P:(i + 1) * P], z_w[half][:, :, kc, :],
                                        start=(kc == 0), stop=(kc == KC - 1))
                ins.then_inc(v_mm, 1)

            def mix(p):
                pe.wait_ge(v_scaled, NT)
                pe.wait_ge(rows_in, 112)
                if p >= 2:
                    pe.wait_ge(s_read, p - 1)
                if p == 1:
                    pe.wait_ge(mod_ready, 2)
                for i in range(NT):
                    for h in range(2):
                        g = 2 * p + h
                        ins = pe.matmul(ps[64 * h:64 * h + 64, 4 + 2 * (p % 2) + i // 4, (i % 4) * P:(i % 4 + 1) * P],
                                        vg[:, i, 64 * g:64 * g + 64], wst[:, g, :], start=True, stop=True)
                ins.then_inc(s_mm, 1)

            for p in range(NP):
                n = 2 + p // 2
                weights_here(pe, n)
                for h in range(2):
                    m = 2 * p + h
                    pe.wait_ge(v_gelu, NT)
                    if m >= 4:
                        pe.wait_ge(u_gelu, m - 3)
                    for kc in range(KC):
                        ins = pe.matmul(bank(m % 4), z_w[n][:, p % 2, kc, :], hT[:, kc, h * 512:(h + 1) * 512], start=(kc == 0), stop=(kc == KC - 1))
                    ins.then_inc(u_mm, 1)
            pe.wait_ge(mod_acc, 3 * KC)
            pe.wait_ge(u_gelu, 2 * NP)
            mod_row(1, 0, 0)
            mod_row(2, D, 2)
            mod_columns(1, D, 7, 0)
            mod_columns(2, 0, 7, KC).then_inc(mod_mm, 1)
            for p in range(NP):
                mix(p)


def prepare_recurrence(sb, env, g_d, bonus_d):
    nc, a, ps, k, col, row, bank, banks, sem = (env[n] for n in ("nc", "a", "ps", "k", "col", "row", "bank", "banks", "sem"))
    hT, ring, rt, at, bt, kt, vt, pc = (env[n] for n in ("hT", "ring", "rt", "at", "bt", "kt", "vt", "pc"))
    reset = sb("reset", [P, T])
    zraw = sb("zraw", [P, 2, T + 1])
    dz = sb("dz", [P, T])
    wa = sb("wa", [P, T])
    sg = sb("sg", [P, T])
    lora = sb("lora", [P, W])
    g2 = sb("g2", [P, W])
    L = sb("L", [P, T])
    kk = sb("kk", [P, T])
    t1 = sb("t1", [P, T])
    ein = sb("ein", [P, T])
    gst = sb("gst", [P, T])
    bst = sb("bst", [P, T])
    oka = sb("oka", [P, NP])
    names = ("p_reset_in p_lora_in p_z_mm p_z_evac p_z_mixed p_thw p_sg p_q_mm p_a_mm p_g_mm p_ss_mm p_bs_mm p_dl p_a p_L p_Lx p_ein p_en p_ex "
             "p_g_evac p_kkraw p_sq p_nrm p_kkn p_t1 p_b1 p_bonus p_at p_bt p_kt p_rt p_bta p_zero p_chain p_kmod").split()
    S = {n: sem(n) for n in names}
    w_slot = [sem(f"p_w_slot{i}") for i in range(3)]
    g_out, b_out = sem("p_g_out"), sem("p_b_out")
    NZ = 14
    dst_of = [None, None] + [t for p in range(NP) for t in ((rt, p), (kt, p), (vt, p))]

    with nc.Block() as block:
        @block.sync
        def _(sp):
            sp.dma_start(reset[:], a["chunk_start"]).then_inc(S["p_reset_in"], 16)
            sp.dma_start(lora[0:64, :], a["w2"]).then_inc(S["p_lora_in"], 16)
            sp.dma_start(lora[64:128, :], a["a2"]).then_inc(S["p_lora_in"], 16)
            sp.dma_start(g2[:], a["g2"]).then_inc(S["p_lora_in"], 16)
            for n in range(2, NZ // 2):
                if n >= 3:
                    sp.wait_ge(S["p_z_mm"], 4 * (n - 2))
                sp.dma_start(ring[:, n % 3].rearrange("p c k n -> p c (k n)"), a["w_in"][2 * n:2 * n + 2].rearrange("c p n -> p c n")).then_inc(w_slot[n % 3], 16)
            for p in range(NP):
                sp.wait_ge(S["p_g_evac"], p + 1)
                sp.dma_start(g_d[p], gst[:]).then_inc(g_out, 16)
                sp.wait_ge(S["p_bonus"], p + 1)
                sp.dma_start(bonus_d[p], bst[:]).then_inc(b_out, 16)
            sp.wait_ge(g_out, 16 * NP)
            sp.wait_ge(b_out, 16 * NP)

        @block.tensor
        def _(pe):
            def z(n):
                if n % 2 == 0:
                    pe.wait_ge(w_slot[n // 2 % 3], 16 * (n // 2 // 3 + 1))
                for h in range(2):
                    m = 2 * n + h
                    if m >= 4:
                        pe.wait_ge(S["p_z_evac"], m - 3)
                    for kc in range(KC):
                        ins = pe.matmul(bank(m % 4), ring[:, n // 2 % 3, n % 2, kc, :], hT[:, kc, h * 512:(h + 1) * 512], start=(kc == 0), stop=(kc == KC - 1))
                    ins.then_inc(S["p_z_mm"], 1)

            def both(b, lhsT, rhs, done):
                for h in range(2):
                    ins = pe.matmul(bank(b + h), lhsT, rhs[:, h * 512:(h + 1) * 512], start=True, stop=True)
                ins.then_inc(S[done], 1)

            z(0)
            z(1)
            z(2)
            for p in range(NP):
                if p == 0:
                    pe.wait_ge(S["p_thw"], 1)
                    pe.wait_ge(S["p_z_mixed"], 2)
                    pe.wait_ge(S["p_lora_in"], 48)
                if p >= 1:
                    pe.wait_ge(S["p_bonus"], p)
                    pe.wait_ge(S["p_g_evac"], p)
                both(4, lora[0:64, p * P:(p + 1) * P], wa[0:64, :], "p_q_mm")
                both(6, lora[64:128, p * P:(p + 1) * P], wa[64:128, :], "p_a_mm")
                z(3 + 3 * p)
                pe.wait_ge(S["p_sg"], 1)
                pe.wait_ge(S["p_a"], p + 1)
                both(6, g2[:, p * P:(p + 1) * P], sg[:], "p_g_mm")
                z(4 + 3 * p)
                pe.wait_ge(S["p_dl"], p + 1)
                pe.wait_ge(S["p_sq"], p + 1)
                both(4, k["headones"], t1[:], "p_ss_mm")
                if p + 1 < NP:
                    z(5 + 3 * p)
                pe.wait_ge(S["p_b1"], p + 1)
                pe.wait_ge(S["p_nrm"], p + 1)
                both(4, k["headones"], dz[:], "p_bs_mm")

        @block.scalar
        def _(act):
            def evac(n):
                if n >= 2:
                    act.wait_ge(S["p_z_mixed"], n - 1)
                if n == 0:
                    act.wait_ge(S["p_zero"], 1)
                for h in range(2):
                    act.wait_ge(S["p_z_mm"], 2 * n + h + 1)
                    act.copy(zraw[:, n % 2, 1 + h * 512:1 + (h + 1) * 512], bank((2 * n + h) % 4)).then_inc(S["p_z_evac"], 1)

            evac(0)
            evac(1)
            act.wait_ge(S["p_z_mixed"], 1)
            act.activation(wa[0:64, :], wa[0:64, :], ACT.Tanh).then_inc(S["p_thw"], 1)
            act.wait_ge(S["p_z_mixed"], 2)
            act.activation(sg[:], sg[:], ACT.Sigmoid).then_inc(S["p_sg"], 1)
            evac(2)
            for p in range(NP):
                dl, ap_ = at[:, p, :], bt[:, p, :]
                act.wait_ge(S["p_q_mm"], p + 1)
                act.activation(dl, banks(4), ACT.Sigmoid, bias=col("w0", p)).then_inc(S["p_dl"], 1)
                act.wait_ge(S["p_a_mm"], p + 1)
                act.activation(ap_, banks(6), ACT.Sigmoid, bias=col("a0", p)).then_inc(S["p_a"], 1)
                act.wait_ge(S["p_L"], p + 1)
                if p:
                    act.wait_ge(S["p_rt"], p)
                act.activation(ein[:], L[:], ACT.Exp, scale=-DECAY).then_inc(S["p_ein"], 1)
                evac(3 + 3 * p)
                act.wait_ge(S["p_g_mm"], p + 1)
                if p:
                    act.wait_ge(g_out, 16 * p)
                act.copy(gst[:], banks(6)).then_inc(S["p_g_evac"], 1)
                act.wait_ge(S["p_Lx"], p + 1)
                act.activation(dl, dl, ACT.Exp, scale=-DECAY).then_inc(S["p_ex"], 1)
                act.wait_ge(S["p_ein"], p + 1)
                act.activation(L[:], L[:], ACT.Exp, scale=DECAY).then_inc(S["p_en"], 1)
                evac(4 + 3 * p)
                act.wait_ge(S["p_ss_mm"], p + 1)
                act.activation(t1[:], banks(4), ACT.Sqrt).then_inc(S["p_nrm"], 1)
                if p + 1 < NP:
                    evac(5 + 3 * p)

        @block.gpsimd
        def _(pool):
            for p in range(NP):
                pool.wait_ge(S["p_kkraw"], p + 1)
                if p:
                    pool.wait_ge(S["p_kt"], p)
                    pool.wait_ge(S["p_bt"], p)
                pool.tensor_tensor(t1[:], kk[:], kk[:], ALU.mult).then_inc(S["p_sq"], 1)
                pool.wait_ge(S["p_b1"], p + 1)
                pool.wait_ge(S["p_ein"], p + 1)
                pool.tensor_tensor(rt[:, p, :], rt[:, p, :], ein[:], ALU.mult)
                pool.tensor_copy(pc[:, p, :], ein[:, C - 1::C]).then_inc(S["p_rt"], 1)

        @block.vector
        def _(dve):
            chain = [0]

            def link(ins):
                chain[0] += 1
                ins.then_inc(S["p_chain"], 1)
                dve.wait_ge(S["p_chain"], chain[0])

            dve.memset(zraw[:, :, 0:1], 0.0).then_inc(S["p_zero"], 1)
            link(dve.tensor_scalar(oka[:], env["cols"][:, COLS["k_a"][0]:COLS["k_a"][0] + NP], -1.0, 1.0, ALU.mult, ALU.add))

            def mixed(n):
                dve.wait_ge(S["p_z_evac"], 2 * n + 2)
                c = Z_ORDER[n]
                dst = (wa[:], sg[:])[n] if n < 2 else dst_of[n][0][:, dst_of[n][1], :]
                link(dve.tensor_tensor(dz[:], zraw[:, n % 2, 0:T], zraw[:, n % 2, 1:T + 1], ALU.subtract))
                dve.scalar_tensor_tensor(out=dst, in0=dz[:], scalar=col("mu", c), in1=zraw[:, n % 2, 1:T + 1], op0=ALU.mult, op1=ALU.add) \
                    .then_inc(S["p_z_mixed"], 1)
                dve.wait_ge(S["p_z_mixed"], n + 1)

            dve.wait_ge(S["p_zero"], 1)
            mixed(0)
            mixed(1)
            dve.wait_ge(S["p_reset_in"], 16)
            for p in range(NP):
                r_, k_, v_ = rt[:, p, :], kt[:, p, :], vt[:, p, :]
                dl, ap_ = at[:, p, :], bt[:, p, :]
                if p:
                    dve.wait_ge(S["p_bs_mm"], p)
                mixed(2 + 3 * p)
                dve.wait_ge(S["p_dl"], p + 1)
                dve.tensor_tensor_scan(L[:], reset[:], dl, 0.0, ALU.mult, ALU.add).then_inc(S["p_L"], 1)
                dve.wait_ge(S["p_L"], p + 1)
                dve.tensor_tensor(dl, L[:], dl, ALU.subtract).then_inc(S["p_Lx"], 1)
                mixed(3 + 3 * p)
                dve.tensor_scalar(kk[:], k_, col("k_k", p), None, ALU.mult).then_inc(S["p_kkraw"], 1)
                dve.wait_ge(S["p_a"], p + 1)
                link(dve.tensor_scalar(bst[:], ap_, col("k_a", p), oka[:, p:p + 1], ALU.mult, ALU.add) if not p else
                     _after(dve, b_out, 16 * p).tensor_scalar(bst[:], ap_, col("k_a", p), oka[:, p:p + 1], ALU.mult, ALU.add))
                link(dve.tensor_tensor(k_, k_, bst[:], ALU.mult))
                mixed(4 + 3 * p)
                dve.scalar_tensor_tensor(out=dz[:], in0=r_, scalar=col("r_k", p), in1=k_, op0=ALU.mult, op1=ALU.mult).then_inc(S["p_b1"], 1)
                dve.wait_ge(S["p_nrm"], p + 1)
                link(dve.tensor_scalar(t1[:], t1[:], 1e-12, None, ALU.max))
                link(dve.reciprocal(t1[:], t1[:]))
                link(dve.tensor_tensor(kk[:], kk[:], t1[:], ALU.mult))
                dve.wait_ge(S["p_ex"], p + 1)
                dve.scalar_tensor_tensor(out=at[:, p, :], in0=kk[:], scalar=-1.0, in1=dl, op0=ALU.mult, op1=ALU.mult).then_inc(S["p_at"], 1)
                link(dve.tensor_tensor(t1[:], kk[:], ap_, ALU.mult))
                dve.wait_ge(S["p_bs_mm"], p + 1)
                dve.tensor_tensor(bst[:], banks(4), v_, ALU.mult).then_inc(S["p_bonus"], 1)
                dve.wait_ge(S["p_en"], p + 1)
                dve.tensor_tensor(bt[:, p, :], t1[:], L[:], ALU.mult).then_inc(S["p_bt"], 1)
                dve.tensor_tensor(k_, k_, L[:], ALU.mult).then_inc(S["p_kt"], 1)
                dve.wait_ge(S["p_kt"], p + 1)


def _after(eng, s, value):
    eng.wait_ge(s, value)
    return eng


def run_recurrence(sb, env, gates_d, ys_d):
    nc, a, ps, k, col, row, bank, banks, sem = (env[n] for n in ("nc", "a", "ps", "k", "col", "row", "bank", "banks", "sem"))
    hT, ring, rt, at, bt, kt, vt, pc = (env[n] for n in ("hT", "ring", "rt", "at", "bt", "kt", "vt", "pc"))
    m = {n: sb("m_" + n, [P, NP, P]) for n in "abd bbd kbd rbd vbd bhbd khbd x2 X o8 o16 o32 Y RB AK RK y2 x4 R V BH KH S".split()}
    xraw, Tt, Z, U0, U, SPC = m["x2"], m["x2"], m["y2"], m["x4"], m["Y"], m["X"]
    gst = sb("gst2", [P, 2, 512])
    nought = sb("nought", [P, P])
    names = ("abd bbd kbd rbd vbd bhbd khbd y0_mm x0_mm rb_mm ak_mm rk_mm v_tr bh_tr kh_tr xraw X offs Y R1 RB AK RK V BH KH x2_mm y2_mm x2 y2 "
             "x4_mm r2_mm x4 R2 r4_mm R4 T_mm Z_mm T Z rz_mm R u0_mm U0 u_mm U sp_mm y_mm SPC S yout gate_mm gate_sig init").split()
    S = {n: sem("c_" + n) for n in names}
    gw = [sem("c_gw0"), sem("c_gw1")]
    g_out = [sem("c_g_out0"), sem("c_g_out1")]
    nought_ready, zeros_out = sem("c_nought"), sem("c_zeros_out")
    NI = NC // 2

    signals = {
        "sync": (),
        "gpsimd": "abd vbd bhbd offs SPC".split(),
        "scalar": "kbd rbd xraw V BH KH x2 x4 T U0 U yout gate_sig".split(),
        "vector": "bbd khbd Y R1 X RB AK RK y2 R2 R4 Z R S".split(),
        "tensor": [n for n in names if n.endswith("_mm") or n.endswith("_tr")],
    }

    def start_at_one(eng, which):
        for n in signals[which]:
            eng.sem_inc(S[n], 1)

    def quads(b):
        return ps[:, b, :].rearrange("p (q n) -> p q n", q=NP)

    def mask(name):
        return k[name].unsqueeze(1).to_broadcast([P, NP, P])

    def diag(t, h):
        return t[64 * h:64 * h + 64, :, 64 * h:64 * h + 64]

    def chunk(t, c, h):
        return t[64 * h:64 * h + 64, :, ds(c * C, C)]

    def decay(c, h):
        return pc[64 * h:64 * h + 64, :, ds(c, 1)].to_broadcast([64, NP, C])

    with nc.Block() as block:
        @block.sync
        def _(sp):
            for h in range(2):
                sp.sem_inc(g_out[h], 16)
            def load(c, q):
                sp.dma_start(ring[:, 0, q].rearrange("p k n -> p (k n)"), a["w_in"][ds(c + Z_GATE, 1)].rearrange("c p n -> p (c n)")).then_inc(gw[q], 16)

            def store(c):
                for h in range(2):
                    sp.wait_ge(S["gate_sig"], 2 * c + h + 2)
                    sp.dma_start(gates_d[ds(c, 1), :, h * 512:(h + 1) * 512].rearrange("c p n -> p (c n)"), gst[:, h, :]).then_inc(g_out[h], 16)

            load(0, 0)
            load(1, 1)
            sp.dma_start(branch_b_weights(ring), a["w_branch_b"].rearrange("(k p) n -> p k n", p=P)).then_inc(sem("x_w_b"), 16)
            sp.wait_ge(nought_ready, 1)
            sp.dma_start(ys_d[E * P:, :].rearrange("(p b) (n c) -> p (b n) c", p=P, c=P),
                         nought[:].unsqueeze(1).to_broadcast([P, (NB + 1 - E) * KC, P])).then_inc(zeros_out, 16)
            with sp.Fori(0, NI - 1) as i:
                for q in range(2):
                    store(2 * i + q)
                    load(2 * i + q + 2, q)
            store(NC - 2)
            store(NC - 1)
            for h in range(2):
                sp.wait_ge(g_out[h], 16 * NC + 16)
            sp.wait_ge(zeros_out, 16)

        @block.gpsimd
        def _(pool):
            start_at_one(pool, "gpsimd")
            pool.memset(nought[:], 0.0).then_inc(nought_ready, 1)
            for n in "abd vbd bhbd".split():
                ins = pool.memset(m[n][:], 0.0)
            ins.then_inc(S["init"], 1)
            pool.wait_ge(S["init"], 2)

            def body(c):
                pool.wait_ge(S["u0_mm"], c + 1)
                pool.wait_ge(S["SPC"], c + 1)
                for h in range(2):
                    ins = pool.tensor_copy(diag(m["abd"], h), chunk(at, c, h))
                ins.then_inc(S["abd"], 1)
                pool.wait_ge(S["abd"], c + 2)
                pool.wait_ge(S["v_tr"], c + 1)
                for h in range(2):
                    ins = pool.tensor_copy(diag(m["vbd"], h), chunk(vt, c, h))
                ins.then_inc(S["vbd"], 1)
                pool.wait_ge(S["vbd"], c + 2)
                pool.wait_ge(S["init"], 2)
                pool.wait_ge(S["bh_tr"], c + 1)
                for h in range(2):
                    ins = pool.tensor_tensor(diag(m["bhbd"], h), chunk(bt, c, h), decay(c, h), ALU.mult)
                ins.then_inc(S["bhbd"], 1)
                pool.wait_ge(S["bhbd"], c + 2)
                pool.wait_ge(S["xraw"], c + 2)
                pool.wait_ge(S["Z_mm"], 3 * c + 1)
                for n in ("o8", "o16", "o32"):
                    ins = pool.tensor_tensor(m[n][:], xraw[:], mask(n), ALU.mult)
                ins.then_inc(S["offs"], 1)
                pool.wait_ge(S["init"], 2)
                pool.wait_ge(S["S"], c + 1)
                pool.wait_ge(S["R2"], c + 2)
                pool.tensor_tensor(SPC[:], m["S"][:], pc[:, :, ds(c, 1)].to_broadcast([P, NP, P]), ALU.mult).then_inc(S["SPC"], 1)

            with pool.Fori(0, NC) as c:
                body(c)

        @block.scalar
        def _(act):
            start_at_one(act, "scalar")
            act.wait_ge(S["init"], 2)

            def sigmoid(c, h):
                act.wait_ge(S["gate_mm"], 2 * c + h + 2)
                act.wait_ge(g_out[h], 16 * c + 16)
                act.activation(gst[:, h, :], bank(6 + h), ACT.Sigmoid).then_inc(S["gate_sig"], 1)

            def body(c):
                for n, src, last, at_ in (("kbd", kt, "rk_mm", c), ("rbd", rt, "y_mm", c)):
                    act.wait_ge(S["init"], 2)
                    act.wait_ge(S[last], at_ + 1)
                    for h in range(2):
                        ins = act.copy(diag(m[n], h), chunk(src, c, h))
                    ins.then_inc(S[n], 1)

                def evac(b, ready, value, dst, done):
                    act.wait_ge(S[ready], value + 1)
                    act.copy(dst[:], quads(b)).then_inc(S[done], 1)

                act.wait_ge(S["rz_mm"], 3 * c + 1)
                evac(1, "x0_mm", c + 1, xraw, "xraw")
                act.wait_ge(S["y_mm"], c + 1)
                evac(4, "v_tr", c + 1, m["V"], "V")
                act.wait_ge(S["sp_mm"], c + 1)
                evac(0, "bh_tr", c + 1, m["BH"], "BH")
                evac(1, "kh_tr", c + 1, m["KH"], "KH")
                act.wait_ge(S["X"], c + 2)
                act.wait_ge(S["offs"], c + 2)
                evac(2, "x2_mm", c + 1, m["x2"], "x2")
                act.wait_ge(S["u_mm"], c + 1)
                evac(4, "x4_mm", c + 1, m["x4"], "x4")
                for j in range(3):
                    if j == 0:
                        act.wait_ge(S["r2_mm"], c + 2)
                        act.wait_ge(S["x4_mm"], c + 2)
                    evac(1, "T_mm", 3 * c + j + 1, Tt, "T")
                    if j == 0:
                        sigmoid(c, 0)
                act.wait_ge(S["r4_mm"], c + 2)
                evac(4, "u0_mm", c + 1, U0, "U0")
                evac(5, "u_mm", c + 1, U, "U")
                sigmoid(c, 1)
                act.wait_ge(S["init"], 2)
                act.wait_ge(S["y_mm"], c + 2)
                for h in range(2):
                    ins = act.copy(chunk(rt, c, h), quads(4)[64 * h:64 * h + 64, :, 64 * h:64 * h + 64])
                ins.then_inc(S["yout"], 1)

            with act.Fori(0, NC) as c:
                body(c)

        @block.vector
        def _(dve):
            start_at_one(dve, "vector")
            for n in "bbd kbd rbd khbd S".split():
                ins = dve.memset(m[n][:], 0.0)
            ins.then_inc(S["init"], 1)
            dve.wait_ge(S["init"], 2)

            def body(c):
                dve.wait_ge(S["rb_mm"], c + 1)
                for h in range(2):
                    ins = dve.tensor_copy(diag(m["bbd"], h), chunk(bt, c, h))
                ins.then_inc(S["bbd"], 1)
                dve.wait_ge(S["kh_tr"], c + 1)
                for h in range(2):
                    ins = dve.tensor_tensor(diag(m["khbd"], h), chunk(kt, c, h), decay(c, h), ALU.mult)
                ins.then_inc(S["khbd"], 1)

                def masked(b, ready, dst, name, done):
                    dve.wait_ge(S[ready], c + 2)
                    dve.tensor_tensor(dst[:], quads(b), mask(name), ALU.mult).then_inc(S[done], 1)

                dve.wait_ge(S["y_mm"], c + 1)
                masked(0, "y0_mm", m["Y"], "y8", "Y")
                dve.wait_ge(S["Y"], c + 2)
                dve.wait_ge(S["u_mm"], c + 1)
                dve.tensor_tensor(m["R"][:], m["Y"][:], mask("ident"), ALU.add).then_inc(S["R1"], 1)
                dve.wait_ge(S["xraw"], c + 2)
                dve.tensor_tensor(m["X"][:], xraw[:], mask("x8"), ALU.mult).then_inc(S["X"], 1)
                masked(2, "rb_mm", m["RB"], "upinc", "RB")
                masked(3, "ak_mm", m["AK"], "up", "AK")
                masked(5, "rk_mm", m["RK"], "upinc", "RK")
                dve.wait_ge(S["y2_mm"], c + 2)
                dve.wait_ge(S["rz_mm"], 3 * c + 1)
                dve.tensor_copy(m["y2"][:], quads(3)).then_inc(S["y2"], 1)
                dve.wait_ge(S["r2_mm"], c + 2)
                dve.wait_ge(S["R1"], c + 2)
                dve.tensor_tensor(m["R"][:], m["R"][:], quads(5), ALU.add).then_inc(S["R2"], 1)
                dve.wait_ge(S["r4_mm"], c + 2)
                dve.wait_ge(S["R2"], c + 2)
                dve.tensor_tensor(m["R"][:], m["R"][:], quads(0), ALU.add).then_inc(S["R4"], 1)
                dve.wait_ge(S["R4"], c + 2)
                for j in range(3):
                    dve.wait_ge(S["Z_mm"], 3 * c + j + 2)
                    dve.wait_ge(S["x4_mm"], c + 2)
                    dve.tensor_copy(Z[:], quads(2)).then_inc(S["Z"], 1)
                    dve.wait_ge(S["rz_mm"], 3 * c + j + 2)
                    dve.tensor_tensor(m["R"][:], m["R"][:], quads(3), ALU.add).then_inc(S["R"], 1)
                    dve.wait_ge(S["R"], 3 * c + j + 2)
                dve.wait_ge(S["SPC"], c + 2)
                dve.wait_ge(S["y_mm"], c + 2)
                dve.wait_ge(S["sp_mm"], c + 2)
                dve.tensor_tensor(m["S"][:], SPC[:], quads(0), ALU.add).then_inc(S["S"], 1)

            with dve.Fori(0, NC) as c:
                body(c)

        @block.tensor
        def _(pe):
            start_at_one(pe, "tensor")
            pe.wait_ge(S["init"], 2)

            def each(b, pairs, done, transpose=False):
                for p in range(NP):
                    dst = ps[:, b, p * P:(p + 1) * P]
                    for n, (x, y) in enumerate(pairs):
                        if transpose:
                            ins = pe.transpose(dst, m[x][:, p, :], k["ident"])
                        else:
                            xt, yt = (m[x] if isinstance(x, str) else x), (m[y] if isinstance(y, str) else y)
                            ins = pe.matmul(dst, xt[:, p, :], yt[:, p, :], start=(n == 0), stop=(n == len(pairs) - 1))
                ins.then_inc(S[done], 1)

            def body(c, q):
                def gate_products():
                    pe.wait_ge(gw[q], 16 * turns[0])
                    for h in range(2):
                        for kc in range(KC):
                            if kc == 0:
                                pe.wait_ge(S["gate_sig"], 2 * c + 1)
                            ins = pe.matmul(bank(6 + h), ring[:, 0, q, kc, :], hT[:, kc, h * 512:(h + 1) * 512], start=(kc == 0), stop=(kc == KC - 1))
                            if kc == KC - 1:
                                ins.then_inc(S["gate_mm"], 1)
                            yield

                work = gate_products()

                def fill(n=1):
                    for _ in range(n):
                        next(work, None)

                def need(**waits):
                    for n, v in waits.items():
                        pe.wait_ge(S[n], v + 1)

                fill(3)
                need(abd=c + 1, bbd=c + 1, S=c)
                each(0, [("bbd", "abd")], "y0_mm")
                need(T=3 * c)
                each(1, [("abd", "bbd")], "x0_mm")
                need(kbd=c + 1, rbd=c + 1, Z=3 * c, R=3 * c)
                each(2, [("bbd", "rbd")], "rb_mm")
                each(3, [("kbd", "abd")], "ak_mm")
                need(U=c)
                each(5, [("kbd", "rbd")], "rk_mm")
                need(vbd=c + 1, yout=c)
                each(4, [("vbd", None)], "v_tr", transpose=True)
                need(bhbd=c + 1, Y=c + 1)
                each(0, [("bhbd", None)], "bh_tr", transpose=True)
                need(khbd=c + 1, xraw=c + 1)
                each(1, [("khbd", None)], "kh_tr", transpose=True)
                need(X=c + 1, RB=c + 1, AK=c + 1)
                each(2, [("Y", "X")], "x2_mm")
                each(3, [("X", "Y")], "y2_mm")
                fill(2)
                need(x2=c + 1, R1=c + 1, RK=c + 1)
                each(5, [("x2", "R")], "r2_mm")
                need(y2=c + 1, V=c + 1)
                each(4, [("y2", "x2")], "x4_mm")
                fill(1)
                need(x4=c + 1, R2=c + 1, BH=c + 1)
                each(0, [("x4", "R")], "r4_mm")
                fill(1)
                need(offs=c + 1, KH=c + 1)
                for j, off in enumerate(("o8", "o16", "o32")):
                    need(R4=c + 1) if j == 0 else need(R=3 * c + j)
                    each(1, [("R", None)], "T_mm", transpose=True)
                    each(2, [(off, "R")], "Z_mm")
                    fill(1)
                    need(T=3 * c + j + 1, Z=3 * c + j + 1)
                    each(3, [(Tt, Z)], "rz_mm")
                    fill(1)
                need(S=c)
                each(4, [("abd", "S"), ("AK", "V")], "u0_mm")
                fill(2)
                need(U0=c + 1, R=3 * c + 3)
                each(5, [("R", U0)], "u_mm")
                fill(1)
                need(U=c + 1)
                each(0, [("BH", U), ("KH", "V")], "sp_mm")
                each(4, [("S", "rbd"), (U, "RB"), ("V", "RK")], "y_mm")
                fill(16)

            turns = [None]
            with pe.Fori(0, NI) as i:
                turns[0] = i + 1
                for q in range(2):
                    body(2 * i + q, q)


def branch_b_weights(ring):
    return ring[:, 1:3].rearrange("p s c k n -> p (s c k n)").rearrange("p (k n) -> p k n", n=D)


def mix_branches(sb, env, x1, x1_d, logits, g_d, bonus_d, yb_d, gates_d, n2_d):
    nc, a, ps, k, col, row, bank, banks, sem = (env[n] for n in ("nc", "a", "ps", "k", "col", "row", "bank", "banks", "sem"))
    rt, modc, gate1b = env["rt"], env["modc"], env["gate1b"]
    yb = sb("yb2", [P, NP, T])
    mixed = sb("mixed", [P, KC, T])
    wa, wb = sb("wa_branch", [P, NP, D]), branch_b_weights(env["ring"])
    wob = sb("wob", [P, KC, D // 2])
    gs = sb("gs", [P, 2, T])
    gg, bo, yc, sq = (sb(n, [P, 2, T]) for n in ("gg", "bo", "yc", "sq"))
    tmp = sb("tmp", [P, T])
    eps = sb("eps", [P, 1])
    norm_after = {0: 0, 1: 1, 3: 2, 5: 3}
    names = ("w_b w_a yb_in gg_in0 gg_in1 bo_in0 bo_in1 mean_mm var_mm yc sq sd gn ya pb_mm pa_mm mb ma chain pchain "
             "gin0 gin1 eps").split()
    S = {n: sem("x_" + n) for n in names}
    wo_hi = yb[:].rearrange("p q (a n) -> p (q a) n", a=2)
    wo_in = {n: sem("o_" + n) for n in ("o_in", "o2_in")}
    with nc.Block() as block:
        @block.sync
        def _(sp):
            sp.dma_start(yb[:], yb_d.rearrange("q p t -> p q t")).then_inc(S["yb_in"], 16)
            for n in range(2 * KC):
                if n >= 2:
                    sp.wait_ge(S["mb"], min(n - 1, KC))
                if n >= KC + 2:
                    sp.wait_ge(S["ma"], n - 1 - KC)
                sp.dma_start(gs[:, n % 2, :], gates_d[n]).then_inc(S[f"gin{n % 2}"], 16)
                if n == 1:
                    sp.dma_start(wa[:], a["w_branch_a"].rearrange("(k p) n -> p k n", p=P)).then_inc(S["w_a"], 16)
                if n == KC - 1:
                    sp.wait_ge(S["pb_mm"], KC)
                    w = a["w_out"].rearrange("(k p) n -> p k n", p=P)
                    sp.dma_start(wob[:], w[:, :, 0:512]).then_inc(wo_in["o_in"], 16)
                    sp.dma_start(wo_hi, w[:, :, 512:1024]).then_inc(wo_in["o2_in"], 16)

        @block.scalar
        def _(act):
            act.wait_ge(S["eps"], 1)
            for p in range(NP):
                if p >= 2:
                    act.wait_ge(S["ya"], p - 1)
                act.dma_start(gg[:, p % 2, :], g_d[p]).then_inc(S[f"gg_in{p % 2}"], 16)
                act.dma_start(bo[:, p % 2, :], bonus_d[p]).then_inc(S[f"bo_in{p % 2}"], 16)
                if p >= 1:
                    act.wait_ge(S["var_mm"], p)
                    act.activation(sq[:, (p - 1) % 2, :], banks(2), ACT.Sqrt, bias=eps[:]).then_inc(S["sd"], 1)
            act.wait_ge(S["var_mm"], NP)
            act.activation(sq[:, (NP - 1) % 2, :], banks(2), ACT.Sqrt, bias=eps[:]).then_inc(S["sd"], 1)

        @block.gpsimd
        def _(pool):
            def square(p):
                pool.wait_ge(S["yc"], p + 1)
                if p >= 2:
                    pool.wait_ge(S["gn"], p - 1)
                pool.tensor_tensor(sq[:, p % 2, :], yc[:, p % 2, :], yc[:, p % 2, :], ALU.mult).then_inc(S["sq"], 1)

            square(0)
            for p in range(NP):
                q = p % 2
                if p + 1 < NP:
                    square(p + 1)
                pool.wait_ge(S["gn"], p + 1)
                pool.wait_ge(S[f"bo_in{q}"], 16 * (p // 2 + 1))
                pool.wait_ge(S[f"gg_in{q}"], 16 * (p // 2 + 1))
                pool.tensor_tensor(yc[:, q, :], yc[:, q, :], bo[:, q, :], ALU.add).then_inc(S["pchain"], 1)
                pool.wait_ge(S["pchain"], p + 1)
                pool.tensor_tensor(rt[:, p, :], yc[:, q, :], gg[:, q, :], ALU.mult).then_inc(S["ya"], 1)

        @block.vector
        def _(dve):
            chain = [0]

            def link(ins):
                chain[0] += 1
                ins.then_inc(S["chain"], 1)
                dve.wait_ge(S["chain"], chain[0])

            def branch_b(j):
                dve.wait_ge(S["pb_mm"], j + 1)
                dve.wait_ge(S[f"gin{j % 2}"], 16 * (j // 2 + 1))
                dve.tensor_tensor(mixed[:, j, :], banks(4 + 2 * (j % 2)), gs[:, j % 2, :], ALU.mult).then_inc(S["mb"], 1)

            def centre(p):
                dve.wait_ge(S["mean_mm"], p + 1)
                if p >= 2:
                    dve.wait_ge(S["ya"], p - 1)
                dve.tensor_tensor(yc[:, p % 2, :], rt[:, p, :], banks(0), ALU.subtract).then_inc(S["yc"], 1)

            dve.memset(eps[:], GN_EPS).then_inc(S["eps"], 1)
            centre(0)
            for j in range(KC):
                branch_b(j)
                if j in norm_after:
                    p = norm_after[j]
                    if p + 1 < NP:
                        centre(p + 1)
                    y, sd = yc[:, p % 2, :], sq[:, p % 2, :]
                    dve.wait_ge(S["sd"], p + 1)
                    link(dve.reciprocal(sd, sd))
                    link(dve.tensor_tensor(y, y, sd, ALU.mult))
                    dve.tensor_scalar(y, y, col("gn_g", p), col("gn_b", p), ALU.mult, ALU.add).then_inc(S["gn"], 1)
            for j in range(KC):
                dve.wait_ge(S["pa_mm"], j + 1)
                dve.wait_ge(S[f"gin{j % 2}"], 16 * ((KC + j) // 2 + 1))
                dve.tensor_tensor(tmp[:], banks(4 + 2 * (j % 2)), gs[:, j % 2, :], ALU.mult).then_inc(S["ma"], 1)
                dve.wait_ge(S["ma"], j + 1)
                dve.wait_ge(S["mb"], KC)
                link(dve.tensor_tensor(mixed[:, j, :], mixed[:, j, :], tmp[:], ALU.add))

        @block.tensor
        def _(pe):
            def heads(b, src, done):
                for h in range(2):
                    ins = pe.matmul(bank(b + h), k["headmean"], src[:, h * 512:(h + 1) * 512], start=True, stop=True)
                ins.then_inc(S[done], 1)

            def project(j, w, src, done):
                for h in range(2):
                    for q in range(NP):
                        ins = pe.matmul(bank(4 + 2 * (j % 2) + h), w[:, q, j * P:(j + 1) * P], src[:, q, h * 512:(h + 1) * 512], start=(q == 0), stop=(q == NP - 1))
                ins.then_inc(S[done], 1)

            heads(0, rt[:, 0, :], "mean_mm")
            pe.wait_ge(S["w_b"], 16)
            pe.wait_ge(S["yb_in"], 16)
            for j in range(KC):
                if j >= 2:
                    pe.wait_ge(S["mb"], j - 1)
                project(j, wb, yb, "pb_mm")
                if j in norm_after:
                    p = norm_after[j]
                    pe.wait_ge(S["sq"], p + 1)
                    if p:
                        pe.wait_ge(S["sd"], p)
                    heads(2, sq[:, p % 2, :], "var_mm")
                    if p + 1 < NP:
                        pe.wait_ge(S["yc"], p + 1)
                        heads(0, rt[:, p + 1, :], "mean_mm")
            pe.wait_ge(S["w_a"], 16)
            pe.wait_ge(S["ya"], NP)
            for j in range(KC):
                if j < 2:
                    pe.wait_ge(S["mb"], KC)
                else:
                    pe.wait_ge(S["ma"], j - 1)
                project(j, wa, rt, "pa_mm")

    env["phase_ends"](keep=("o_o_in", "o_o2_in"))
    rows, xs, n2 = gg, bo[:, 0, :], bo[:, 1, :]
    h2 = yc[:, 0, :].rearrange("p (k n) -> p k n", n=P)
    rw = sb("rw", [P, KC, E])
    st = sb("st", [P, 4, 6])
    mv = sb("mv2", [P, 2, 2])
    names = "x_in rows_in rw_in o_in o2_in o_mm stat sd x1r x1s x1 stat2 sd2 n2 n2_out n2_tr h2 r_mm chain res o_read x1_out".split()
    Q = {n: sem("o_" + n) for n in names}
    with nc.Block() as block:
        @block.sync
        def _(sp):
            sp.dma_start(rows[:, 0, :], row("ln1_g")).then_inc(Q["rows_in"], 16)
            sp.dma_start(rows[:, 1, :], row("ln1_b")).then_inc(Q["rows_in"], 16)
            sp.dma_start(rw[:], a["router_w"].rearrange("(k p) n -> p k n", p=P)).then_inc(Q["rw_in"], 16)
            for i in range(NT):
                if i:
                    sp.wait_ge(Q["res"], i)
                sp.dma_start(xs, a["x"][i * P:(i + 1) * P, :]).then_inc(Q["x_in"], 16)
                if i:
                    sp.wait_ge(Q["n2"], i)
                    sp.dma_start(n2_d[(i - 1) * P:i * P, :], n2).then_inc(Q["n2_out"], 16)
                if i > NT // 2:
                    j = i - 1 - NT // 2
                    sp.dma_start(x1_d[j * P:(j + 1) * P, :], x1[i - 1]).then_inc(Q["x1_out"], 16)
            sp.wait_ge(Q["n2"], NT)
            sp.dma_start(n2_d[(NT - 1) * P:, :], n2).then_inc(Q["n2_out"], 16)
            sp.dma_start(x1_d[(NT // 2 - 1) * P:, :], x1[NT - 1]).then_inc(Q["x1_out"], 16)
            sp.wait_ge(Q["x1_out"], 16 * (NT // 2))
            sp.wait_ge(Q["n2_out"], 16 * NT)

        @block.scalar
        def _(act):
            for i in range(NT):
                act.wait_ge(Q["stat"], i + 1)
                act.activation(mv[:, 0, 1:2], mv[:, 0, 1:2], ACT.Sqrt).then_inc(Q["sd"], 1)
                act.wait_ge(Q["stat2"], i + 1)
                act.activation(mv[:, 1, 1:2], mv[:, 1, 1:2], ACT.Sqrt).then_inc(Q["sd2"], 1)
                act.wait_ge(Q["n2_tr"], i + 1)
                if i:
                    act.wait_ge(Q["r_mm"], i)
                for kc in range(KC):
                    ins = act.activation(h2[:, kc, :], ps[:, 4 + kc // 4, (kc % 4) * P:(kc % 4 + 1) * P], ACT.Identity,
                                         bias=modc[:, 2, kc:kc + 1], scale=modc[:, 3, kc:kc + 1])
                ins.then_inc(Q["h2"], 1)

        @block.gpsimd
        def _(pool):
            pool.wait_ge(Q["rows_in"], 32)
            for i in range(NT):
                pool.wait_ge(Q["x1s"], i + 1)
                pool.tensor_tensor(x1[i], x1[i], rows[:, 1, :], ALU.add).then_inc(Q["x1"], 1)

        @block.vector
        def _(dve):
            chain = [0]

            def link(ins):
                chain[0] += 1
                ins.then_inc(Q["chain"], 1)
                dve.wait_ge(Q["chain"], chain[0])

            def norm(src, dst, w, stat, sd, i, done):
                for h in range(2):
                    ins = dve.bn_stats(st[:, 2 * w + h, :], src[:, h * 512:(h + 1) * 512])
                link(ins)
                link(dve.bn_aggr(mv[:, w, :], st[:, 2 * w:2 * w + 2, :].rearrange("p a b -> p (a b)")))
                dve.tensor_scalar(mv[:, w, 1:2], mv[:, w, 1:2], LN_EPS, None, ALU.add).then_inc(Q[stat], 1)
                dve.wait_ge(Q[sd], i + 1)
                link(dve.reciprocal(mv[:, w, 1:2], mv[:, w, 1:2]))
                return dve.tensor_scalar(dst, src, mv[:, w, 0:1], mv[:, w, 1:2], ALU.subtract, ALU.mult).then_inc(Q[done], 1)

            for i in range(NT):
                dve.wait_ge(Q["o_mm"], i + 1)
                dve.tensor_tensor(tmp[:], banks(2 * (i % 2)), gate1b[:], ALU.mult).then_inc(Q["o_read"], 1)
                dve.wait_ge(Q["o_read"], i + 1)
                dve.wait_ge(Q["x_in"], 16 * (i + 1))
                dve.scalar_tensor_tensor(out=tmp[:], in0=xs, scalar=ALPHA, in1=tmp[:], op0=ALU.mult, op1=ALU.add).then_inc(Q["res"], 1)
                dve.wait_ge(Q["res"], i + 1)
                norm(tmp[:], x1[i], 0, "stat", "sd", i, "x1r")
                dve.wait_ge(Q["x1r"], i + 1)
                dve.wait_ge(Q["rows_in"], 32)
                dve.tensor_tensor(x1[i], x1[i], rows[:, 0, :], ALU.mult).then_inc(Q["x1s"], 1)
                dve.wait_ge(Q["x1"], i + 1)
                if i:
                    dve.wait_ge(Q["n2_out"], 16 * i)
                    dve.wait_ge(Q["n2_tr"], i)
                norm(x1[i], n2, 1, "stat2", "sd2", i, "n2")
            dve.wait_ge(Q["r_mm"], NT)
            link(dve.tensor_copy(logits[:].rearrange("p i e -> p (i e)"), bank(6, NT * E)))

        @block.tensor
        def _(pe):
            pe.wait_ge(Q["o_in"], 16)
            pe.wait_ge(Q["o2_in"], 16)

            def out_tile(i):
                if i >= 2:
                    pe.wait_ge(Q["o_read"], i - 1)
                for h, w in enumerate((wob[:], wo_hi)):
                    for kc in range(KC):
                        ins = pe.matmul(bank(2 * (i % 2) + h), mixed[:, kc, i * P:(i + 1) * P], w[:, kc, :], start=(kc == 0), stop=(kc == KC - 1))
                ins.then_inc(Q["o_mm"], 1)

            def turn(i):
                pe.wait_ge(Q["n2"], i + 1)
                if i:
                    pe.wait_ge(Q["h2"], i)
                else:
                    pe.wait_ge(Q["rw_in"], 16)
                for kc in range(KC):
                    ins = pe.transpose(ps[:, 4 + kc // 4, (kc % 4) * P:(kc % 4 + 1) * P], n2[:, kc * P:(kc + 1) * P], k["ident"])
                ins.then_inc(Q["n2_tr"], 1)

            def router(i):
                pe.wait_ge(Q["h2"], i + 1)
                for kc in range(KC):
                    ins = pe.matmul(ps[:, 6, i * E:(i + 1) * E], h2[:, kc, :], rw[:, kc, :], start=(kc == 0), stop=(kc == KC - 1))
                ins.then_inc(Q["r_mm"], 1)

            out_tile(0)
            out_tile(1)
            for i in range(NT):
                turn(i)
                if i + 2 < NT:
                    out_tile(i + 2)
                router(i)


def expert_weights(sb, env):
    nc, a = env["nc"], env["a"]
    w = [sb(f"w{n}", [P, KC, F] if n != "d" else [P, FC, D]) for n in "gud"]
    full = [env["sem"](f"e_w{n}") for n in "gud"]

    def load(sp, e, n):
        name = ("e_gate", "e_up", "e_down")[n]
        sp.dma_start(w[n][:], a[name][ds(e, 1)].rearrange("e (k p) f -> p (e k) f", p=P)).then_inc(full[n], 16)

    return w, full, load


def route(sb, env, logits, dest, wts, bounds, slots):
    nc, a, ps, k, row, sem, small = (env[n] for n in ("nc", "a", "ps", "k", "row", "sem", "small"))
    NE = NT * E
    t = {n: sb("r_" + n, [P, NE]) for n in "score sel gs eq eq2 masked M1 M2 M wk tot".split()}
    pair = sb("r_pair", [P, NT * EG, 3])
    base = sb("r_base", [P, NT + 1, E])
    nblk = sb("r_nblk", [P, E])
    bend = sb("r_bend", [P, E])
    bst = sb("r_bst", [P, E])
    first = sb("r_first", [P, E])
    one = sb("r_one", [P, E])
    gq = {n: sb("r_g" + n, [P, NT * EG]) for n in "abcd"}
    c8 = {n: sb("r_c" + n, [P, NT]) for n in "abc"}
    rb = sb("r_rb", [P, E])
    destf = sb("r_destf", [P, 2, NT])
    place = sb("r_place", [P, 2, 2 * NT], I32)
    placef = sb("r_placef", [P, 2, 2 * NT])
    of_block = sb("r_of_block", [P, 2 * NT, NB + 2])
    at_pos = sb("r_at_pos", [P, 2 * NT, P])
    names = "score rb_in M_ready rank_mm chain of_block at_pos slots_mm".split()
    S = {n: sem("r_" + n) for n in names}
    prio_g, prio_e = small[:, 0:EG], small[:, EG:EG + E]

    def ie(x):
        return x[:].rearrange("p (i e) -> p i e", e=E)

    def ig(x):
        return x[:].rearrange("p (i g) -> p i g", g=EG)

    with nc.Block() as block:
        @block.sync
        def _(sp):
            sp.dma_start(rb[:], row("router_b")).then_inc(S["rb_in"], 16)
            for n in range(3):
                env["weights"][2](sp, 0, n)

        @block.scalar
        def _(act):
            act.activation(t["score"][:], logits[:].rearrange("p i e -> p (i e)"), ACT.Sigmoid).then_inc(S["score"], 1)

        @block.tensor
        def _(pe):
            pe.wait_ge(S["M_ready"], 1)
            pe.matmul(ps[:, 0, 0:NE], k["upfull"], t["M"][:], start=True, stop=True)
            pe.matmul(ps[:, 1, 0:NE], k["ones"], t["M"][:], start=True, stop=True).then_inc(S["rank_mm"], 1)
            pe.wait_ge(S["of_block"], 1)
            for n in range(2 * NT):
                if n % NT == 0:
                    pe.wait_ge(S["at_pos"], n // NT + 1)
                ins = pe.matmul(ps[:, 2, 0:NB + 2], at_pos[:, n, :], of_block[:, n, :], start=(n == 0), stop=(n == 2 * NT - 1))
            ins.then_inc(S["slots_mm"], 1)

        @block.vector
        def _(dve):
            chain = [0]

            def link(ins):
                chain[0] += 1
                ins.then_inc(S["chain"], 1)
                dve.wait_ge(S["chain"], chain[0])

            def tt(o, x, y, op):
                link(dve.tensor_tensor(o, x, y, op))

            dve.wait_ge(S["score"], 1)
            dve.wait_ge(S["rb_in"], 16)
            tt(ie(t["sel"]), ie(t["score"]), rb[:].unsqueeze(1).to_broadcast([P, NT, E]), ALU.add)
            x4 = t["sel"][:].rearrange("p (m e) -> p m e", e=4)
            ga, gb = gq["a"][:].unsqueeze(2), gq["b"][:]
            tt(pair[:], x4[:, :, 0:3], x4[:, :, 1:4], ALU.add)
            link(dve.tensor_reduce(gb, pair[:], AX.X, ALU.max))
            tt(pair[:, :, 0:2], x4[:, :, 0:2], x4[:, :, 2:4], ALU.add)
            tt(pair[:, :, 2:3], x4[:, :, 0:1], x4[:, :, 3:4], ALU.add)
            link(dve.tensor_reduce(gq["a"][:], pair[:], AX.X, ALU.max))
            tt(gb, gb, gq["a"][:], ALU.max)
            link(dve.tensor_reduce(c8["a"][:], ig(gq["b"]), AX.X, ALU.max))
            tt(ig(gq["c"]), ig(gq["b"]), c8["a"][:].unsqueeze(2).to_broadcast([P, NT, EG]), ALU.is_equal)
            tt(ig(gq["c"]), ig(gq["c"]), prio_g.unsqueeze(1).to_broadcast([P, NT, EG]), ALU.mult)
            link(dve.tensor_reduce(c8["a"][:], ig(gq["c"]), AX.X, ALU.max))
            tt(ig(gq["c"]), ig(gq["c"]), c8["a"][:].unsqueeze(2).to_broadcast([P, NT, EG]), ALU.is_equal)
            link(dve.tensor_scalar(gq["d"][:], gq["c"][:], -1.0, BIG, ALU.add, ALU.mult))
            tt(t["masked"][:].rearrange("p (m e) -> p m e", e=4), x4, gq["d"][:].unsqueeze(2).to_broadcast([P, NT * EG, 4]), ALU.add)
            for n, M in enumerate(("M1", "M2")):
                link(dve.tensor_reduce(c8["a"][:], ie(t["masked"]), AX.X, ALU.max))
                tt(ie(t["eq"]), ie(t["masked"]), c8["a"][:].unsqueeze(2).to_broadcast([P, NT, E]), ALU.is_equal)
                tt(ie(t["eq"]), ie(t["eq"]), prio_e.unsqueeze(1).to_broadcast([P, NT, E]), ALU.mult)
                link(dve.tensor_reduce(c8["a"][:], ie(t["eq"]), AX.X, ALU.max))
                tt(ie(t[M]), ie(t["eq"]), c8["a"][:].unsqueeze(2).to_broadcast([P, NT, E]), ALU.is_equal)
                if n == 0:
                    link(dve.scalar_tensor_tensor(out=t["masked"][:], in0=t[M][:], scalar=-BIG, in1=t["masked"][:], op0=ALU.mult, op1=ALU.add))
            dve.tensor_tensor(t["M"][:], t["M1"][:], t["M2"][:], ALU.add).then_inc(S["M_ready"], 1)
            for n, M in enumerate(("M1", "M2")):
                tt(t["wk"][:], t["score"][:], t[M][:], ALU.mult)
                link(dve.tensor_reduce(wts[:, n, :], ie(t["wk"]), AX.X, ALU.add))
            tt(c8["b"][:], wts[:, 0, :], wts[:, 1, :], ALU.add)
            link(dve.reciprocal(c8["b"][:], c8["b"][:]))
            for n in range(2):
                tt(wts[:, n, :], wts[:, n, :], c8["b"][:], ALU.mult)
            link(dve.memset(base[:, 0, :], 0.0))
            link(dve.memset(one[:], 1.0))
            link(dve.memset(nblk[:], 0.0))
            dve.wait_ge(S["rank_mm"], 1)
            for i in range(NT):
                tt(base[:, i + 1, :], base[:, i, :], ps[:, 1, i * E:(i + 1) * E], ALU.add)
            link(dve.tensor_scalar(nblk[:], nblk[:], 1.0, None, ALU.add))
            for j in range(1, T // P):
                link(dve.scalar_tensor_tensor(out=nblk[:], in0=base[:, NT, :], scalar=float(P * j), in1=nblk[:], op0=ALU.is_gt, op1=ALU.add))
            link(dve.tensor_tensor_scan(bend[:], one[:], nblk[:], 0.0, ALU.mult, ALU.add))
            tt(first[:], bend[:], nblk[:], ALU.subtract)
            link(dve.tensor_scalar(bst[:], first[:], float(P), None, ALU.mult))
            tt(ie(t["wk"]), ps[:, 0, 0:NE].rearrange("p (i e) -> p i e", e=E), base[:, 0:NT, :], ALU.add)
            tt(ie(t["wk"]), ie(t["wk"]), bst[:].unsqueeze(1).to_broadcast([P, NT, E]), ALU.add)
            for n, M in enumerate(("M1", "M2")):
                tt(t["eq"][:], t["wk"][:], t[M][:], ALU.mult)
                link(dve.tensor_reduce(destf[:, n, :], ie(t["eq"]), AX.X, ALU.add))
            link(dve.tensor_copy(dest[:], destf[:]))
            flat = dest[:].rearrange("p c i -> p (c i)")
            dve.tensor_scalar(place[:, 0, :], flat, P.bit_length() - 1, None, ALU.arith_shift_right)
            link(dve.tensor_scalar(place[:, 1, :], flat, P - 1, None, ALU.bitwise_and))
            link(dve.tensor_copy(placef[:], place[:]))
            tt(of_block[:], small[:, COUNT:COUNT + NB + 2].unsqueeze(1).to_broadcast([P, 2 * NT, NB + 2]),
               placef[:, 0, :].unsqueeze(2).to_broadcast([P, 2 * NT, NB + 2]), ALU.is_equal)
            for c in range(2):
                h = slice(c * NT, (c + 1) * NT)
                ins = dve.tensor_tensor(of_block[:, h, :], of_block[:, h, :],
                                        small[:, TOKEN:TOKEN + NT].unsqueeze(2).to_broadcast([P, NT, NB + 2]), ALU.mult)
            ins.then_inc(S["of_block"], 1)
            for c in range(2):
                h = slice(c * NT, (c + 1) * NT)
                dve.tensor_tensor(at_pos[:, h, :], small[:, COUNT:COUNT + P].unsqueeze(1).to_broadcast([P, NT, P]),
                                  placef[:, 1, h].unsqueeze(2).to_broadcast([P, NT, P]), ALU.is_equal).then_inc(S["at_pos"], 1)
            link(dve.tensor_copy(bounds[:, 0:E], first[0:1, :]))
            link(dve.tensor_scalar(bend[:], bend[:], -1.0, None, ALU.add))
            link(dve.tensor_copy(bounds[:, E:], bend[0:1, :]))
            dve.wait_ge(S["slots_mm"], 1)
            link(dve.tensor_copy(slots[:], ps[:, 2, 0:NB + 2]))


def run_experts(sb, env, bounds, slots, n2_d, ys_d, gate2_d):
    nc, a, ps, k, bank, banks, sem, modc = (env[n] for n in ("nc", "a", "ps", "k", "bank", "banks", "sem", "modc"))
    raw, full, load = env["weights"]
    hi, lo = ([sb(f"w{n}_{part}", [P, KC, F] if n != "d" else [P, FC, D], F32R) for n in "gud"] for part in ("hi", "lo"))
    GATE, UP, DOWN = range(3)
    HI, LO = ("wg_hi", "wu_hi", "wd_hi"), ("wg_lo", "wu_lo", "wd_lo")
    FIRST, LAST = range(2)
    gate2b = env["gate1b"]
    idx = sb("idx", [P, 1], I32)
    xg = sb("xg", [P, D])
    xT = sb("xT", [P, KC, P])
    x_hi, x_lo = (sb(f"x_{n}", [P, KC, P], F32R) for n in ("hi", "lo"))
    sil = sb("sil", [P, F])
    hid = sb("hid", [P, F])
    h_hi, h_lo = (sb(f"h_{n}", [P, FC, P], F32R) for n in ("hi", "lo"))
    yst = sb("yst", [P, D])
    signals = {"tensor": "xt_mm g_mm gu_mm ht_mm d_mm", "scalar": "xT x_hi sil h_hi wg_hi wu_hi wd_hi",
               "vector": "x_lo hid h_lo y wg_lo wu_lo wd_lo", "gpsimd": "idx xg wg_lo2", "sync": "yout"}
    S = {n: sem("e_" + n) for names in signals.values() for n in names.split()}
    g_in, started = sem("e_gate2"), sem("e_started")

    by_dma = ("xg", "yout")
    starts = {n: 0 if n in ("idx", "xg") else 16 if n == "yout" else 1 for n in S}
    ys_rows = ys_d.rearrange("(b p) n -> b p n", p=P)

    def start_above_zero(eng, which):
        for n in signals[which].split():
            if starts[n]:
                eng.sem_inc(S[n], starts[n])

    def need(eng, **counts):
        for n, count in counts.items():
            eng.wait_ge(S[n], (16 * count if n in by_dma else count) + starts[n])

    def bound(eng, e, which):
        return eng.value_load(bounds[0:1, ds(e + E * which, 1)], min_val=0, max_val=NB - 1)

    def total(eng):
        return bound(eng, E - 1, LAST) + 1

    def over_blocks(eng, steps):
        def expert(e, following):
            first, last = bound(eng, e, FIRST), bound(eng, e, LAST)
            with eng.If(first < last):
                with eng.Fori(first, last) as b:
                    steps(b, e, None)
            steps(last, e, following)

        with eng.Fori(0, E - 1) as e:
            expert(e, e + 1)
        expert(E - 1, None)

    def half(t, h):
        n = t.shape[1] // 2
        return t[:, h * n:(h + 1) * n, :]

    def lower_parts_made(eng, n, experts):
        eng.wait_ge(S[LO[n]], (1 if n == GATE else 2) * experts + 1)
        if n == GATE:
            eng.wait_ge(S["wg_lo2"], experts + 1)

    with nc.Block() as block:
        @block.sync
        def _(sp):
            start_above_zero(sp, "sync")
            sp.dma_start(gate2b[:], gate2_d).then_inc(g_in, 16)
            with sp.Fori(1, E) as e:
                for n in range(3):
                    lower_parts_made(sp, n, e)
                    load(sp, e, n)

        @block.gpsimd
        def _(pool):
            start_above_zero(pool, "gpsimd")
            pool.sem_inc(started, 1)

            def gather(n):
                pool.wait_ge(started, 1)
                pool.wait_ge(S["xt_mm"], n)
                pool.tensor_copy(idx[:], slots[:, ds(n - 1, 1)]).then_inc(S["idx"], 1)
                pool.wait_ge(started, 1)
                pool.wait_ge(S["idx"], n)
                pool.indirect_dma_start(out=xg[:], out_offset=None, in_=n2_d,
                                        in_offset=bass.IndirectOffsetOnAxis(ap=idx[:].bitcast(U32), axis=0)).then_inc(S["xg"], 16)

            def split_gate(e):
                pool.wait_ge(S[HI[GATE]], 2 * e + 3)
                pool.sem_inc(started, 1)
                pool.wait_ge(started, 1)
                pool.tensor_tensor(half(lo[GATE], 1), half(raw[GATE], 1), half(hi[GATE], 1).bitcast(F32), ALU.subtract).then_inc(S["wg_lo2"], 1)

            def steps(b, e, following):
                if following is not None:
                    split_gate(following)
                gather(pool.snap(b + 3))

            gather(1)
            split_gate(0)
            gather(2)
            over_blocks(pool, steps)
            n = total(pool)
            need(pool, xg=n + 2)
            need(pool, yout=n)

        @block.scalar
        def _(act):
            start_above_zero(act, "scalar")

            def inputs(b, used):
                need(act, xt_mm=b + 1, gu_mm=used, x_lo=used)
                for kc in range(KC):
                    ins = act.activation(xT[:, kc, :], ps[:, 2 + kc // 4, (kc % 4) * P:(kc % 4 + 1) * P], ACT.Identity,
                                         bias=modc[:, 2, kc:kc + 1], scale=modc[:, 3, kc:kc + 1])
                ins.then_inc(S["xT"], 1)
                need(act, xT=b + 1)
                act.copy(x_hi[:], xT[:]).then_inc(S["x_hi"], 1)

            def split(e, n, used):
                act.wait_ge(full[n], 16 * (e + 1))
                need(act, **{("g_mm", "gu_mm", "d_mm")[n]: used})
                for h in range(2):
                    act.copy(half(hi[n], h), half(raw[n], h)).then_inc(S[HI[n]], 1)

            def steps(b, e, following):
                need(act, g_mm=b + 1, hid=b)
                act.activation(sil[:], bank(0), ACT.Silu).then_inc(S["sil"], 1)
                if following is not None:
                    split(following, GATE, b + 1)
                need(act, ht_mm=b + 1, d_mm=b)
                act.copy(h_hi[:].rearrange("p k t -> p (k t)"), bank(4)).then_inc(S["h_hi"], 1)
                inputs(b + 1, b + 1)
                if following is not None:
                    split(following, UP, b + 1)
                need(act, y=b + 1)
                act.dma_start(ys_rows[ds(b, 1)].rearrange("b p n -> p (b n)"), yst[:]).then_inc(S["yout"], 16)
                if following is not None:
                    split(following, DOWN, b + 1)

            split(0, GATE, 0)
            inputs(0, 0)
            split(0, UP, 0)
            split(0, DOWN, 0)
            over_blocks(act, steps)

        @block.vector
        def _(dve):
            start_above_zero(dve, "vector")

            def split(e, n):
                for h in range(1 if n == GATE else 2):
                    dve.wait_ge(S[HI[n]], 2 * e + h + 2)
                    dve.tensor_tensor(half(lo[n], h), half(raw[n], h), half(hi[n], h).bitcast(F32), ALU.subtract).then_inc(S[LO[n]], 1)

            def inputs(b, used):
                need(dve, x_hi=b + 1, gu_mm=used)
                dve.tensor_tensor(x_lo[:], xT[:], x_hi[:].bitcast(F32), ALU.subtract).then_inc(S["x_lo"], 1)

            def steps(b, e, following):
                need(dve, sil=b + 1, gu_mm=b + 1, ht_mm=b)
                dve.tensor_tensor(hid[:], sil[:], bank(1), ALU.mult).then_inc(S["hid"], 1)
                need(dve, h_hi=b + 1, d_mm=b)
                dve.tensor_tensor(h_lo[:].rearrange("p k t -> p (k t)"), bank(4), h_hi[:].bitcast(F32).rearrange("p k t -> p (k t)"), ALU.subtract) \
                    .then_inc(S["h_lo"], 1)
                if following is not None:
                    split(following, GATE)
                inputs(b + 1, b + 1)
                if following is not None:
                    split(following, UP)
                need(dve, d_mm=b + 1, yout=b)
                dve.tensor_tensor(yst[:], banks(6), gate2b[:], ALU.mult).then_inc(S["y"], 1)
                if following is not None:
                    split(following, DOWN)

            dve.wait_ge(g_in, 16)
            split(0, GATE)
            inputs(0, 0)
            split(0, UP)
            split(0, DOWN)
            over_blocks(dve, steps)

        @block.tensor
        def _(pe):
            start_above_zero(pe, "tensor")

            def split_product(out, x, w, chunks, n, e, x_lo_ready):
                terms = ((x[0], w[0]), (x[0], w[1]), (x[1], w[0]))
                for m, (xx, ww) in enumerate(terms):
                    if m == 0:
                        pe.wait_ge(S[HI[n]], 2 * e + 3)
                    elif m == 1:
                        lower_parts_made(pe, n, e + 1)
                    else:
                        x_lo_ready()
                    for kc in range(chunks):
                        ins = pe.matmul(out, xx[:, kc, :], ww(kc), start=(m == 0 and kc == 0), stop=(m == 2 and kc == chunks - 1))
                return ins

            def turn(b, used):
                need(pe, xg=b + 1, xT=used)
                for kc in range(KC):
                    ins = pe.transpose(ps[:, 2 + kc // 4, (kc % 4) * P:(kc % 4 + 1) * P], xg[:, kc * P:(kc + 1) * P], k["ident"])
                ins.then_inc(S["xt_mm"], 1)

            def steps(b, e, _):
                need(pe, x_hi=b + 1, hid=b)
                for n, done in ((GATE, "g_mm"), (UP, "gu_mm")):
                    w = [lambda kc, t=t: t[:, kc, :] for t in (hi[n], lo[n])]
                    split_product(bank(n), (x_hi, x_lo), w, KC, n, e, lambda: need(pe, x_lo=b + 1)).then_inc(S[done], 1)
                turn(b + 1, b + 1)
                need(pe, hid=b + 1, h_hi=b, h_lo=b)
                for kc in range(FC):
                    ins = pe.transpose(ps[:, 4, kc * P:(kc + 1) * P], hid[:, kc * P:(kc + 1) * P], k["ident"])
                ins.then_inc(S["ht_mm"], 1)
                need(pe, h_hi=b + 1, y=b)
                for h in range(2):
                    w = [lambda kc, t=t: t[:, kc, h * 512:(h + 1) * 512] for t in (hi[DOWN], lo[DOWN])]
                    ins = split_product(bank(6 + h), (h_hi, h_lo), w, FC, DOWN, e, lambda: need(pe, h_lo=b + 1))
                ins.then_inc(S["d_mm"], 1)

            turn(0, 0)
            over_blocks(pe, steps)


def combine(sb, env, rt, x1_d, dest, wts, ys_d, out):
    nc, a, row, sem = (env[n] for n in ("nc", "a", "row", "sem"))
    R = 5
    ya = [sb(f"ya{i}", [P, D]) for i in range(R)]
    yb = [sb(f"ybb{i}", [P, D]) for i in range(R)]
    f = sb("f", [P, R, D])
    x1b = sb("x1_back", [P, NT // 2, D])
    x1 = [rt[:, i, :] if i < NT // 2 else x1b[:, i - NT // 2, :] for i in range(NT)]
    rows = sb("rows3", [P, 2, D])
    st = sb("st3", [P, R, 2, 6])
    mv = sb("mv3", [P, R, 3])
    names = "rows_in x1_in first stat sd chain shift n s1 fin".split()
    S = {n: sem("f_" + n) for n in names}
    fetched, stored = ([sem(f"f_{n}{i}") for i in range(R)] for n in ("fetched", "stored"))
    with nc.Block() as block:
        @block.sync
        def _(sp):
            sp.dma_start(rows[:, 0, :], row("ln2_g")).then_inc(S["rows_in"], 16)
            sp.dma_start(rows[:, 1, :], row("ln2_b")).then_inc(S["rows_in"], 16)
            sp.wait_ge(S["first"], 2)
            sp.dma_start(x1b[:], x1_d.rearrange("(i p) n -> p i n", p=P)).then_inc(S["x1_in"], 16)
            for i in range(NT):
                sp.wait_ge(S["fin"], i + 1)
                sp.dma_start(out[i * P:(i + 1) * P, :], f[:, i % R, :]).then_inc(stored[i % R], 16)
            for q in range(R):
                sp.wait_ge(stored[q], 16 * len(range(q, NT, R)))

        @block.gpsimd
        def _(pool):
            def fetch(i):
                if i >= R:
                    pool.wait_ge(S["n"], i - R + 1)
                for c, t in enumerate((ya[i % R], yb[i % R])):
                    pool.indirect_dma_start(out=t[:], out_offset=None, in_=ys_d,
                                            in_offset=bass.IndirectOffsetOnAxis(ap=dest[:, c, i:i + 1].bitcast(U32), axis=0)) \
                        .then_inc(fetched[i % R], 16)

            for i in range(R):
                fetch(i)
            pool.wait_ge(S["rows_in"], 32)
            for i in range(NT):
                if i + R < NT:
                    fetch(i + R)
                pool.wait_ge(S["s1"], i + 1)
                pool.tensor_tensor(f[:, i % R, :], f[:, i % R, :], rows[:, 1, :], ALU.add).then_inc(S["fin"], 1)

        @block.scalar
        def _(act):
            for i in range(NT + 2):
                if i < NT:
                    act.wait_ge(fetched[i % R], 32 * (i // R + 1))
                    act.activation(ya[i % R][:], ya[i % R][:], ACT.Identity, scale=wts[:, 0, i:i + 1]).then_inc(S["first"], 1)
                if 1 <= i <= NT:
                    act.wait_ge(S["stat"], i)
                    act.activation(mv[:, (i - 1) % R, 1:2], mv[:, (i - 1) % R, 1:2], ACT.Sqrt).then_inc(S["sd"], 1)
                if i >= 2:
                    j, q = i - 2, (i - 2) % R
                    act.wait_ge(S["shift"], j + 1)
                    if j >= R:
                        act.wait_ge(stored[q], 16 * (j // R))
                    act.activation(f[:, q, :], ya[q][:], ACT.Identity, bias=mv[:, q, 2:3], scale=mv[:, q, 1:2]).then_inc(S["n"], 1)

        @block.vector
        def _(dve):
            chain = [0]

            def link(ins):
                chain[0] += 1
                ins.then_inc(S["chain"], 1)
                dve.wait_ge(S["chain"], chain[0])

            def add_up(i, q):
                dve.wait_ge(S["first"], i + 1)
                if i == NT // 2:
                    dve.wait_ge(S["x1_in"], 16)
                dve.wait_ge(fetched[q], 32 * (i // R + 1))
                link(dve.scalar_tensor_tensor(out=ya[q][:], in0=x1[i], scalar=ALPHA, in1=ya[q][:], op0=ALU.mult, op1=ALU.add))
                link(dve.scalar_tensor_tensor(out=ya[q][:], in0=yb[q][:], scalar=wts[:, 1, i:i + 1], in1=ya[q][:], op0=ALU.mult, op1=ALU.add))
                for h in range(2):
                    ins = dve.bn_stats(st[:, q, h, :], ya[q][:, h * 512:(h + 1) * 512])
                link(ins)
                link(dve.bn_aggr(mv[:, q, 0:2], st[:, q].rearrange("p a b -> p (a b)")))
                dve.tensor_scalar(mv[:, q, 1:2], mv[:, q, 1:2], LN_EPS, None, ALU.add).then_inc(S["stat"], 1)

            def scale_and_shift(i, q):
                dve.wait_ge(S["sd"], i + 1)
                link(dve.reciprocal(mv[:, q, 1:2], mv[:, q, 1:2]))
                dve.scalar_tensor_tensor(out=mv[:, q, 2:3], in0=mv[:, q, 0:1], scalar=-1.0, in1=mv[:, q, 1:2], op0=ALU.mult, op1=ALU.mult) \
                    .then_inc(S["shift"], 1)

            dve.wait_ge(S["rows_in"], 32)
            for i in range(NT + 2):
                if i < NT:
                    add_up(i, i % R)
                if 1 <= i <= NT:
                    scale_and_shift(i - 1, (i - 1) % R)
                if i >= 2:
                    q = (i - 2) % R
                    dve.wait_ge(S["n"], i - 1)
                    dve.tensor_tensor(f[:, q, :], f[:, q, :], rows[:, 0, :], ALU.mult).then_inc(S["s1"], 1)


def kernel(**inputs):
    import concourse.bacc as _bacc
    from concourse.bass_utils import run_bass_kernel_spmd as _run

    v = {n: np.asarray(x) for n, x in inputs.items()}

    def chunks(w):
        return np.ascontiguousarray(w.reshape(KC, P, -1, P).transpose(2, 1, 0, 3)).reshape(-1, P, KC * P)

    def cols(x):
        return x.reshape(-1, P).T

    b_mod = v["b_mod"][0].reshape(6, D)
    col_of = {"mu": v["rwkv_mu"][0], "w0": v["w0"][0], "a0": v["a0"][0], "k_k": v["k_k"][0], "k_a": v["k_a"][0],
              "r_k": v["r_k"][0].reshape(-1), "gn_g": v["gn_g"][0], "gn_b": v["gn_b"][0], "shift1": b_mod[0],
              "scale1": b_mod[1], "shift2": b_mod[3], "scale2": b_mod[4], "c": v["c"][0]}
    row_of = {"sg_ln_g": v["sg_ln_g"][0], "sg_ln_b": v["sg_ln_b"][0], "gate1": b_mod[2], "gate2": b_mod[5],
              "ln1_g": v["ln1_g"][0], "ln1_b": v["ln1_b"][0], "ln2_g": v["ln2_g"][0], "ln2_b": v["ln2_b"][0],
              "router_b": v["router_b"]}
    table, chunk_start, small = constants()
    arrays = {
        "x": v["x"][0], "w_mod": v["w_mod"][0], "w_in": chunks(v["w_in"][0])[Z_ORDER],
        "cols": np.concatenate([cols(col_of[n]) for n in COLS], axis=1),
        "rows": np.concatenate([row_of[n] for n in ROWS]),
        "table": table, "chunk_start": chunk_start, "small": small,
        "w2": v["w2"][0], "a2": v["a2"][0], "g2": v["g2"][0],
        "w_s": v["w_s"][0].transpose(2, 0, 1), "b_s": v["b_s"][0],
        "w_branch_a": v["w_branch_a"][0], "w_branch_b": v["w_branch_b"][0], "w_out": v["w_out"][0],
        "router_w": v["router_w"], "e_gate": v["e_gate"][0], "e_up": v["e_up"][0], "e_down": v["e_down"][0],
    }
    arrays = {f"{n}_dram": np.ascontiguousarray(x) for n, x in arrays.items()}
    nc = _bacc.Bacc("TRN2", target_bir_lowering=False, num_devices=1)
    a = {n[:-5]: nc.dram_tensor(n, x.shape, mybir.dt.from_np(x.dtype), kind="ExternalInput").ap() for n, x in arrays.items()}
    out = nc.dram_tensor("out_dram", (T, D), F32, kind="ExternalOutput").ap()
    build(nc, a, out)
    r = _run(nc, [arrays], core_ids=[0])
    return r.results[0]["out_dram"].reshape(1, T, D)
```
